# Optimizing a Trainium2 kernel written in Bass

```python
import jax, jax.numpy as jnp
from jax import lax
import numpy as np

D_MODEL = 1024
BATCH = 1
SEQ = 1024
DEPTH = 1
DEC_BATCH = 8
DEC_SEQ = 1
PAST_LEN = 8192
PAGE_SIZE = 128

HGRN_HEADS = 8
HGRN_DK = 128
HGRN_F = HGRN_HEADS * HGRN_DK
HGRN_DV = D_MODEL // HGRN_HEADS
HGRN_V = HGRN_HEADS * HGRN_DV
HGRN_CHUNK = 64
LRU_WIDTH = D_MODEL
LRU_BLOCKS = 8
LRU_BW = LRU_WIDTH // LRU_BLOCKS
LRU_C = 8.0
CONV_W = 4
D_FF = 2816
EPS = 1e-6
IN_SPLITS = (HGRN_F, HGRN_F, HGRN_V, HGRN_V, LRU_WIDTH, LRU_WIDTH, D_MODEL, D_MODEL)
IN_WIDTH = HGRN_F * 2 + HGRN_V * 2 + LRU_WIDTH * 2 + D_MODEL * 2

kernel_name = "hgrn2_rglru_gated_macaron_step"

def rmsnorm(x, g):
    xf = x.astype(jnp.float32)
    y = xf * lax.rsqrt(jnp.mean(xf * xf, axis=-1, keepdims=True) + EPS)
    return (y * g.astype(jnp.float32)).astype(x.dtype)

def swiglu(x, w_gate, w_up, w_down):
    return (jax.nn.silu(x @ w_gate) * (x @ w_up)) @ w_down

def hgrn2_chunked(q, logf, k, v, s0):
    B, T, H, DK = q.shape
    DV = v.shape[-1]
    C = min(HGRN_CHUNK, T)
    pad = (-T) % C
    nc = (T + pad) // C

    def prep(a):
        a = jnp.pad(a, ((0, 0), (0, pad), (0, 0), (0, 0)))
        return a.reshape(B, nc, C, H, a.shape[-1]).transpose(1, 0, 3, 2, 4)

    qc, gc, kc, vc = prep(q), prep(logf), prep(k), prep(v)
    mask = jnp.tril(jnp.ones((C, C), dtype=bool))

    def step(S, inp):
        qi, gi, ki, vi = inp
        b = jnp.cumsum(gi, axis=2)
        bl = b[:, :, -1:, :]
        qe = qi * jnp.exp(b)
        ke = ki * jnp.exp(-b)
        inter = jnp.einsum('bhck,bhkv->bhcv', qe, S)
        A = jnp.where(mask, jnp.einsum('bhck,bhsk->bhcs', qe, ke), 0.0)
        intra = jnp.einsum('bhcs,bhsv->bhcv', A, vi)
        S_new = jnp.exp(bl[:, :, 0, :])[..., None] * S + jnp.einsum(
            'bhsk,bhsv->bhkv', ki * jnp.exp(bl - b), vi)
        return S_new, inter + intra

    s_fin, o = lax.scan(step, s0, (qc, gc, kc, vc))
    o = o.transpose(1, 0, 3, 2, 4).reshape(B, nc * C, H, DV)[:, :T]
    return o, s_fin

def causal_conv(x, buf, w, b):
    T = x.shape[1]
    xc = jnp.concatenate([buf.astype(x.dtype), x], axis=1)
    out = b
    for j in range(CONV_W):
        out = out + xc[:, j:j + T] * w[j]
    return out, xc[:, -(CONV_W - 1):]

def block_diag(x, w, b):
    B, T, D = x.shape
    xb = x.reshape(B, T, LRU_BLOCKS, LRU_BW)
    return jnp.einsum('btnc,ncd->btnd', xb, w).reshape(B, T, D) + b

def rglru(x, r, i, lam, h0):
    log_a = -LRU_C * r * jax.nn.softplus(-lam)
    a = jnp.exp(log_a)
    mult = jnp.sqrt(-jnp.expm1(2.0 * log_a))
    bterm = mult * (i * x)
    bterm = bterm.at[:, 0].add(a[:, 0] * h0)

    def combine(l, rr):
        a1, b1 = l
        a2, b2 = rr
        return a1 * a2, a2 * b1 + b2

    _, h = lax.associative_scan(combine, (a, bterm), axis=1)
    return h, h[:, -1]

def layer(x, s_hgrn, h_lru, c_conv, lb,
          n1, f1g, f1u, f1d, nmix, w_in, o_norm, conv_w, conv_b,
          w_a, b_a, w_x, b_x, lam, w_a_up, w_b_up, w_out, n3, f2g, f2u, f2d):
    f32 = jnp.float32
    B, T, _ = x.shape
    x = x + 0.5 * swiglu(rmsnorm(x, n1), f1g, f1u, f1d)
    h = rmsnorm(x, nmix)
    proj = h @ w_in
    idx = [int(v) for v in np.cumsum(IN_SPLITS)[:-1]]
    q, fpre, vin, gout, xr, yr, ga, gb = jnp.split(proj, idx, axis=-1)

    lbf = lb.astype(f32)
    f = lbf + (1.0 - lbf) * jax.nn.sigmoid(fpre.astype(f32))
    logf = jnp.log(f)
    kk = 1.0 - f
    qh = jax.nn.silu(q.astype(f32)).reshape(B, T, HGRN_HEADS, HGRN_DK)
    oA, s_new = hgrn2_chunked(qh, logf.reshape(B, T, HGRN_HEADS, HGRN_DK),
                              kk.reshape(B, T, HGRN_HEADS, HGRN_DK),
                              vin.astype(f32).reshape(B, T, HGRN_HEADS, HGRN_DV),
                              s_hgrn.astype(f32))
    oA = oA * lax.rsqrt(jnp.mean(oA * oA, axis=-1, keepdims=True) + EPS)
    oA = oA.reshape(B, T, HGRN_V) * o_norm.astype(f32) * jax.nn.silu(gout.astype(f32))
    oA = oA.astype(x.dtype)

    xc, c_new = causal_conv(xr, c_conv, conv_w, conv_b)
    r = jax.nn.sigmoid(block_diag(xc, w_a, b_a).astype(f32))
    ig = jax.nn.sigmoid(block_diag(xc, w_x, b_x).astype(f32))
    hs, h_new = rglru(xc.astype(f32), r, ig, lam.astype(f32), h_lru.astype(f32))
    oB = (hs.astype(x.dtype) * jax.nn.gelu(yr))

    m = jax.nn.sigmoid(ga) * (oA @ w_a_up) + jax.nn.sigmoid(gb) * (oB @ w_b_up)
    x = x + m @ w_out
    x = x + 0.5 * swiglu(rmsnorm(x, n3), f2g, f2u, f2d)
    return x, s_new, h_new, c_new

def setup_inputs(seed: int = 0) -> dict:
    key = jax.random.key(seed)
    ks = jax.random.split(key, 32)
    f32 = jnp.float32
    nrm = lambda k, shape, s: (jax.random.normal(k, shape, f32) * s)
    gain = lambda k, shape: 1.0 + 0.05 * jax.random.normal(k, shape, f32)
    u = jax.random.uniform(ks[20], (DEPTH, LRU_WIDTH), f32, 0.9, 0.999)
    sl = u ** (1.0 / LRU_C)
    lam = jnp.log(sl) - jnp.log1p(-sl)
    return {
        "x_prompt": nrm(ks[0], (BATCH, SEQ, D_MODEL), 1.0),
        "x_sample": nrm(ks[1], (DEC_BATCH, DEC_SEQ, D_MODEL), 1.0),
        "state_hgrn": nrm(ks[2], (DEPTH, DEC_BATCH, HGRN_HEADS, HGRN_DK, HGRN_DV), 0.5),
        "state_lru": nrm(ks[3], (DEPTH, DEC_BATCH, LRU_WIDTH), 0.5),
        "state_conv": nrm(ks[4], (DEPTH, DEC_BATCH, CONV_W - 1, LRU_WIDTH), 1.0),
        "ffn1_norm": gain(ks[5], (DEPTH, D_MODEL)),
        "ffn1_w_gate": nrm(ks[6], (DEPTH, D_MODEL, D_FF), D_MODEL ** -0.5),
        "ffn1_w_up": nrm(ks[7], (DEPTH, D_MODEL, D_FF), D_MODEL ** -0.5),
        "ffn1_w_down": nrm(ks[8], (DEPTH, D_FF, D_MODEL), D_FF ** -0.5),
        "mix_norm": gain(ks[9], (DEPTH, D_MODEL)),
        "w_in": nrm(ks[10], (DEPTH, D_MODEL, IN_WIDTH), D_MODEL ** -0.5),
        "hgrn_lower_bounds": nrm(ks[11], (DEPTH + 1, HGRN_F), 0.1),
        "hgrn_out_norm": gain(ks[12], (DEPTH, HGRN_V)),
        "conv_w": nrm(ks[13], (DEPTH, CONV_W, LRU_WIDTH), CONV_W ** -0.5),
        "conv_b": nrm(ks[14], (DEPTH, LRU_WIDTH), 0.01),
        "lru_w_a": nrm(ks[15], (DEPTH, LRU_BLOCKS, LRU_BW, LRU_BW), LRU_BW ** -0.5),
        "lru_b_a": nrm(ks[16], (DEPTH, LRU_WIDTH), 0.01),
        "lru_w_x": nrm(ks[17], (DEPTH, LRU_BLOCKS, LRU_BW, LRU_BW), LRU_BW ** -0.5),
        "lru_b_x": nrm(ks[18], (DEPTH, LRU_WIDTH), 0.01),
        "lru_lambda": lam,
        "w_a_up": nrm(ks[21], (DEPTH, HGRN_V, D_MODEL), HGRN_V ** -0.5),
        "w_b_up": nrm(ks[22], (DEPTH, LRU_WIDTH, D_MODEL), LRU_WIDTH ** -0.5),
        "w_out": nrm(ks[23], (DEPTH, D_MODEL, D_MODEL), D_MODEL ** -0.5),
        "ffn2_norm": gain(ks[24], (DEPTH, D_MODEL)),
        "ffn2_w_gate": nrm(ks[25], (DEPTH, D_MODEL, D_FF), D_MODEL ** -0.5),
        "ffn2_w_up": nrm(ks[26], (DEPTH, D_MODEL, D_FF), D_MODEL ** -0.5),
        "ffn2_w_down": nrm(ks[27], (DEPTH, D_FF, D_MODEL), D_FF ** -0.5),
        "final_norm": gain(ks[28], (D_MODEL,)),
    }

def reference(x_prompt, x_sample, state_hgrn, state_lru, state_conv,
              ffn1_norm, ffn1_w_gate, ffn1_w_up, ffn1_w_down, mix_norm, w_in,
              hgrn_lower_bounds, hgrn_out_norm, conv_w, conv_b,
              lru_w_a, lru_b_a, lru_w_x, lru_b_x, lru_lambda,
              w_a_up, w_b_up, w_out, ffn2_norm, ffn2_w_gate, ffn2_w_up, ffn2_w_down,
              final_norm):
    lb_all = jnp.cumsum(jax.nn.softmax(hgrn_lower_bounds.astype(jnp.float32), axis=0), axis=0)

    def run(x, s_in, h_in, c_in):
        s_out, h_out, c_out = [], [], []
        for l in range(DEPTH):
            x, s, h, c = layer(
                x, s_in[l], h_in[l], c_in[l], lb_all[l],
                ffn1_norm[l], ffn1_w_gate[l], ffn1_w_up[l], ffn1_w_down[l], mix_norm[l], w_in[l],
                hgrn_out_norm[l], conv_w[l], conv_b[l], lru_w_a[l], lru_b_a[l], lru_w_x[l], lru_b_x[l],
                lru_lambda[l], w_a_up[l], w_b_up[l], w_out[l],
                ffn2_norm[l], ffn2_w_gate[l], ffn2_w_up[l], ffn2_w_down[l])
            s_out.append(s)
            h_out.append(h)
            c_out.append(c)
        return rmsnorm(x, final_norm), jnp.stack(s_out), jnp.stack(h_out), jnp.stack(c_out)

    bp = x_prompt.shape[0]
    s0 = jnp.zeros((DEPTH, bp, HGRN_HEADS, HGRN_DK, HGRN_DV), jnp.float32)
    h0 = jnp.zeros((DEPTH, bp, LRU_WIDTH), jnp.float32)
    c0 = jnp.zeros((DEPTH, bp, CONV_W - 1, LRU_WIDTH), x_prompt.dtype)
    y_prompt, hgrn_p, lru_p, conv_p = run(x_prompt, s0, h0, c0)
    y_sample, hgrn_s, lru_s, conv_s = run(x_sample, state_hgrn, state_lru, state_conv)
    return (y_prompt, y_sample, hgrn_p, lru_p, conv_p, hgrn_s, lru_s, conv_s)


_drawn_inputs = setup_inputs


def setup_inputs(seed=0):
    import zlib

    import numpy as np

    out = dict(_drawn_inputs(seed))
    spreads = {}
    factors = {'hgrn_out_norm': 3.738, 'lru_b_a': 22.194, 'lru_b_x': 8.0, 'ffn2_norm': 3.013}
    for name, (base, spread) in spreads.items():
        noise = np.random.default_rng([zlib.crc32(name.encode()), seed]).standard_normal(out[name].shape)
        drawn = base * np.exp(spread * noise) if base else spread * noise
        out[name] = __import__('jax').numpy.asarray(drawn.astype(out[name].dtype))
    for name, factor in factors.items():
        out[name] = (out[name] * factor).astype(out[name].dtype)
    return out
```

```python
from contextlib import ExitStack

import concourse.bass as bass
from concourse import mybir

ALU = mybir.AluOpType
ACT = mybir.ActivationFunctionType
F32 = mybir.dt.float32
F32R = mybir.dt.float32r
BF16 = mybir.dt.bfloat16
U8 = mybir.dt.uint8

P = 128
D = 1024
KT = D // P
SEQ = 1024
DEC = 8
T = SEQ + DEC
NT = 3
TG = T // NT
FT = 2816 // P
PAIRS = FT // 2
HEADS = 8
CHUNK = 64
TILES = SEQ // P
EPS = 1e-6

(G1, GMIX, G2, GFIN, GO, CB, CW0, CW1, CW2, CW3, BA, BX, LAM, LB0, LB1) = range(15)
NVEC = 15

FFN_SLABS = 3 * FT
SLAB_FFN1 = 0
SLAB_A = SLAB_FFN1 + FFN_SLABS
SLAB_MA = SLAB_A + 4 * HEADS
SLAB_B = SLAB_MA + 2 * KT
SLAB_MB = SLAB_B + 2 * KT
SLAB_OUT = SLAB_MB + 2 * KT
SLAB_FFN2 = SLAB_OUT + KT
SLABS = SLAB_FFN2 + FFN_SLABS


class Names(dict):

    def __getattr__(self, name):
        return self[name]

    def __setattr__(self, name, value):
        self[name] = value


def tg(t):
    return slice(t * TG, (t + 1) * TG)


def wait(eng, sem, value):
    if not (isinstance(value, int) and value <= 0):
        eng.wait_ge(sem, value)


def wait_apart(eng, sem, value, passed):
    eng.wait_ge(sem, value)
    eng.sem_inc(passed)


class Slab:

    def __init__(self, first, per, i, c):
        self.number = i * per + (first + c)
        self.pair = i * (per // 2) + (first + c) // 2
        self.buf = (first + c) % 2



def load_slab(sp, k, slab):
    wait(sp, k.slab_ready, slab.number - 1)
    src = k.w_slabs[bass.ds(slab.number, 1)].rearrange("a p c -> p (a c)")
    sp.dma_start(k.raw[slab.buf][:, :], src).then_inc(k.slab_loaded[slab.buf], 16)


def split_hi(act, k, slab, slot):
    act.wait_ge(k.slab_loaded[slab.buf], slab.pair * 16 + 16)
    act.activation(k.w_hi[slot][:, :], k.raw[slab.buf][:, :], ACT.Copy).then_inc(k.slab_hi, 1)


def split_lo(dve, k, slab, slot):
    dve.wait_ge(k.slab_hi, slab.number + 1)
    dve.tensor_tensor(k.w_lo[slot][:, :], k.raw[slab.buf][:, :], k.w_hi[slot][:, :].bitcast(F32),
                      ALU.subtract).then_inc(k.slab_ready, 1)


def weight(k, slot, b):
    cols = slice(b * P, (b + 1) * P)
    return k.w_hi[slot][:, cols], k.w_lo[slot][:, cols]


def three(pe, out, w, x, start, stop):
    (wh, wl), (xh, xl) = w, x
    pe.matmul(out, wh, xh, start=start, stop=False)
    pe.matmul(out, wh, xl, start=False, stop=False)
    return pe.matmul(out, wl, xh, start=False, stop=stop)


def product(pe, k, out, slot, hi, lo, cols, tiles=range(KT)):
    for m in tiles:
        last = three(pe, out, weight(k, slot, m), (hi[:, m, cols], lo[:, m, cols]), m == 0, m == KT - 1)
    return last



def norm_scalar(act, k, s):
    for t in range(NT):
        s.x_ready(act, t)
        wait(act, s.summed, t - 1)
        act.activation(k.sq8[t % 2][:, :, :], k.x[:, :, tg(t)], ACT.Square).then_inc(s.squared, 1)
    if s.spill:
        act.dma_start(k.x_dram, k.x[:, :, :].rearrange("p m t -> p (m t)")).then_inc(k.x_spilled, 16)
    for t in range(NT):
        act.wait_ge(s.mean_ready, t + 1)
        act.activation(k.rstd[:, tg(t)], k.bank[t][:, 0:TG], ACT.Ln, bias=k.eps[:, 0:1]).then_inc(s.ln, 1)
        act.wait_ge(s.ln, t + 1)
        act.activation(k.rstd[:, tg(t)], k.rstd[:, tg(t)], ACT.Exp, scale=-0.5).then_inc(s.rstd_ready, 1)
        if s.final:
            continue
        for m in range(KT):
            act.wait_ge(s.h_ready, t * KT + m + 1)
            act.activation(k.h_hi[:, m, tg(t)], k.htmp[m % 4][:, :], ACT.Copy).then_inc(s.h_hi, 1)


def norm_gpsimd(pool, k, s):
    for t in range(NT):
        sq = k.sq8[t % 2]
        pool.wait_ge(s.squared, t + 1)
        pool.tensor_tensor(sq[:, 0:4, :], sq[:, 0:4, :], sq[:, 4:8, :], ALU.add).then_inc(s.tree, 1)
        pool.wait_ge(s.tree, 2 * t + 1)
        pool.tensor_tensor(sq[:, 0:2, :], sq[:, 0:2, :], sq[:, 2:4, :], ALU.add).then_inc(s.tree, 1)
        pool.wait_ge(s.tree, 2 * t + 2)
        wait(pool, s.mean_ready, t - 1)
        pool.tensor_tensor(k.sumsq[t % 2][:, :], sq[:, 0, :], sq[:, 1, :], ALU.add).then_inc(s.summed, 1)


def norm_tensor(pe, k, s):
    for t in range(NT):
        pe.wait_ge(s.summed, t + 1)
        pe.matmul(k.bank[t][:, 0:TG], k.ones_d[:, :], k.sumsq[t % 2][:, :], start=True, stop=True)\
            .then_inc(s.mean_ready, 1)


def norm_vector(dve, k, s):
    for t in range(NT):
        dve.wait_ge(s.rstd_ready, t + 1)
        if s.final:
            for m in range(KT):
                dve.scalar_tensor_tensor(k.y[:, m, tg(t)], k.x[:, m, tg(t)], k.vec[:, s.gain, m:m + 1],
                                         k.rstd[:, tg(t)], ALU.mult, ALU.mult).then_inc(s.h_ready, 1)
            continue

        def low(m):
            dve.wait_ge(s.h_hi, t * KT + m + 1)
            dve.tensor_tensor(k.h_lo[:, m, tg(t)], k.htmp[m % 4][:, :], k.h_hi[:, m, tg(t)].bitcast(F32),
                              ALU.subtract).then_inc(s.h_lo, 1)

        for m in range(KT):
            wait(dve, s.h_lo, t * KT + m - 3)
            dve.scalar_tensor_tensor(k.htmp[m % 4][:, :], k.x[:, m, tg(t)], k.vec[:, s.gain, m:m + 1],
                                     k.rstd[:, tg(t)], ALU.mult, ALU.mult).then_inc(s.h_ready, 1)
            if m >= 2:
                low(m - 2)
        low(KT - 2)
        low(KT - 1)



def ffn_tensor(pe, k, s):
    def group(i):
        for f in range(2):
            for which, slot in (("gate", 2 * f), ("up", 2 * f + 1)):
                pe.wait_ge(k.slab_ready, Slab(s.first, 6, i, slot).number + 1)
                for t in range(NT):
                    u = i * 6 + (3 * f + t)
                    if isinstance(i, int) and f == 0 and which == "gate":
                        pe.wait_ge(s.norm.h_lo, (t + 1) * KT)
                    if which == "gate":
                        wait(pe, s.gate_used, u - 1)
                        bank, ready = k.bank[(3 * f + t) % 2], s.gate_ready
                    else:
                        wait(pe, s.hidden, u - 1)
                        bank, ready = k.bank[2 + (3 * f + t) % 2], s.up_ready
                    product(pe, k, bank[:, 0:TG], slot, k.h_hi, k.h_lo, tg(t)).then_inc(ready, 1)
        for f in range(2):
            pe.wait_ge(k.slab_ready, Slab(s.first, 6, i, 4 + f).number + 1)
        for t in range(NT):
            pe.wait_ge(s.hidden_lo, i * 6 + (3 + t + 1))
            for m in range(KT):
                wait(pe, s.down_used, i * 24 + (8 * t + m - 3))
                for f in range(2):
                    last = three(pe, k.bank[4 + m % 4][:, 0:TG], weight(k, 4 + f, m),
                                 (k.hid_hi[:, f, tg(t)], k.hid_lo[:, f, tg(t)]), f == 0, f == 1)
                last.then_inc(s.down_ready, 1)

    group(0)
    with pe.Fori(1, PAIRS) as i:
        group(i)


def ffn_scalar(act, k, s):
    def ahead(i, last, c):
        if not last:
            split_hi(act, k, Slab(s.first, 6, i, c + 6), c)
        elif s.next_slabs > c:
            split_hi(act, k, Slab(s.first + FFN_SLABS, 0, 0, c), c)

    def group(i, last=False):
        for f in range(2):
            for t in range(NT):
                u = i * 6 + (3 * f + t)
                act.wait_ge(s.gate_ready, u + 1)
                wait(act, s.hidden, u - 2)
                act.activation(k.gate[:, tg(t)], k.bank[(3 * f + t) % 2][:, 0:TG], ACT.Silu).then_inc(s.gate_used, 1)
            ahead(i, last, 2 * f)
            for t in range(NT):
                u = i * 6 + (3 * f + t)
                act.wait_ge(s.hidden, u + 1)
                act.activation(k.hid_hi[:, f, tg(t)], k.hid[(3 * f + t) % 2][:, :], ACT.Copy).then_inc(s.hidden_hi, 1)
            ahead(i, last, 2 * f + 1)
        act.wait_ge(s.down_ready, i * 24 + 24)
        ahead(i, last, 4)
        ahead(i, last, 5)

    group(0)
    with act.Fori(1, PAIRS - 1) as i:
        group(i)
    group(PAIRS - 1, last=True)


def ffn_vector(dve, k, s):
    def ahead(i, last, c):
        if not last:
            split_lo(dve, k, Slab(s.first, 6, i, c + 6), c)
        elif s.next_slabs > c:
            split_lo(dve, k, Slab(s.first + FFN_SLABS, 0, 0, c), c)

    def group(i, last=False):
        for f in range(2):
            ahead(i, last, 2 * f)
            for t in range(NT):
                u = i * 6 + (3 * f + t)
                dve.wait_ge(s.up_ready, u + 1)
                dve.wait_ge(s.gate_used, u + 1)
                wait(dve, s.hidden_hi, u - 1)
                hid = k.hid[(3 * f + t) % 2]
                dve.tensor_tensor(hid[:, :], k.gate[:, tg(t)], k.bank[2 + (3 * f + t) % 2][:, 0:TG],
                                  ALU.mult).then_inc(s.hidden, 1)
                dve.wait_ge(s.hidden_hi, u + 1)
                dve.tensor_tensor(k.hid_lo[:, f, tg(t)], hid[:, :], k.hid_hi[:, f, tg(t)].bitcast(F32),
                                  ALU.subtract).then_inc(s.hidden_lo, 1)
            ahead(i, last, 2 * f + 1)
        for t in range(NT):
            for m in range(KT):
                w = i * 24 + (8 * t + m)
                dve.wait_ge(s.down_ready, w + 1)
                dve.scalar_tensor_tensor(k.x[:, m, tg(t)], k.bank[4 + m % 4][:, 0:TG], 0.5, k.x[:, m, tg(t)],
                                         ALU.mult, ALU.add).then_inc(s.down_used, 1)
        ahead(i, last, 4)
        ahead(i, last, 5)

    group(0)
    with dve.Fori(1, PAIRS - 1) as i:
        group(i)
    group(PAIRS - 1, last=True)



UNITS = 12
V_UNIT = 6
G_UNIT = 9


def branch_a(engine, body):
    body(0, True, False)
    body(1, True, True)
    with engine.Fori(2, HEADS) as j:
        body(j, True, True)
    body(HEADS, False, True)


def a_tensor(pe, k, s):
    def keys(h, n):
        tok = slice(n * P, (n + 1) * P)
        wait(pe, s.kt_used, h * 9 + n)
        pe.transpose(k.bank[4][:, 0:P], k.ke[:, tok], k.ident[:, :]).then_inc(s.kt_ready, 1)
        wait(pe, s.sc_used, h * 8 + n)
        pe.matmul(k.bank[5][:, 0:P], k.ke[:, tok], k.qe[:, tok], start=True, stop=True).then_inc(s.sc_ready, 1)

    def updates(h, n):
        pe.wait_ge(s.kt_used, h * 9 + (n + 1))
        wait(pe, s.u_used, h * 16 + 2 * n)
        for c in range(2):
            rows = slice(c * CHUNK, (c + 1) * CHUNK)
            pe.matmul(k.bank[6 + c][:, 0:P], k.kt[n % 2][rows, :], k.v[rows, n, :], start=True, stop=True)\
                .then_inc(s.u_ready, 1)

    def output(h, n):
        pe.wait_ge(s.state, h * 17 + (2 * n + 2))
        pe.wait_ge(s.sc_used, h * 8 + (n + 1))
        wait(pe, s.o_used, h * 9 + n)
        o = k.bank[3]
        for c in range(2):
            cols = slice(n * P + c * CHUNK, n * P + (c + 1) * CHUNK)
            pe.matmul(o[:, c * CHUNK:(c + 1) * CHUNK], k.s[(2 * n + c) % 4][:, :], k.qe[:, cols],
                      start=c == 0, stop=False, skip_group_check=True)
        pe.matmul(o[:, 0:P], k.v[:, n, :], k.sc[n % 2][:, :], start=False, stop=True, skip_group_check=True)\
            .then_inc(s.o_ready, 1)

    def slot(h, n):
        if 2 <= n < 10:
            output(h, n - 2)
        if 1 <= n < 9:
            updates(h, n - 1)
        if n == 0:
            pe.wait_ge(s.ke_ready, h * 1 + 1)
            pe.wait_ge(s.qe_ready, h * 1 + 1)
            pe.wait_ge(s.v_ready, h * 3 + 3)
        if n < 8:
            keys(h, n)
        if n == 8:
            pe.wait_ge(s.kt_used, h * 9 + 8)
            pe.transpose(k.bank[4][0:DEC, 0:P], k.ke[:, SEQ:T], k.ident[:, :]).then_inc(s.kt_ready, 1)
        if n in (9, 10):
            q = n - 9
            pe.wait_ge(s.kt_used, h * 9 + 9)
            pe.wait_ge(s.vm_ready, h * 2 + (q + 1))
            pe.wait_ge(s.u_used, h * 16 + 16)
            pe.matmul(k.bank[6 + q][:, 0:4 * P], k.kt[0][0:DEC, :], k.vm[0:DEC, :, :], start=True, stop=True)\
                .then_inc(s.u_ready, 1)
        if n == 11:
            pe.wait_ge(s.ss_new, h * 8 + 8)
            pe.wait_ge(s.o_used, h * 9 + 8)
            for b in range(DEC):
                last = pe.matmul(k.bank[3][:, b:b + 1], k.ss[:, b, :], k.qe[:, SEQ + b:SEQ + b + 1],
                                 start=True, stop=True)
            last.then_inc(s.o_ready, 1)

    def means(h):
        pe.wait_ge(s.squared, h * 1 + 1)
        pe.wait_ge(s.kt_used, h * 9 + 9)
        for t in range(NT):
            pe.matmul(k.bank[3 + t][:, 0:TG], k.ones_h[:, :], k.sq[:, tg(t)], start=True, stop=True)\
                .then_inc(s.mean_ready, 1)

    def turn(j, core):
        pe.wait_ge(s.unit_used, j * UNITS + (V_UNIT + 3))
        if core:
            pe.wait_ge(s.ln, (j - 1) * 3 + 3)
        for n in range(TILES + 1):
            rows = min(P, T - n * P)
            last = pe.transpose(k.bank[(6, 7, 4)[n // 4]][0:rows, (n % 4) * P:(n % 4 + 1) * P],
                                k.f[:, n * P:n * P + rows], k.ident[:, :])
            if n in (3, 7, 8):
                last.then_inc(s.vt_ready, 1)

    def iteration(j, proj, core):
        h = j - 1

        def free(c):
            wait(pe, s.unit_used, j * UNITS + (c - 2))
            return k.bank[c % 3]

        for half in range(12):
            u = half // 2
            if proj:
                if half % 6 == 0:
                    pe.wait_ge(k.slab_ready, Slab(SLAB_A, 4, j, u // 3).number + 1)
                if half % 2 == 0:
                    if not core and u < 3:
                        pe.wait_ge(s.norm.h_lo, (u + 1) * KT)
                    bank = free(u)
                last = product(pe, k, bank[:, 0:TG], u // 3, k.h_hi, k.h_lo, tg(u % 3),
                               range(4 * (half % 2), 4 * (half % 2) + 4))
                if half % 2:
                    last.then_inc(s.unit_ready, 1)
            if core:
                slot(h, half)
        if proj:
            pe.wait_ge(k.slab_ready, Slab(SLAB_A, 4, j, 2).number + 1)
        for c in range(3):
            if proj:
                bank = free(V_UNIT + c)
                product(pe, k, bank[:, 0:TG], 2, k.h_hi, k.h_lo, tg(c), range(0, 4))
            if core and c == 0:
                means(h)
            if proj:
                product(pe, k, bank[:, 0:TG], 2, k.h_hi, k.h_lo, tg(c), range(4, 8)).then_inc(s.unit_ready, 1)
        if proj:
            pe.wait_ge(k.slab_ready, Slab(SLAB_A, 4, j, 3).number + 1)
            for t in range(NT):
                bank = free(G_UNIT + t)
                product(pe, k, bank[:, 0:TG], 3, k.h_hi, k.h_lo, tg(t)).then_inc(s.unit_ready, 1)
                if t == 0:
                    turn(j, core)

    branch_a(pe, iteration)


def a_scalar(act, k, s):
    def slot(h, n):
        if 1 <= n < 9:
            m = n - 1
            for c in range(2):
                act.wait_ge(s.u_ready, h * 18 + (2 * m + c + 1))
                if m >= 2:
                    act.wait_ge(s.state, h * 17 + (2 * m - 1))
                act.activation(k.ue[m % 2][:, c, :], k.bank[6 + c][:, 0:P], ACT.Identity,
                               scale=k.el[:, 2 * m + c:2 * m + c + 1]).then_inc(s.u_used, 1)
        if n < 9:
            rows = P if n < 8 else DEC
            act.wait_ge(s.kt_ready, h * 9 + (n + 1))
            if n >= 2:
                act.wait_ge(s.u_ready, h * 18 + 2 * (n - 1))
            act.activation(k.kt[n % 2][0:rows, :], k.bank[4][0:rows, 0:P], ACT.Copy).then_inc(s.kt_used, 1)

    def iteration(j, proj, core):
        h = j - 1
        for half in range(12):
            u = half // 2
            if proj and half % 2:
                act.wait_ge(s.unit_ready, j * UNITS + (u + 1))
                if u < 3:
                    act.activation(k.f[:, tg(u)], k.bank[u % 3][:, 0:TG], ACT.Sigmoid).then_inc(s.unit_used, 1)
                else:
                    wait(act, s.qe_ready, j * 1)
                    act.activation(k.q[:, tg(u % 3)], k.bank[u % 3][:, 0:TG], ACT.Silu).then_inc(s.unit_used, 1)
                if u % 3 == 2:
                    split_hi(act, k, Slab(SLAB_A, 4, j, 4 + u // 3), u // 3)
            if core:
                slot(h, half)
        if core:
            act.wait_ge(s.o_used, h * 9 + 9)
            wait(act, s.scaled, h * 1)
            act.activation(k.sq[:, :], k.qe[:, :], ACT.Square).then_inc(s.squared, 1)
        if proj:
            act.wait_ge(s.f_ready, j * 1 + 1)
            act.activation(k.b[:, :], k.f[:, 0:SEQ], ACT.Ln).then_inc(s.logf, 1)
        if core:
            for t in range(NT):
                act.wait_ge(s.mean_ready, h * 3 + (t + 1))
                act.activation(k.sq[:, tg(t)], k.bank[3 + t][:, 0:TG], ACT.Ln, bias=k.eps[:, 0:1]).then_inc(s.ln, 1)
        if proj:
            act.wait_ge(s.cum, j * 1 + 1)
            act.activation(k.ke[:, 0:SEQ], k.b[:, :], ACT.Exp, scale=-1.0).then_inc(s.exp_minus, 1)
            act.activation(k.b[:, :], k.b[:, :], ACT.Exp).then_inc(s.exp_plus, 1)
        if core:
            act.wait_ge(s.ln, h * 3 + 3)
            act.activation(k.sq[:, :], k.sq[:, :], ACT.Exp, scale=-0.5).then_inc(s.rstd, 1)
        if proj:
            act.wait_ge(s.ke_ready, j * 1 + 1)
        for c in range(3):
            if proj:
                act.wait_ge(s.unit_ready, j * UNITS + (V_UNIT + c + 1))
                act.activation(k.f[:, tg(c)], k.bank[c][:, 0:TG], ACT.Copy).then_inc(s.unit_used, 1)
            if core and c == 1:
                wait_apart(act, s.gated, h * 1 + 1, s.act_passed)
                act.activation(k.o_hi[:, bass.ds(h, 1), :].rearrange("p a t -> p (a t)"), k.qe[:, :],
                               ACT.Copy).then_inc(s.out_hi, 1)
        if proj:
            split_hi(act, k, Slab(SLAB_A, 4, j, 6), 2)
            for t in range(NT):
                act.wait_ge(s.unit_ready, j * UNITS + (G_UNIT + t + 1))
                wait(act, s.gated, j * 1)
                act.activation(k.sg[:, tg(t)], k.bank[t][:, 0:TG], ACT.Silu).then_inc(s.unit_used, 1)
                if t == 0:
                    for n, bank in enumerate((6, 7, 4)):
                        act.wait_ge(s.vt_ready, j * 3 + (n + 1))
                        rows, tiles = (P, 4) if n < 2 else (DEC, 1)
                        act.activation(k.v[0:rows, 4 * n:4 * n + tiles, :].rearrange("p a d -> p (a d)"),
                                       k.bank[bank][0:rows, 0:tiles * P], ACT.Copy).then_inc(s.v_ready, 1)
            split_hi(act, k, Slab(SLAB_A, 4, j, 7), 3)

    act.wait_ge(k.x_spilled, 16)
    branch_a(act, iteration)


def a_vector(dve, k, s):
    def slot(h, n):
        if n == 0:
            dve.memset(k.s[0][:, :], 0.0).then_inc(s.state, 1)
        if 2 <= n < 10:
            m = n - 2
            dve.wait_ge(s.o_ready, h * 9 + (m + 1))
            dve.tensor_copy(k.qe[:, m * P:(m + 1) * P], k.bank[3][:, 0:P]).then_inc(s.o_used, 1)
        if 1 <= n < 9:
            for c in (2 * (n - 1), 2 * (n - 1) + 1):
                dve.wait_ge(s.u_used, h * 16 + (c + 1))
                dve.wait_ge(s.state, h * 17 + (c + 1))
                dve.scalar_tensor_tensor(k.s[(c + 1) % 4][:, :], k.s[c % 4][:, :], k.el[:, c:c + 1],
                                         k.ue[(n - 1) % 2][:, c % 2, :], ALU.mult, ALU.add).then_inc(s.state, 1)
        if n < 8:
            wait_apart(dve, s.sc_ready, h * 8 + (n + 1), s.dve_passed)
            dve.copy_predicated(k.sc[n % 2][:, :], k.mask[:, :], k.bank[5][:, 0:P]).then_inc(s.sc_used, 1)
        if n in (8, 9):
            q = n - 8
            if q:
                dve.wait_ge(s.u_ready, h * 18 + 17)
            dve.tensor_tensor(k.vm[0:DEC, :, :], k.v[0:DEC, 8:9, :].to_broadcast((DEC, 4, P)),
                              k.ident[0:DEC, 4 * q:4 * q + 4].unsqueeze(2).to_broadcast((DEC, 4, P)),
                              ALU.mult).then_inc(s.vm_ready, 1)
        if n in (9, 10):
            q = n - 9
            dve.wait_ge(s.u_ready, h * 18 + (17 + q))
            dve.wait_ge(s.ss_loaded, h * 16 + 16)
            for b in range(4 * q, 4 * q + 4):
                dve.scalar_tensor_tensor(k.ss[:, b, :], k.ss[:, b, :], k.el[:, 16 + b:17 + b],
                                         k.bank[6 + q][:, (b % 4) * P:(b % 4 + 1) * P],
                                         ALU.mult, ALU.add).then_inc(s.ss_new, 1)
        if n == 11:
            dve.wait_ge(s.o_ready, h * 9 + 9)
            dve.tensor_copy(k.qe[:, SEQ:T], k.bank[3][:, 0:DEC]).then_inc(s.o_used, 1)
            wait(dve, s.pstate_stored, h * 16)
            dve.wait_ge(s.state, h * 17 + 17)
            dve.tensor_copy(k.s_out[:, :], k.s[0][:, :]).then_inc(s.pstate_ready, 1)

    def iteration(j, proj, core):
        h = j - 1
        for half in range(12):
            if core:
                slot(h, half)
            if proj and half == 5:
                split_lo(dve, k, Slab(SLAB_A, 4, j, 4), 0)
                dve.wait_ge(s.unit_used, j * UNITS + 3)
                dve.tensor_scalar(k.f[:, :], k.f[:, :], k.par[:, 1, bass.ds(j, 1)], k.par[:, 0, bass.ds(j, 1)],
                                  ALU.mult, ALU.add).then_inc(s.f_ready, 1)
        if proj:
            split_lo(dve, k, Slab(SLAB_A, 4, j, 5), 1)
            dve.wait_ge(s.f_ready, j * 1 + 1)
            dve.tensor_copy(k.el[:, 16:24], k.f[:, SEQ:T]).then_inc(s.el_s, 1)
            dve.wait_ge(s.logf, j * 1 + 1)
            dve.tensor_tensor_scan(k.b[:, :], k.reset[:, :], k.b[:, :], 0.0, ALU.mult, ALU.add).then_inc(s.cum, 1)
            dve.wait_ge(s.el_s, j * 1 + 1)
            dve.tensor_scalar(k.f[:, :], k.f[:, :], -1.0, 1.0, ALU.mult, ALU.add).then_inc(s.key, 1)
            dve.wait_ge(s.key, j * 1 + 1)
            dve.tensor_copy(k.ke[:, SEQ:T], k.f[:, SEQ:T]).then_inc(s.ke_s, 1)
            dve.wait_ge(s.exp_minus, j * 1 + 1)
            dve.tensor_tensor(k.ke[:, 0:SEQ], k.ke[:, 0:SEQ], k.f[:, 0:SEQ], ALU.mult).then_inc(s.ke_ready, 1)
            dve.wait_ge(s.exp_plus, j * 1 + 1)
            dve.tensor_copy(k.el[:, 0:16], k.b[:, CHUNK - 1:SEQ:CHUNK]).then_inc(s.el_p, 1)
        if core:
            o = k.qe[:, :]
            dve.wait_ge(s.rstd, h * 1 + 1)
            dve.scalar_tensor_tensor(o, o, k.vec[:, GO, bass.ds(h, 1)], k.sq[:, :], ALU.mult, ALU.mult)\
                .then_inc(s.scaled, 1)
            dve.wait_ge(s.scaled, h * 1 + 1)
            dve.tensor_tensor(o, o, k.sg[:, :], ALU.mult).then_inc(s.gated, 1)
            dve.wait_ge(s.out_hi, h * 1 + 1)
            one = bass.ds(h, 1)
            dve.tensor_tensor(k.o_lo[:, one, :].rearrange("p a t -> p (a t)"), o,
                              k.o_hi[:, one, :].rearrange("p a t -> p (a t)").bitcast(F32),
                              ALU.subtract).then_inc(s.out_lo, 1)
        if proj:
            wait(dve, s.out_lo, j * 1)
            dve.wait_ge(s.unit_used, j * UNITS + 6)
            dve.tensor_copy(k.qe[:, SEQ:T], k.q[:, SEQ:T]).then_inc(s.qe_s, 1)
            dve.wait_ge(s.el_p, j * 1 + 1)
            dve.wait_ge(s.qe_s, j * 1 + 1)
            dve.tensor_tensor(k.qe[:, 0:SEQ], k.q[:, 0:SEQ], k.b[:, :], ALU.mult).then_inc(s.qe_ready, 1)
            split_lo(dve, k, Slab(SLAB_A, 4, j, 6), 2)
            split_lo(dve, k, Slab(SLAB_A, 4, j, 7), 3)

    branch_a(dve, iteration)


def a_sync(sp, k, s):
    def slabs(j):
        for c in range(4):
            load_slab(sp, k, Slab(SLAB_A, 4, j, c))

    slabs(0)
    slabs(1)
    a_states(sp, k, s, None, 0)
    slabs(2)
    with sp.Fori(3, HEADS) as j:
        a_states(sp, k, s, j - 3, j - 2)
        slabs(j)
    a_states(sp, k, s, HEADS - 3, HEADS - 2)


def a_states(sp, k, s, store, load):
    if store is not None:
        sp.wait_ge(s.ss_new, store * 8 + 8)
        sp.wait_ge(s.o_ready, store * 9 + 9)
        sp.dma_start(k.hgrn_s[bass.ds(store, 1)].rearrange("a p c -> p (a c)"),
                     k.ss[:, :, :].rearrange("p b d -> p (b d)")).then_inc(s.ss_stored, 16)
        sp.wait_ge(s.pstate_ready, store * 1 + 1)
        sp.dma_start(k.hgrn_p[bass.ds(store, 1)].rearrange("a p c -> p (a c)"), k.s_out[:, :])\
            .then_inc(s.pstate_stored, 16)
        sp.wait_ge(s.ss_stored, store * 16 + 16)
    if load is not None:
        sp.dma_start(k.ss[:, :, :].rearrange("p b d -> p (b d)"),
                     k.state_hgrn[bass.ds(load, 1)].rearrange("a p c -> p (a c)")).then_inc(s.ss_loaded, 16)



def merge_tensor(pe, k, s):
    def pair(i):
        for p in range(2):
            for c, (hi, lo) in enumerate(((k.h_hi, k.h_lo), (k.o_hi, k.o_lo))):
                slot = 2 * p + c
                pe.wait_ge(k.slab_ready, Slab(s.first, 4, i, slot).number + 1)
                for t in range(NT):
                    wait(pe, (s.gate_used, s.up_used)[c], i * 6 + (3 * p + t - 2))
                    if isinstance(i, int) and p == 0 and c == 1 and t == 0:
                        s.branch_done(pe)
                    product(pe, k, k.bank[3 * c + t][:, 0:TG], slot, hi, lo, tg(t))\
                        .then_inc((s.gate_ready, s.up_ready)[c], 1)

    s.banks_free(pe)
    pair(0)
    with pe.Fori(1, KT // 2) as i:
        pair(i)


def merge_scalar(act, k, s):
    def store(j, buf):
        act.wait_ge(s.up_used, j * 3 + 3)
        act.dma_start(k.m_dram[bass.ds(j, 1)].rearrange("a p t -> p (a t)"), k.mt[buf][:, :])\
            .then_inc(s.stored[buf], 16)

    def pair(i):
        first = isinstance(i, int)
        for p in range(2):
            for t in range(NT):
                u = i * 6 + (3 * p + t)
                act.wait_ge(s.gate_ready, u + 1)
                wait(act, s.multiplied, u - 2)
                act.activation(s.sgt[:, tg(t)], k.bank[t][:, 0:TG], ACT.Sigmoid).then_inc(s.gate_used, 1)
            split_hi(act, k, Slab(s.first, 4, i, 4 + 2 * p), 2 * p)
            if s.spill and not (first and p == 0):
                store(i * 2 + (p - 1), 1 - p)
            act.wait_ge(s.up_ready, i * 6 + 3 * (p + 1))
            split_hi(act, k, Slab(s.first, 4, i, 5 + 2 * p), 2 * p + 1)

    pair(0)
    with act.Fori(1, KT // 2) as i:
        pair(i)
    if s.spill:
        store(KT - 1, 1)


def merge_vector(dve, k, s):
    def pair(i):
        for p in range(2):
            split_lo(dve, k, Slab(s.first, 4, i, 4 + 2 * p), 2 * p)
            for t in range(NT):
                u = i * 6 + (3 * p + t)
                dve.wait_ge(s.up_ready, u + 1)
                dve.wait_ge(s.gate_used, u + 1)
                if s.spill:
                    if t == 0:
                        wait(dve, s.stored[p], i * 16)
                    dve.tensor_tensor(k.mt[p][:, tg(t)], s.sgt[:, tg(t)], k.bank[3 + t][:, 0:TG], ALU.mult)\
                        .then_inc(s.up_used, 1)
                else:
                    dve.tensor_tensor(k.mtb[:, tg(t)], s.sgt[:, tg(t)], k.bank[3 + t][:, 0:TG], ALU.mult)\
                        .then_inc(s.up_used, 1)
                    dve.wait_ge(s.up_used, u + 1)
                    at = (slice(None), bass.ds(i * 2 + p, 1), tg(t))
                    m = k.m[at].rearrange("p a t -> p (a t)")
                    dve.tensor_tensor(m, m, k.mtb[:, tg(t)], ALU.add).then_inc(s.m_ready, 1)
            split_lo(dve, k, Slab(s.first, 4, i, 5 + 2 * p), 2 * p + 1)

    if not s.spill:
        dve.wait_ge(s.m_loaded, 16 * KT)
    pair(0)
    with dve.Fori(1, KT // 2) as i:
        pair(i)




def branch_b(engine, body):
    body(0, 0, 0, False)
    body(1, 1, 0, True)
    with engine.Fori(1, KT // 2) as i:
        body(i * 2, 0, i, True)
        body(i * 2 + 1, 1, i, True)


def b_tensor(pe, k, s):
    def gates(j, p, t):
        if t == 0:
            pe.wait_ge(s.conv, j * 8 + 8)
            pe.wait_ge(s.blocks_ready, j * 1 + 1)
        wait(pe, s.gates_used, j * 6 + (2 if t == 2 else 0))
        for c in range(2):
            pe.matmul(k.bank[3 + 2 * c + t % 2][:, 0:TG], k.lw[p][:, c, :], k.xc[:, tg(t)],
                      start=True, stop=True).then_inc(s.gates_ready, 1)

    def block(j, p, i, before):
        for c in range(2):
            pe.wait_ge(k.slab_ready, Slab(SLAB_B, 4, i, 2 * p + c).number + 1)
            for t in range(NT):
                wait(pe, s.unit_used, j * 6 + (3 * c + t - 2))
                product(pe, k, k.bank[t][:, 0:TG], 2 * p + c, k.h_hi, k.h_lo, tg(t)).then_inc(s.unit_ready, 1)
                if before and c == 0:
                    gates(j - 1, 1 - p, t)

    s.banks_free(pe)
    branch_b(pe, block)
    for t in range(NT):
        gates(KT - 1, 1, t)


def b_gpsimd(pool, k, s):
    def block(j, p):
        wait(pool, s.gates_ready, j * 6 - 6)
        pool.tensor_copy(k.lw[p][:, :, :], k.lru_w[:, :, bass.ds(j, 1), :].rearrange("p a b d -> p (a b) d"))\
            .then_inc(s.blocks_ready, 1)

    pool.wait_ge(k.lru_w_loaded, 16)
    block(0, 0)
    block(1, 1)
    with pool.Fori(1, KT // 2) as i:
        block(i * 2, 0)
        block(i * 2 + 1, 1)


def b_scalar(act, k, s):
    def gates(j, t):
        for c, (dst, bias) in enumerate(((k.rb, BA), (k.ib, BX))):
            wait_apart(act, s.gates_ready, j * 6 + (2 * t + c + 1), s.act_passed)
            act.activation(dst[:, tg(t)], k.bank[3 + 2 * c + t % 2][:, 0:TG], ACT.Sigmoid,
                           bias=k.vec[:, bias, bass.ds(j, 1)]).then_inc(s.gates_used, 1)

    def decay(j):
        wait_apart(act, s.gates_used, j * 6 + 6, s.act_passed)
        act.activation(k.tb[:, :], k.rb[:, :], ACT.Tanh, scale=k.par[:, 2, bass.ds(j, 1)]).then_inc(s.decay, 1)
        act.activation(k.rb[:, :], k.rb[:, :], ACT.Exp, scale=k.par[:, 3, bass.ds(j, 1)]).then_inc(s.decay, 1)
        act.wait_ge(s.decay, j * 3 + 2)
        wait(act, s.out_lo, j * 1)
        act.activation(k.z[:, :], k.rb[:, :], ACT.Square).then_inc(s.decay, 1)

    def tail(j):
        act.wait_ge(s.mult2, j * 1 + 1)
        act.activation(k.tb[:, :], k.tb[:, :], ACT.Sqrt).then_inc(s.mult, 1)
        wait_apart(act, s.ob_ready, j * 1 + 1, s.act_passed)
        act.activation(k.o_hi[:, bass.ds(j, 1), :].rearrange("p a t -> p (a t)"), k.z[:, :], ACT.Copy)\
            .then_inc(s.out_hi, 1)

    def block(j, p, i, before):
        for t in range(NT):
            act.wait_ge(s.unit_ready, j * 6 + (t + 1))
            wait(act, s.conv, j * 8)
            act.activation(k.xr[:, 3 + t * TG:3 + (t + 1) * TG], k.bank[t][:, 0:TG], ACT.Copy).then_inc(s.unit_used, 1)
            if before:
                gates(j - 1, t)
        split_hi(act, k, Slab(SLAB_B, 4, i, 4 + 2 * p), 2 * p)
        if before:
            decay(j - 1)
        for t in range(NT):
            act.wait_ge(s.unit_ready, j * 6 + (3 + t + 1))
            act.activation(k.yb[p][:, tg(t)], k.bank[t][:, 0:TG], ACT.Gelu_apprx_tanh).then_inc(s.unit_used, 1)
        split_hi(act, k, Slab(SLAB_B, 4, i, 5 + 2 * p), 2 * p + 1)
        if before:
            tail(j - 1)

    s.memory_free(act)
    act.wait_ge(k.par_ready, 1)
    branch_b(act, block)
    for t in range(NT):
        gates(KT - 1, t)
    decay(KT - 1)
    tail(KT - 1)


def b_vector(dve, k, s):
    def gated(j):
        dve.wait_ge(s.gates_used, j * 6 + 6)
        dve.tensor_tensor(k.ib[:, :], k.ib[:, :], k.xc[:, :], ALU.mult).then_inc(s.gated_in, 1)

    def mult2(j):
        dve.wait_ge(s.decay, j * 3 + 3)
        dve.scalar_tensor_tensor(k.tb[:, :], k.z[:, :], 1.0, k.tb[:, :], ALU.add, ALU.mult).then_inc(s.mult2, 1)

    def tail(j, p):
        one = bass.ds(j, 1)
        dve.wait_ge(s.mult, j * 1 + 1)
        dve.wait_ge(s.gated_in, j * 1 + 1)
        dve.tensor_tensor(k.ib[:, :], k.ib[:, :], k.tb[:, :], ALU.mult).then_inc(s.driven, 1)
        dve.wait_ge(s.driven, j * 1 + 1)
        dve.tensor_tensor_scan(k.tb[:, 0:SEQ], k.rb[:, 0:SEQ], k.ib[:, 0:SEQ], 0.0, ALU.mult, ALU.add)\
            .then_inc(s.states, 1)
        dve.tensor_tensor(k.tb[:, SEQ:T], k.rb[:, SEQ:T], k.h0[:, one, :].rearrange("p a b -> p (a b)"), ALU.mult)\
            .then_inc(s.states, 1)
        dve.wait_ge(s.states, j * 5 + 2)
        dve.tensor_tensor(k.tb[:, SEQ:T], k.tb[:, SEQ:T], k.ib[:, SEQ:T], ALU.add).then_inc(s.states, 1)
        dve.wait_ge(s.states, j * 5 + 3)
        dve.tensor_copy(k.lru_out[:, one, 0:1].rearrange("p a b -> p (a b)"), k.tb[:, SEQ - 1:SEQ]).then_inc(s.states, 1)
        dve.tensor_copy(k.lru_out[:, one, 1:9].rearrange("p a b -> p (a b)"), k.tb[:, SEQ:T]).then_inc(s.states, 1)
        dve.tensor_tensor(k.z[:, :], k.tb[:, :], k.yb[p][:, :], ALU.mult).then_inc(s.ob_ready, 1)
        dve.wait_ge(s.out_hi, j * 1 + 1)
        dve.tensor_tensor(k.o_lo[:, one, :].rearrange("p a t -> p (a t)"), k.z[:, :],
                          k.o_hi[:, one, :].rearrange("p a t -> p (a t)").bitcast(F32), ALU.subtract)\
            .then_inc(s.out_lo, 1)

    def block(j, p, i, before):
        one = bass.ds(j, 1)
        w = [k.vec[:, CW0 + n, one] for n in range(4)]

        def old(n):
            return k.conv_s[:, one, n * DEC:(n + 1) * DEC].rearrange("p a b -> p (a b)")

        split_lo(dve, k, Slab(SLAB_B, 4, i, 4 + 2 * p), 2 * p)
        if before:
            gated(j - 1)
        dve.wait_ge(s.unit_used, j * 6 + 3)
        wait(dve, s.gated_in, j * 1)
        dve.tensor_scalar(k.xc[:, 0:SEQ], k.xr[:, 0:SEQ], w[0], k.vec[:, CB, one], ALU.mult, ALU.add)\
            .then_inc(s.conv, 1)
        dve.tensor_scalar(k.xc[:, SEQ:T], old(0), w[0], k.vec[:, CB, one], ALU.mult, ALU.add).then_inc(s.conv, 1)
        for n in range(1, 4):
            dve.wait_ge(s.conv, j * 8 + 2 * n)
            dve.scalar_tensor_tensor(k.xc[:, 0:SEQ], k.xr[:, n:n + SEQ], w[n], k.xc[:, 0:SEQ], ALU.mult, ALU.add)\
                .then_inc(s.conv, 1)
            dve.scalar_tensor_tensor(k.xc[:, SEQ:T], old(n) if n < 3 else k.xr[:, SEQ + 3:T + 3], w[n],
                                     k.xc[:, SEQ:T], ALU.mult, ALU.add).then_inc(s.conv, 1)
            if n == 2:
                dve.tensor_copy(k.conv_po[:, one, :].rearrange("p a b -> p (a b)"), k.xr[:, SEQ:SEQ + 3])\
                    .then_inc(s.kept, 1)
                dve.tensor_copy(k.conv_so[:, one, 0:2 * DEC].rearrange("p a b -> p (a b)"),
                                k.conv_s[:, one, DEC:3 * DEC].rearrange("p a b -> p (a b)")).then_inc(s.kept, 1)
                dve.tensor_copy(k.conv_so[:, one, 2 * DEC:3 * DEC].rearrange("p a b -> p (a b)"),
                                k.xr[:, SEQ + 3:T + 3]).then_inc(s.kept, 1)
        if before:
            mult2(j - 1)
        split_lo(dve, k, Slab(SLAB_B, 4, i, 5 + 2 * p), 2 * p + 1)
        if before:
            tail(j - 1, 1 - p)

    s.memory_free(dve)
    dve.memset(k.xr[:, 0:3], 0.0).then_inc(s.pad, 1)
    dve.wait_ge(s.pad, 1)
    branch_b(dve, block)
    gated(KT - 1)
    mult2(KT - 1)
    tail(KT - 1, 1)



def out_scalar(act, k, s):
    act.wait_ge(s.merge.up_ready, 3 * KT)
    act.dma_start(k.x[:, :, :].rearrange("p m t -> p (m t)"), k.x_dram).then_inc(s.x_loaded, 16)
    act.wait_ge(s.merge.m_ready, 3 * KT)
    for t in range(NT):
        act.activation(k.h_hi[:, :, tg(t)], k.m[:, :, tg(t)], ACT.Copy).then_inc(s.m_hi, 1)
    for c in range(KT):
        act.wait_ge(s.unit_ready, 3 * c + 3)
        split_hi(act, k, Slab(SLAB_OUT, 4, 1, c), c % 4)
    act.wait_ge(s.m_lo, NT)
    for c in (4, 5):
        split_hi(act, k, Slab(SLAB_FFN2, 6, 0, c), c)


def out_vector(dve, k, s):
    for t in range(NT):
        dve.wait_ge(s.m_hi, t + 1)
        dve.tensor_tensor(k.h_lo[:, :, tg(t)], k.m[:, :, tg(t)], k.h_hi[:, :, tg(t)].bitcast(F32), ALU.subtract)\
            .then_inc(s.m_lo, 1)
    dve.wait_ge(s.x_loaded, 16)
    for c in range(KT):
        for t in range(NT):
            dve.wait_ge(s.unit_ready, 3 * c + t + 1)
            dve.tensor_tensor(k.x[:, c, tg(t)], k.x[:, c, tg(t)], k.bank[t][:, 0:TG], ALU.add).then_inc(s.unit_used, 1)
        split_lo(dve, k, Slab(SLAB_OUT, 4, 1, c), c % 4)
    for c in (4, 5):
        split_lo(dve, k, Slab(SLAB_FFN2, 6, 0, c), c)


def out_tensor(pe, k, s):
    for c in range(KT):
        pe.wait_ge(k.slab_ready, SLAB_OUT + c + 1)
        for t in range(NT):
            if c == 0:
                pe.wait_ge(s.m_lo, t + 1)
            wait(pe, s.unit_used, 3 * c + t - 2)
            product(pe, k, k.bank[t][:, 0:TG], c % 4, k.h_hi, k.h_lo, tg(t)).then_inc(s.unit_ready, 1)



def params_scalar(act, k, s):
    act.wait_ge(s.arg, 5)
    for dst, n in ((2, 2), (4, 4), (5, 5)):
        act.activation(k.tmp[:, dst, :], k.tmp[:, n, :], ACT.Exp).then_inc(s.exp, 1)


def params_vector(dve, k, s):
    lb, oml, c8, neg_c8 = (k.par[:, n, :] for n in range(4))
    mx, x, z, w, e0, e1, q, s2 = (k.tmp[:, n, :] for n in range(8))
    l0, l1, lam = k.vec[:, LB0, :], k.vec[:, LB1, :], k.vec[:, LAM, :]
    done = [0]

    def then(ins):
        done[0] += 1
        ins.then_inc(s.arg, 1)
        dve.wait_ge(s.arg, done[0])

    dve.memset(k.eps[:, :], EPS).then_inc(s.eps, 1)
    dve.wait_ge(k.vec_loaded, 16)
    then(dve.tensor_tensor(mx, l0, l1, ALU.max))
    then(dve.tensor_tensor(e0, l0, mx, ALU.subtract))
    then(dve.tensor_tensor(e1, l1, mx, ALU.subtract))
    then(dve.tensor_scalar(x, lam, -1.0, None, ALU.mult))
    then(dve.tensor_tensor(z, x, lam, ALU.min))
    dve.wait_ge(s.exp, 3)
    then(dve.tensor_tensor(w, e0, e1, ALU.add))
    then(dve.reciprocal(w, w))
    then(dve.tensor_tensor(lb, e0, w, ALU.mult))
    then(dve.tensor_scalar(oml, lb, -1.0, 1.0, ALU.mult, ALU.add))
    then(dve.tensor_scalar(w, z, 2.0, None, ALU.add))
    then(dve.reciprocal(w, w))
    then(dve.tensor_tensor(z, z, w, ALU.mult))
    then(dve.tensor_tensor(s2, z, z, ALU.mult))
    then(dve.tensor_scalar(q, s2, 1.0 / 17, None, ALU.mult))
    for n in (15, 13, 11, 9, 7, 5, 3):
        then(dve.scalar_tensor_tensor(q, q, 1.0 / n, s2, ALU.add, ALU.mult))
    then(dve.scalar_tensor_tensor(q, q, 1.0, z, ALU.add, ALU.mult))
    then(dve.tensor_scalar(x, x, 0.0, 8.0, ALU.max, ALU.mult))
    then(dve.scalar_tensor_tensor(c8, q, 16.0, x, ALU.mult, ALU.add))
    dve.tensor_scalar(neg_c8, c8, -1.0, None, ALU.mult).then_inc(k.par_ready, 1)



def build(nc, x_t, w_slabs, lru_w, vec, state_hgrn, state_lru, state_conv, consts,
          y_out, hgrn_p, hgrn_s, lru_out, conv_p, conv_s):
    k = Names(w_slabs=w_slabs, state_hgrn=state_hgrn, hgrn_p=hgrn_p, hgrn_s=hgrn_s)
    k.x_dram = nc.dram_tensor("x_kept", (P, KT * T), F32, kind="Internal").ap()
    k.m_dram = nc.dram_tensor("m_kept", (KT, P, T), F32, kind="Internal").ap()
    x_t = x_t.rearrange("(m p) t -> p m t", p=P)
    y_out = y_out.rearrange("(m p) t -> p m t", p=P)

    class Region:
        def __init__(self, start, end):
            self.at, self.end = start, end

        def put(self, name, shape, dtype):
            size = {F32: 4, F32R: 4, BF16: 2, U8: 1}[dtype]
            for n in shape[1:]:
                size *= n
            t = nc.alloc_sbuf_tensor_at(name, list(shape), dtype, offset=self.at)
            self.at += (size + 31) // 32 * 32
            assert self.at <= self.end, (name, self.at, self.end)
            return t

    ACTS = KT * T * 4
    fixed = Region(1280, 8704)
    k.vec = fixed.put("vec", [P, NVEC, KT], F32)
    k.par = fixed.put("par", [P, 4, KT], F32)
    k.tmp = fixed.put("tmp", [P, 8, KT], F32)
    k.eps = fixed.put("eps", [P, 1], F32)
    k.consts = fixed.put("consts", [P, 4, P], F32)
    k.ident, k.ones_d, k.ones_h = (k.consts[:, n, :] for n in range(3))
    k.mask = fixed.put("mask", [P, P], U8)
    k.reset = fixed.put("reset", [P, SEQ], BF16)
    k.conv_s = fixed.put("conv_state", [P, KT, 3 * DEC], F32)
    k.conv_so = fixed.put("conv_state_new", [P, KT, 3 * DEC], F32)
    k.conv_po = fixed.put("conv_state_prompt", [P, KT, 3], F32)
    k.h0 = fixed.put("lru_state", [P, KT, DEC], F32)
    k.lru_out = fixed.put("lru_state_new", [P, KT, DEC + 1], F32)

    acts = Region(8704, 8704 + 2 * ACTS)
    k.h_hi = acts.put("h_hi", [P, KT, T], F32R)
    k.h_lo = acts.put("h_lo", [P, KT, T], F32R)
    k.y = Region(8704, 8704 + ACTS).put("y", [P, KT, T], F32)

    second = acts.end
    outs = Region(second, second + 2 * ACTS)
    k.o_hi = outs.put("o_hi", [P, KT, T], F32R)
    k.o_lo = outs.put("o_lo", [P, KT, T], F32R)
    ffn = Region(second, second + 2 * ACTS)
    k.x = ffn.put("x", [P, KT, T], F32)
    k.hid_hi = ffn.put("hid_hi", [P, 2, T], F32R)
    k.hid_lo = ffn.put("hid_lo", [P, 2, T], F32R)
    k.sq8 = [ffn.put("sq8_0", [P, KT, TG], F32)]

    ring = Region(outs.end, outs.end + 4096 * 14)
    k.raw = [ring.put(f"raw{n}", [P, KT * P], F32) for n in range(2)]
    k.w_hi, k.w_lo = [], []
    for n in range(6):
        if n == 4:
            work = ring.at
        k.w_hi.append(ring.put(f"w_hi{n}", [P, KT * P], F32R))
        k.w_lo.append(ring.put(f"w_lo{n}", [P, KT * P], F32R))

    end = 229344
    r = Region(ring.at, end)
    k.gate = r.put("gate", [P, T], F32)
    k.hid = [r.put(f"hid{n}", [P, TG], F32) for n in range(2)]
    k.rstd = r.put("rstd", [P, T], F32)
    k.htmp = [r.put(f"htmp{n}", [P, TG], F32) for n in range(4)]
    k.sq8.append(r.put("sq8_1", [P, KT, TG], F32))
    k.sumsq = [r.put(f"sumsq{n}", [P, TG], F32) for n in range(2)]

    r = Region(work, end)
    k.f = r.put("f", [P, T], F32)
    k.b = r.put("b", [P, SEQ], F32)
    k.q = r.put("q", [P, T], F32)
    k.v = r.put("v", [P, TILES + 1, P], F32)
    k.ke = r.put("ke", [P, T], F32)
    k.qe = r.put("qe", [P, T], F32)
    k.sg = r.put("sg", [P, T], F32)
    k.ss = r.put("ss", [P, DEC, P], F32)
    k.vm = r.put("vm", [P, 4, P], F32)
    k.el = r.put("el", [P, 24], F32)
    k.s = [r.put(f"s{n}", [P, P], F32) for n in range(4)]
    k.s_out = r.put("s_out", [P, P], F32)
    k.kt = [r.put(f"kt{n}", [P, P], F32) for n in range(2)]
    k.sc = [r.put(f"sc{n}", [P, P], F32) for n in range(2)]
    k.ue = [r.put(f"ue{n}", [P, 2, P], F32) for n in range(2)]
    k.sq = r.put("sq", [P, T], F32)

    r = Region(work, end)
    k.sgt_a = r.put("sgt_a", [P, T], F32)
    k.mt = [r.put(f"mt{n}", [P, T], F32) for n in range(2)]

    r = Region(work, end)
    k.rb = r.put("rb", [P, T], F32)
    k.tb = r.put("tb", [P, T], F32)
    k.ib = r.put("ib", [P, T], F32)
    k.xr = r.put("xr", [P, T + 3], F32)
    k.xc = r.put("xc", [P, T], F32)
    k.yb = [r.put(f"yb{n}", [P, T], F32) for n in range(2)]
    k.z = r.put("z", [P, T], F32)
    k.lru_w = r.put("lru_w", [P, 2, KT, P], F32)
    k.lw = [r.put(f"lw{n}", [P, 2, P], F32) for n in range(2)]

    r = Region(work, end)
    k.m = r.put("m", [P, KT, T], F32)
    k.sgt_b = r.put("sgt_b", [P, T], F32)
    k.mtb = r.put("mtb", [P, T], F32)

    with ExitStack() as ctx:
        k.bank = [ctx.enter_context(nc.psum_tensor(f"bank{n}", [P, 512], F32)) for n in range(8)]

        def sem(name):
            return ctx.enter_context(nc.semaphore(name))

        def stage(prefix, names, **fields):
            s = Names(**fields)
            for name in names.split():
                s[name] = sem(f"{prefix}_{name}")
            return s

        k.slab_loaded = [sem("slab_loaded0"), sem("slab_loaded1")]
        for name in ("slab_hi", "slab_ready", "x_spilled", "vec_loaded", "consts_loaded", "lru_w_loaded",
                     "states_loaded", "reset_ready", "par_ready", "stored"):
            k[name] = sem(name)
        x_loaded = [sem(f"x_loaded{t}") for t in range(NT)]

        NORM = "squared tree summed mean_ready ln rstd_ready h_ready h_hi h_lo"
        FFN = "gate_ready gate_used up_ready hidden hidden_hi hidden_lo down_ready down_used"
        par = stage("par", "arg exp eps")
        n1 = stage("n1", NORM, gain=G1, spill=False, final=False)
        f1 = stage("f1", FFN, first=SLAB_FFN1, next_slabs=4, norm=n1)
        nm = stage("nm", NORM, gain=GMIX, spill=True, final=False)
        a = stage("a", "unit_ready unit_used kt_ready kt_used sc_ready sc_used u_ready u_used state o_ready "
                  "o_used ss_new ss_loaded ss_stored pstate_ready pstate_stored vm_ready squared mean_ready ln "
                  "rstd scaled gated out_hi out_lo f_ready logf cum key exp_minus exp_plus el_s el_p ke_s "
                  "ke_ready qe_s qe_ready vt_ready v_ready zeroed act_passed dve_passed", norm=nm)
        ma = stage("ma", "gate_ready gate_used up_ready up_used", first=SLAB_MA, spill=True,
                   stored=[sem("ma_stored0"), sem("ma_stored1")])
        ma.multiplied = ma.up_used
        b = stage("b", "unit_ready unit_used conv kept blocks_ready gates_ready gates_used decay mult2 mult "
                  "gated_in driven states ob_ready out_hi out_lo pad act_passed")
        mb = stage("mb", "gate_ready gate_used up_ready up_used m_ready", first=SLAB_MB, spill=False,
                   m_loaded=sem("m_loaded"))
        mb.multiplied = mb.up_used
        o = stage("o", "x_loaded m_hi m_lo unit_ready unit_used", merge=mb)
        n2 = stage("n2", NORM, gain=G2, spill=False, final=False)
        f2 = stage("f2", FFN, first=SLAB_FFN2, next_slabs=0, norm=n2)
        n3 = stage("n3", NORM, gain=GFIN, spill=False, final=True)

        n1.x_ready = lambda eng, t: eng.wait_ge(x_loaded[t], 16)
        nm.x_ready = lambda eng, t: eng.wait_ge(f1.down_used, (PAIRS - 1) * 24 + 8 * (t + 1))
        n2.x_ready = lambda eng, t: eng.wait_ge(o.unit_used, 3 * (KT - 1) + t + 1)
        n3.x_ready = lambda eng, t: eng.wait_ge(f2.down_used, (PAIRS - 1) * 24 + 8 * (t + 1))

        def ma_banks(pe):
            pe.wait_ge(a.unit_used, UNITS * HEADS)

        def ma_branch(pe):
            pe.wait_ge(a.out_lo, HEADS)

        def b_banks(pe):
            pe.wait_ge(ma.gate_used, 3 * KT)
            pe.wait_ge(ma.up_used, 3 * KT)

        def b_memory(eng):
            for n in range(2):
                eng.wait_ge(ma.stored[n], 16 * KT // 2)
            eng.wait_ge(a.ss_stored, 16 * HEADS)
            eng.wait_ge(a.pstate_stored, 16 * HEADS)

        def mb_banks(pe):
            pe.wait_ge(b.unit_used, 6 * KT)
            pe.wait_ge(b.gates_used, 6 * KT)

        def mb_branch(pe):
            pe.wait_ge(b.out_lo, KT)

        ma.banks_free, ma.branch_done, ma.sgt = ma_banks, ma_branch, k.sgt_a
        b.banks_free, b.memory_free = b_banks, b_memory
        mb.banks_free, mb.branch_done, mb.sgt = mb_banks, mb_branch, k.sgt_b

        block = ctx.enter_context(nc.Block())

        @block.sync
        def _(sp):
            sp.dma_start(k.vec[:, :, :], vec).then_inc(k.vec_loaded, 16)
            for n in range(SLAB_FFN1, 2):
                load_slab(sp, k, Slab(0, 2, 0, n))
            sp.dma_start(k.consts[:, :, :], consts).then_inc(k.consts_loaded, 16)
            sp.dma_start(k.h0[:, :, :], state_lru).then_inc(k.states_loaded, 16)
            sp.dma_start(k.conv_s[:, :, :], state_conv).then_inc(k.states_loaded, 16)
            with sp.Fori(1, FFN_SLABS // 2) as i:
                load_slab(sp, k, Slab(SLAB_FFN1, 2, i, 0))
                load_slab(sp, k, Slab(SLAB_FFN1, 2, i, 1))
            a_sync(sp, k, a)
            for c in range(4):
                load_slab(sp, k, Slab(SLAB_MA, 4, 0, c))
            a_states(sp, k, a, HEADS - 2, HEADS - 1)
            for c in range(4):
                load_slab(sp, k, Slab(SLAB_MA, 4, 1, c))
            a_states(sp, k, a, HEADS - 1, None)
            with sp.Fori(4, (SLAB_B - SLAB_MA) // 2) as i:
                load_slab(sp, k, Slab(SLAB_MA, 2, i, 0))
                load_slab(sp, k, Slab(SLAB_MA, 2, i, 1))
            for c in range(4):
                load_slab(sp, k, Slab(SLAB_B, 4, 0, c))
            b_memory(sp)
            sp.wait_ge(a.out_lo, HEADS)
            sp.dma_start(k.lru_w[:, :, :, :], lru_w).then_inc(k.lru_w_loaded, 16)
            with sp.Fori(2, (SLAB_OUT - SLAB_B) // 2) as i:
                load_slab(sp, k, Slab(SLAB_B, 2, i, 0))
                load_slab(sp, k, Slab(SLAB_B, 2, i, 1))
            sp.wait_ge(b.out_lo, KT)
            sp.dma_start(lru_out, k.lru_out[:, :, :]).then_inc(k.stored, 16)
            sp.dma_start(conv_p, k.conv_po[:, :, :]).then_inc(k.stored, 16)
            sp.dma_start(conv_s, k.conv_so[:, :, :]).then_inc(k.stored, 16)
            with sp.Fori(0, (SLABS - SLAB_OUT) // 2) as i:
                load_slab(sp, k, Slab(SLAB_OUT, 2, i, 0))
                load_slab(sp, k, Slab(SLAB_OUT, 2, i, 1))
            for t in range(NT):
                sp.wait_ge(n3.h_ready, (t + 1) * KT)
                sp.dma_start(y_out[:, :, tg(t)], k.y[:, :, tg(t)]).then_inc(k.stored, 16)
            sp.wait_ge(k.stored, 16 * (3 + NT))
            sp.wait_ge(a.ss_stored, 16 * HEADS)
            sp.wait_ge(a.pstate_stored, 16 * HEADS)

        @block.scalar
        def _(act):
            for t in range(NT):
                act.dma_start(k.x[:, :, tg(t)], x_t[:, :, tg(t)]).then_inc(x_loaded[t], 16)
            params_scalar(act, k, par)
            act.wait_ge(par.eps, 1)
            for n in range(2):
                split_hi(act, k, Slab(0, 2, 0, n), n)
            norm_scalar(act, k, n1)
            for n in range(2, 6):
                split_hi(act, k, Slab(0, 2, 0, n), n)
            ffn_scalar(act, k, f1)
            norm_scalar(act, k, nm)
            a_scalar(act, k, a)
            merge_scalar(act, k, ma)
            b_scalar(act, k, b)
            act.wait_ge(b.out_lo, KT)
            for m in range(KT):
                act.dma_start(k.m[:, m, :], k.m_dram[m]).then_inc(mb.m_loaded, 16)
            merge_scalar(act, k, mb)
            out_scalar(act, k, o)
            norm_scalar(act, k, n2)
            ffn_scalar(act, k, f2)
            norm_scalar(act, k, n3)

        @block.vector
        def _(dve):
            params_vector(dve, k, par)
            for n in range(2):
                split_lo(dve, k, Slab(0, 2, 0, n), n)
            norm_vector(dve, k, n1)
            for n in range(2, 6):
                split_lo(dve, k, Slab(0, 2, 0, n), n)
            ffn_vector(dve, k, f1)
            norm_vector(dve, k, nm)
            dve.wait_ge(k.reset_ready, 2)
            dve.wait_ge(k.consts_loaded, 16)
            dve.tensor_copy(k.mask[:, :], k.consts[:, 3, :]).then_inc(a.zeroed, 1)
            for n in range(2):
                dve.memset(k.sc[n][:, :], 0.0).then_inc(a.zeroed, 1)
            dve.wait_ge(a.zeroed, 3)
            a_vector(dve, k, a)
            merge_vector(dve, k, ma)
            dve.wait_ge(k.states_loaded, 32)
            b_vector(dve, k, b)
            merge_vector(dve, k, mb)
            out_vector(dve, k, o)
            norm_vector(dve, k, n2)
            ffn_vector(dve, k, f2)
            norm_vector(dve, k, n3)

        @block.gpsimd
        def _(pool):
            pool.memset(k.reset[:, :], 1.0).then_inc(k.reset_ready, 1)
            pool.wait_ge(k.reset_ready, 1)
            pool.memset(k.reset[:, 0:SEQ:CHUNK], 0.0).then_inc(k.reset_ready, 1)
            norm_gpsimd(pool, k, n1)
            norm_gpsimd(pool, k, nm)
            b_gpsimd(pool, k, b)
            norm_gpsimd(pool, k, n2)
            norm_gpsimd(pool, k, n3)

        @block.tensor
        def _(pe):
            pe.wait_ge(k.consts_loaded, 16)
            norm_tensor(pe, k, n1)
            ffn_tensor(pe, k, f1)
            norm_tensor(pe, k, nm)
            a_tensor(pe, k, a)
            merge_tensor(pe, k, ma)
            b_tensor(pe, k, b)
            merge_tensor(pe, k, mb)
            out_tensor(pe, k, o)
            norm_tensor(pe, k, n2)
            ffn_tensor(pe, k, f2)
            norm_tensor(pe, k, n3)



def slabs_of_columns(w):
    n = w.shape[1] // P
    return w.reshape(KT, P, n, P).transpose(2, 1, 0, 3).reshape(n, P, KT * P)


def kernel(**inputs):
    import numpy as np
    import concourse.bacc as bacc
    from concourse.bass_utils import run_bass_kernel_spmd

    a = {name: np.asarray(value) for name, value in inputs.items()}

    def ffn_slabs(n):
        gate, up = (slabs_of_columns(a[f"ffn{n}_w_{w}"][0]) for w in ("gate", "up"))
        down = a[f"ffn{n}_w_down"][0].reshape(FT, P, D)
        order = []
        for i in range(PAIRS):
            for f in (2 * i, 2 * i + 1):
                order += [gate[f], up[f]]
            order += [down[2 * i], down[2 * i + 1]]
        return order

    w_in = slabs_of_columns(a["w_in"][0])
    q, f, v, g, xr, yr, ga, gb = (w_in[KT * n:KT * (n + 1)] for n in range(8))
    order = ffn_slabs(1)
    for j in range(HEADS):
        order += [f[j], q[j], v[j], g[j]]
    up = slabs_of_columns(a["w_a_up"][0])
    for j in range(KT):
        order += [ga[j], up[j]]
    for j in range(KT):
        order += [xr[j], yr[j]]
    up = slabs_of_columns(a["w_b_up"][0])
    for j in range(KT):
        order += [gb[j], up[j]]
    order += list(slabs_of_columns(a["w_out"][0]))
    order += ffn_slabs(2)

    vectors = [a["ffn1_norm"][0], a["mix_norm"][0], a["ffn2_norm"][0], a["final_norm"], a["hgrn_out_norm"][0],
               a["conv_b"][0], *a["conv_w"][0], a["lru_b_a"][0], a["lru_b_x"][0], a["lru_lambda"][0],
               a["hgrn_lower_bounds"][0], a["hgrn_lower_bounds"][1]]
    chunk_of = np.arange(P) // CHUNK
    causal = (chunk_of[:, None] == chunk_of[None, :]) & (np.arange(P)[:, None] <= np.arange(P)[None, :])
    arrays = {
        "x_t": np.ascontiguousarray(np.concatenate([a["x_prompt"][0], a["x_sample"][:, 0]]).T),
        "w_slabs": np.stack(order),
        "lru_w": np.ascontiguousarray(np.stack([a["lru_w_a"][0], a["lru_w_x"][0]]).transpose(2, 0, 1, 3)),
        "vec": np.ascontiguousarray(np.stack(vectors).reshape(NVEC, KT, P).transpose(2, 0, 1)),
        "state_hgrn": np.ascontiguousarray(a["state_hgrn"][0].transpose(1, 2, 0, 3)).reshape(HEADS, P, DEC * P),
        "state_lru": np.ascontiguousarray(a["state_lru"][0].reshape(DEC, KT, P).transpose(2, 1, 0)),
        "state_conv": np.ascontiguousarray(a["state_conv"][0].reshape(DEC, 3, KT, P).transpose(3, 2, 1, 0))
        .reshape(P, KT, 3 * DEC),
        "consts": np.stack([np.eye(P, dtype=np.float32), np.full((P, P), 1.0 / D, np.float32),
                            np.full((P, P), 1.0 / P, np.float32), causal.astype(np.float32)], axis=1),
    }
    outs = {"y_t": (D, T), "hgrn_p": (HEADS, P, P), "hgrn_s": (HEADS, P, DEC * P), "lru": (P, KT, DEC + 1),
            "conv_p": (P, KT, 3), "conv_s": (P, KT, 3 * DEC)}

    nc = bacc.Bacc("TRN2", target_bir_lowering=False, num_devices=1, dynamic_dma_scratch_size=1024)
    args = [nc.dram_tensor(n, v.shape, mybir.dt.from_np(v.dtype), kind="ExternalInput").ap()
            for n, v in arrays.items()]
    args += [nc.dram_tensor(n, shape, F32, kind="ExternalOutput").ap() for n, shape in outs.items()]
    build(nc, *args)
    r = run_bass_kernel_spmd(nc, [arrays], core_ids=[0]).results[0]

    y = r["y_t"].T
    lru = r["lru"].transpose(2, 1, 0).reshape(DEC + 1, D)
    return (
        np.ascontiguousarray(y[:SEQ])[None],
        np.ascontiguousarray(y[SEQ:])[:, None],
        r["hgrn_p"][None, None],
        lru[None, :1],
        np.ascontiguousarray(r["conv_p"].transpose(2, 1, 0)).reshape(1, 1, 3, D),
        np.ascontiguousarray(r["hgrn_s"].reshape(HEADS, P, DEC, P).transpose(2, 0, 1, 3))[None],
        lru[None, 1:],
        np.ascontiguousarray(r["conv_s"].reshape(P, KT, 3, DEC).transpose(3, 2, 1, 0)).reshape(1, DEC, 3, D),
    )
```

```python
from contextlib import ExitStack

import concourse.bass as bass
from concourse import mybir

ALU = mybir.AluOpType
ACT = mybir.ActivationFunctionType
F32 = mybir.dt.float32
F32R = mybir.dt.float32r
BF16 = mybir.dt.bfloat16
U8 = mybir.dt.uint8

P = 128
D = 1024
KT = D // P
SEQ = 1024
DEC = 8
T = SEQ + DEC
NT = 3
TG = T // NT
FT = 2816 // P
PAIRS = FT // 2
HEADS = 8
CHUNK = 64
TILES = SEQ // P
EPS = 1e-6

(G1, GMIX, G2, GFIN, GO, CB, CW0, CW1, CW2, CW3, BA, BX, LAM, LB0, LB1) = range(15)
NVEC = 15

FFN_SLABS = 3 * FT
SLAB_FFN1 = 0
SLAB_A = SLAB_FFN1 + FFN_SLABS
SLAB_MA = SLAB_A + 4 * HEADS
SLAB_B = SLAB_MA + 2 * KT
SLAB_MB = SLAB_B + 2 * KT
SLAB_OUT = SLAB_MB + 2 * KT
SLAB_FFN2 = SLAB_OUT + KT
SLABS = SLAB_FFN2 + FFN_SLABS


class Names(dict):

    def __getattr__(self, name):
        return self[name]

    def __setattr__(self, name, value):
        self[name] = value


def tg(t):
    return slice(t * TG, (t + 1) * TG)


def wait(eng, sem, value):
    if not (isinstance(value, int) and value <= 0):
        eng.wait_ge(sem, value)


def wait_apart(eng, sem, value, passed):
    eng.wait_ge(sem, value)
    eng.sem_inc(passed)


class Slab:

    def __init__(self, first, per, i, c):
        self.number = i * per + (first + c)
        self.pair = i * (per // 2) + (first + c) // 2
        self.buf = (first + c) % 2



def load_slab(sp, k, slab):
    wait(sp, k.slab_ready, slab.number - 1)
    src = k.w_slabs[bass.ds(slab.number, 1)].rearrange("a p c -> p (a c)")
    sp.dma_start(k.raw[slab.buf][:, :], src).then_inc(k.slab_loaded[slab.buf], 16)


def split_hi(act, k, slab, slot):
    act.wait_ge(k.slab_loaded[slab.buf], slab.pair * 16 + 16)
    act.activation(k.w_hi[slot][:, :], k.raw[slab.buf][:, :], ACT.Copy).then_inc(k.slab_hi, 1)


def split_lo(dve, k, slab, slot):
    dve.wait_ge(k.slab_hi, slab.number + 1)
    dve.tensor_tensor(k.w_lo[slot][:, :], k.raw[slab.buf][:, :], k.w_hi[slot][:, :].bitcast(F32),
                      ALU.subtract).then_inc(k.slab_ready, 1)


def weight(k, slot, b):
    cols = slice(b * P, (b + 1) * P)
    return k.w_hi[slot][:, cols], k.w_lo[slot][:, cols]


def three(pe, out, w, x, start, stop):
    (wh, wl), (xh, xl) = w, x
    pe.matmul(out, wh, xh, start=start, stop=False)
    pe.matmul(out, wh, xl, start=False, stop=False)
    return pe.matmul(out, wl, xh, start=False, stop=stop)


def product(pe, k, out, slot, hi, lo, cols, tiles=range(KT)):
    for m in tiles:
        last = three(pe, out, weight(k, slot, m), (hi[:, m, cols], lo[:, m, cols]), m == 0, m == KT - 1)
    return last



def norm_square(act, k, s, t, m):
    n = KT * t + m
    s.x_ready(act, t, m)
    if n >= 4:
        act.wait_ge(s.added, 7 * ((n - 4) // KT) + max((n - 4) % KT, 1))
    act.activation(k.square[n % 4][:, :], k.x[:, m, tg(t)], ACT.Square).then_inc(s.squared, 1)


def norm_rstd(act, k, s, t):
    act.wait_ge(s.mean_ready, t + 1)
    act.activation(k.rstd[:, tg(t)], k.bank[s.bank][:, 0:TG], ACT.Ln, bias=k.eps[:, 0:1]).then_inc(s.ln, 1)
    act.wait_ge(s.ln, t + 1)
    act.activation(k.rstd[:, tg(t)], k.rstd[:, tg(t)], ACT.Exp, scale=-0.5).then_inc(s.rstd_ready, 1)


def norm_hi(act, k, s, t, m):
    if not s.final:
        act.wait_ge(s.h_ready, t * KT + m + 1)
        act.activation(k.h_hi[:, m, tg(t)], k.htmp[m % 4][:, :], ACT.Copy).then_inc(s.h_hi, 1)


def norm_behind_scalar(act, k, s, splits=lambda: None):
    for m in range(KT):
        norm_square(act, k, s, 0, m)
    for m in range(KT):
        norm_square(act, k, s, 1, m)
        if m == 5:
            norm_rstd(act, k, s, 0)
    for m in range(KT):
        norm_hi(act, k, s, 0, m)
        norm_square(act, k, s, 2, m)
        if m == 5:
            norm_rstd(act, k, s, 1)
    if s.spill:
        act.dma_start(k.x_dram, k.x[:, :, :].rearrange("p m t -> p (m t)")).then_inc(k.x_spilled, 16)
    for m in range(KT):
        norm_hi(act, k, s, 1, m)
    splits()
    norm_rstd(act, k, s, 2)
    for m in range(KT):
        norm_hi(act, k, s, 2, m)


def norm_first_scalar(act, k, s):
    for t in range(NT):
        for m in range(KT):
            norm_square(act, k, s, t, m)
        if t:
            norm_rstd(act, k, s, t - 1)
            for m in range(KT):
                norm_hi(act, k, s, t - 1, m)
        split_hi(act, k, Slab(0, 2, 0, t), t)
    norm_rstd(act, k, s, 2)
    for m in range(KT):
        norm_hi(act, k, s, 2, m)
    split_hi(act, k, Slab(0, 2, 0, 3), 3)


def norm_low(eng, k, s, t, m):
    eng.wait_ge(s.h_hi, t * KT + m + 1)
    eng.tensor_tensor(k.h_lo[:, m, tg(t)], k.htmp[m % 4][:, :], k.h_hi[:, m, tg(t)].bitcast(F32),
                      ALU.subtract).then_inc(s.h_lo_pool if on_pool(t, m) else s.h_lo, 1)


def on_pool(t, m):
    return t > 0 and m % 2 == 1


def lows(t, m, pool):
    return sum(on_pool(n // KT, n % KT) == pool for n in range(KT * t + m + 1))


def norm_gpsimd(pool, k, s):
    for t in range(NT):
        wait(pool, s.mean_ready, t - 1)
        for m in range(1, KT):
            pool.wait_ge(s.squared, KT * t + m + 1)
            if m > 1:
                pool.wait_ge(s.added, 7 * t + m - 1)
            before = k.square[0] if m == 1 else k.sumsq[t % 2]
            pool.tensor_tensor(k.sumsq[t % 2][:, :], before[:, :], k.square[m % 4][:, :], ALU.add)\
                .then_inc(s.added, 1)
    if not s.final:
        for n in range(KT, NT * KT):
            if on_pool(n // KT, n % KT):
                norm_low(pool, k, s, n // KT, n % KT)


def norm_mean(pe, k, s, t):
    pe.wait_ge(s.added, 7 * (t + 1))
    wait(pe, s.ln, t)
    pe.matmul(k.bank[s.bank][:, 0:TG], k.ones_d[:, :], k.sumsq[t % 2][:, :], start=True, stop=True)\
        .then_inc(s.mean_ready, 1)


def norm_ready(pe, s, t):
    pe.wait_ge(s.h_lo, lows(t, KT - 1, False))
    if t:
        pe.wait_ge(s.h_lo_pool, lows(t, KT - 1, True))


def norm_apply(dve, k, s, t, m):
    if m == 0:
        dve.wait_ge(s.rstd_ready, t + 1)
    if s.final:
        dve.scalar_tensor_tensor(k.y[:, m, tg(t)], k.x[:, m, tg(t)], k.vec[:, s.gain, m:m + 1],
                                 k.rstd[:, tg(t)], ALU.mult, ALU.mult).then_inc(s.h_ready, 1)
        return
    n = KT * t + m
    if n >= 4:
        dve.wait_ge(s.h_hi, n - 3)
        former = divmod(n - 4, KT)
        if on_pool(*former):
            dve.wait_ge(s.h_lo_pool, lows(*former, True))
        else:
            dve.wait_ge(s.h_lo, lows(*former, False))
    dve.scalar_tensor_tensor(k.htmp[m % 4][:, :], k.x[:, m, tg(t)], k.vec[:, s.gain, m:m + 1],
                             k.rstd[:, tg(t)], ALU.mult, ALU.mult).then_inc(s.h_ready, 1)
    if m and not on_pool(t, m - 1):
        norm_low(dve, k, s, t, m - 1)
    if m == KT - 1 and not on_pool(t, m):
        norm_low(dve, k, s, t, m)


def norm_first_vector(dve, k, s):
    for t in range(NT):
        split_lo(dve, k, Slab(0, 2, 0, t), t)
        for m in range(KT):
            norm_apply(dve, k, s, t, m)
    split_lo(dve, k, Slab(0, 2, 0, 3), 3)


def norm_behind_vector(dve, k, s, add):
    for m in range(KT):
        add(m)
        norm_apply(dve, k, s, 0, m)
    for t in (1, 2):
        for m in range(KT):
            norm_apply(dve, k, s, t, m)



def ffn_slot(s, c):
    return (c + s.shift) % 6


def ffn_tensor(pe, k, s):
    def unit(i, f, t, which):
        u = i * 6 + (3 * f + t)
        slot = ffn_slot(s, 2 * f + (which == "up"))
        if which == "gate":
            wait(pe, s.gate_used, u - 1)
            bank, ready = k.bank[(3 * f + t) % 2], s.gate_ready
        else:
            wait(pe, s.hidden, u - 1)
            bank, ready = k.bank[2 + (3 * f + t) % 2], s.up_ready
        product(pe, k, bank[:, 0:TG], slot, k.h_hi, k.h_lo, tg(t)).then_inc(ready, 1)

    def group(i, first=False, last=False):
        for f in range(2):
            if first and f == 0:
                for t in range(NT):
                    norm_ready(pe, s.norm, t)
                    for c, which in enumerate(("gate", "up")):
                        if t == 0:
                            pe.wait_ge(k.slab_ready, s.first + c + 1)
                            if c:
                                s.banks_read(pe)
                        unit(i, f, t, which)
                    if t == 0:
                        norm_mean(pe, k, s.norm, 2)
                continue
            for c, which in enumerate(("gate", "up")):
                pe.wait_ge(k.slab_ready, Slab(s.first, 6, i, 2 * f + c).number + 1)
                for t in range(NT):
                    unit(i, f, t, which)
        for f in range(2):
            pe.wait_ge(k.slab_ready, Slab(s.first, 6, i, 4 + f).number + 1)
        for t in range(NT):
            pe.wait_ge(s.hidden_lo, i * 6 + (3 + t + 1))
            for m in range(KT):
                wait(pe, s.down_used, i * 24 + (8 * t + m - 3))
                for f in range(2):
                    done = three(pe, k.bank[4 + m % 4][:, 0:TG], weight(k, ffn_slot(s, 4 + f), m),
                                 (k.hid_hi[:, f, tg(t)], k.hid_lo[:, f, tg(t)]), f == 0, f == 1)
                done.then_inc(s.down_ready, 1)
                if last and t and m == 3:
                    norm_mean(pe, k, s.next_norm, t - 1)

    group(0, first=True)
    with pe.Fori(1, PAIRS - 1) as i:
        group(i)
    group(PAIRS - 1, last=True)


def ffn_scalar(act, k, s):
    def ahead(i, last, c):
        if not last:
            split_hi(act, k, Slab(s.first, 6, i, c + 6), ffn_slot(s, c))
        elif s.next_slabs > c:
            split_hi(act, k, Slab(s.first + FFN_SLABS, 0, 0, c), c)

    def silu(i, f, t):
        u = i * 6 + (3 * f + t)
        act.wait_ge(s.gate_ready, u + 1)
        wait(act, s.hidden, u - 2)
        act.activation(k.gate[:, tg(t)], k.bank[(3 * f + t) % 2][:, 0:TG], ACT.Silu).then_inc(s.gate_used, 1)

    def high(i, f, t):
        act.wait_ge(s.hidden, i * 6 + (3 * f + t + 1))
        act.activation(k.hid_hi[:, f, tg(t)], k.hid[(3 * f + t) % 2][:, :], ACT.Copy).then_inc(s.hidden_hi, 1)

    def group(i, first=False, last=False):
        for f in range(2):
            if first and f == 0:
                for t in range(2):
                    silu(i, f, t)
                    high(i, f, t)
                    split_hi(act, k, Slab(s.first, 6, i, 4 + t), ffn_slot(s, 4 + t))
                silu(i, f, 2)
                ahead(i, last, 0)
                high(i, f, 2)
                ahead(i, last, 1)
                continue
            for t in range(NT):
                silu(i, f, t)
            ahead(i, last, 2 * f)
            for t in range(NT):
                high(i, f, t)
            ahead(i, last, 2 * f + 1)
        if last:
            norm_behind_scalar(act, k, s.next_norm)
            return
        act.wait_ge(s.down_ready, i * 24 + 24)
        ahead(i, last, 4)
        ahead(i, last, 5)

    group(0, first=True)
    with act.Fori(1, PAIRS - 1) as i:
        group(i)
    group(PAIRS - 1, last=True)


def ffn_vector(dve, k, s):
    def ahead(i, last, c):
        if not last:
            split_lo(dve, k, Slab(s.first, 6, i, c + 6), ffn_slot(s, c))
        elif s.next_slabs > c:
            split_lo(dve, k, Slab(s.first + FFN_SLABS, 0, 0, c), c)

    def hidden(i, f, t):
        u = i * 6 + (3 * f + t)
        dve.wait_ge(s.up_ready, u + 1)
        dve.wait_ge(s.gate_used, u + 1)
        wait(dve, s.hidden_hi, u - 1)
        dve.tensor_tensor(k.hid[(3 * f + t) % 2][:, :], k.gate[:, tg(t)], k.bank[2 + (3 * f + t) % 2][:, 0:TG],
                          ALU.mult).then_inc(s.hidden, 1)

    def low(i, f, t):
        dve.wait_ge(s.hidden_hi, i * 6 + (3 * f + t + 1))
        dve.tensor_tensor(k.hid_lo[:, f, tg(t)], k.hid[(3 * f + t) % 2][:, :], k.hid_hi[:, f, tg(t)].bitcast(F32),
                          ALU.subtract).then_inc(s.hidden_lo, 1)

    def group(i, first=False, last=False):
        for f in range(2):
            if first and f == 0:
                for t in range(2):
                    hidden(i, f, t)
                    low(i, f, t)
                    split_lo(dve, k, Slab(s.first, 6, i, 4 + t), ffn_slot(s, 4 + t))
                hidden(i, f, 2)
                ahead(i, last, 0)
                low(i, f, 2)
                ahead(i, last, 1)
                continue
            ahead(i, last, 2 * f)
            for t in range(NT):
                hidden(i, f, t)
                low(i, f, t)
            ahead(i, last, 2 * f + 1)

        def add(t, m):
            dve.wait_ge(s.down_ready, i * 24 + (8 * t + m + 1))
            dve.scalar_tensor_tensor(k.x[:, m, tg(t)], k.bank[4 + m % 4][:, 0:TG], 0.5, k.x[:, m, tg(t)],
                                     ALU.mult, ALU.add).then_inc(s.down_used, 1)

        for t in range(2 if last else NT):
            for m in range(KT):
                add(t, m)
        if last:
            norm_behind_vector(dve, k, s.next_norm, lambda m: add(2, m))
            return
        ahead(i, last, 4)
        ahead(i, last, 5)

    group(0, first=True)
    with dve.Fori(1, PAIRS - 1) as i:
        group(i)
    group(PAIRS - 1, last=True)



UNITS = 12
V_UNIT = 6
G_UNIT = 9


def f_or_q(u, core):
    return (u // 3, u % 3) if core else (u % 2, u // 2)



def branch_a(engine, body):
    body(0, True, False)
    body(1, True, True)
    with engine.Fori(2, HEADS) as j:
        body(j, True, True)
    body(HEADS, False, True)


def a_tensor(pe, k, s):
    def keys(h, n):
        tok = slice(n * P, (n + 1) * P)
        wait(pe, s.kt_used, h * 9 + n)
        pe.transpose(k.bank[4][:, 0:P], k.ke[:, tok], k.ident[:, :]).then_inc(s.kt_ready, 1)
        wait(pe, s.sc_used, h * 8 + n)
        pe.matmul(k.bank[5][:, 0:P], k.ke[:, tok], k.qe[:, tok], start=True, stop=True).then_inc(s.sc_ready, 1)

    def updates(h, n):
        pe.wait_ge(s.kt_used, h * 9 + (n + 1))
        wait(pe, s.u_used, h * 16 + 2 * n)
        for c in range(2):
            rows = slice(c * CHUNK, (c + 1) * CHUNK)
            pe.matmul(k.bank[6 + c][:, 0:P], k.kt[n % 2][rows, :], k.v[rows, n, :], start=True, stop=True)\
                .then_inc(s.u_ready, 1)

    def output(h, n):
        pe.wait_ge(s.state, h * 17 + (2 * n + 2))
        pe.wait_ge(s.sc_used, h * 8 + (n + 1))
        wait(pe, s.o_used, h * 9 + n)
        o = k.bank[3]
        for c in range(2):
            cols = slice(n * P + c * CHUNK, n * P + (c + 1) * CHUNK)
            pe.matmul(o[:, c * CHUNK:(c + 1) * CHUNK], k.s[(2 * n + c) % 4][:, :], k.qe[:, cols],
                      start=c == 0, stop=False, skip_group_check=True)
        pe.matmul(o[:, 0:P], k.v[:, n, :], k.sc[n % 2][:, :], start=False, stop=True, skip_group_check=True)\
            .then_inc(s.o_ready, 1)

    def slot(h, n):
        if 2 <= n < 10:
            output(h, n - 2)
        if 1 <= n < 9:
            updates(h, n - 1)
        if n == 0:
            pe.wait_ge(s.ke_ready, h * 1 + 1)
            pe.wait_ge(s.qe_ready, h * 1 + 1)
            pe.wait_ge(s.v_ready, h * 3 + 3)
        if n < 8:
            keys(h, n)
        if n == 8:
            pe.wait_ge(s.kt_used, h * 9 + 8)
            pe.transpose(k.bank[4][0:DEC, 0:P], k.ke[:, SEQ:T], k.ident[:, :]).then_inc(s.kt_ready, 1)
        if n in (9, 10):
            q = n - 9
            pe.wait_ge(s.kt_used, h * 9 + 9)
            pe.wait_ge(s.vm_ready, h * 2 + (q + 1))
            pe.wait_ge(s.u_used, h * 16 + 16)
            pe.matmul(k.bank[6 + q][:, 0:4 * P], k.kt[0][0:DEC, :], k.vm[0:DEC, :, :], start=True, stop=True)\
                .then_inc(s.u_ready, 1)
        if n == 11:
            pe.wait_ge(s.ss_new, h * 8 + 8)
            pe.wait_ge(s.o_used, h * 9 + 8)
            for b in range(DEC):
                last = pe.matmul(k.bank[3][:, b:b + 1], k.ss[:, b, :], k.qe[:, SEQ + b:SEQ + b + 1],
                                 start=True, stop=True)
            last.then_inc(s.o_ready, 1)

    def means(h):
        pe.wait_ge(s.squared, h * 1 + 1)
        pe.wait_ge(s.kt_used, h * 9 + 9)
        for t in range(NT):
            pe.matmul(k.bank[3 + t][:, 0:TG], k.ones_h[:, :], k.sq[:, tg(t)], start=True, stop=True)\
                .then_inc(s.mean_ready, 1)

    def turn(j, core):
        pe.wait_ge(s.unit_used, j * UNITS + (V_UNIT + 3))
        if core:
            pe.wait_ge(s.ln, (j - 1) * 3 + 3)
        for n in range(TILES + 1):
            rows = min(P, T - n * P)
            last = pe.transpose(k.bank[(6, 7, 4)[n // 4]][0:rows, (n % 4) * P:(n % 4 + 1) * P],
                                k.f[:, n * P:n * P + rows], k.ident[:, :])
            if n in (3, 7, 8):
                last.then_inc(s.vt_ready, 1)

    def iteration(j, proj, core):
        h = j - 1

        def free(c):
            wait(pe, s.unit_used, j * UNITS + (c - 2))
            return k.bank[c % 3]

        for half in range(12):
            u = half // 2
            if proj:
                c, t = f_or_q(u, core)
                if half % 2 == 0:
                    if t == 0:
                        pe.wait_ge(k.slab_ready, Slab(SLAB_A, 4, j, c).number + 1)
                    if not core and c == 0:
                        norm_ready(pe, s.norm, t)
                    bank = free(u)
                last = product(pe, k, bank[:, 0:TG], c, k.h_hi, k.h_lo, tg(t),
                               range(4 * (half % 2), 4 * (half % 2) + 4))
                if half % 2:
                    last.then_inc(s.unit_ready, 1)
                if not core and half == 1:
                    norm_mean(pe, k, s.norm, 2)
            if core:
                slot(h, half)
        if proj:
            pe.wait_ge(k.slab_ready, Slab(SLAB_A, 4, j, 2).number + 1)
        for c in range(3):
            if proj:
                bank = free(V_UNIT + c)
                product(pe, k, bank[:, 0:TG], 2, k.h_hi, k.h_lo, tg(c), range(0, 4))
            if core and c == 0:
                means(h)
            if proj:
                product(pe, k, bank[:, 0:TG], 2, k.h_hi, k.h_lo, tg(c), range(4, 8)).then_inc(s.unit_ready, 1)
        if proj:
            pe.wait_ge(k.slab_ready, Slab(SLAB_A, 4, j, 3).number + 1)
            for t in range(NT):
                bank = free(G_UNIT + t)
                product(pe, k, bank[:, 0:TG], 3, k.h_hi, k.h_lo, tg(t)).then_inc(s.unit_ready, 1)
                if t == 0:
                    turn(j, core)

    branch_a(pe, iteration)


def a_scalar(act, k, s):
    def slot(h, n):
        if 1 <= n < 9:
            m = n - 1
            for c in range(2):
                act.wait_ge(s.u_ready, h * 18 + (2 * m + c + 1))
                if m >= 2:
                    act.wait_ge(s.state, h * 17 + (2 * m - 1))
                act.activation(k.ue[m % 2][:, c, :], k.bank[6 + c][:, 0:P], ACT.Identity,
                               scale=k.el[:, 2 * m + c:2 * m + c + 1]).then_inc(s.u_used, 1)
        if n < 9:
            rows = P if n < 8 else DEC
            act.wait_ge(s.kt_ready, h * 9 + (n + 1))
            if n >= 2:
                act.wait_ge(s.u_ready, h * 18 + 2 * (n - 1))
            act.activation(k.kt[n % 2][0:rows, :], k.bank[4][0:rows, 0:P], ACT.Copy).then_inc(s.kt_used, 1)

    def iteration(j, proj, core):
        h = j - 1
        for half in range(12):
            u = half // 2
            if proj and half % 2:
                act.wait_ge(s.unit_ready, j * UNITS + (u + 1))
                c, t = f_or_q(u, core)
                if c == 0:
                    act.activation(k.f[:, tg(t)], k.bank[u % 3][:, 0:TG], ACT.Sigmoid).then_inc(s.unit_used, 1)
                else:
                    wait(act, s.qe_ready, j * 1)
                    act.activation(k.q[:, tg(t)], k.bank[u % 3][:, 0:TG], ACT.Silu).then_inc(s.unit_used, 1)
                if t == 2:
                    split_hi(act, k, Slab(SLAB_A, 4, j, 4 + c), c)
            if core:
                slot(h, half)
        if core:
            act.wait_ge(s.o_used, h * 9 + 9)
            wait(act, s.scaled, h * 1)
            act.activation(k.sq[:, :], k.qe[:, :], ACT.Square).then_inc(s.squared, 1)
        if proj:
            act.wait_ge(s.f_ready, j * 1 + 1)
            act.activation(k.b[:, :], k.f[:, 0:SEQ], ACT.Ln).then_inc(s.logf, 1)
        if core:
            for t in range(NT):
                act.wait_ge(s.mean_ready, h * 3 + (t + 1))
                act.activation(k.sq[:, tg(t)], k.bank[3 + t][:, 0:TG], ACT.Ln, bias=k.eps[:, 0:1]).then_inc(s.ln, 1)
        if proj:
            act.wait_ge(s.cum, j * 1 + 1)
            act.activation(k.ke[:, 0:SEQ], k.b[:, :], ACT.Exp, scale=-1.0).then_inc(s.exp_minus, 1)
            act.activation(k.b[:, :], k.b[:, :], ACT.Exp).then_inc(s.exp_plus, 1)
        if core:
            act.wait_ge(s.ln, h * 3 + 3)
            act.activation(k.sq[:, :], k.sq[:, :], ACT.Exp, scale=-0.5).then_inc(s.rstd, 1)
        if proj:
            act.wait_ge(s.ke_ready, j * 1 + 1)
        for c in range(3):
            if proj:
                act.wait_ge(s.unit_ready, j * UNITS + (V_UNIT + c + 1))
                act.activation(k.f[:, tg(c)], k.bank[c][:, 0:TG], ACT.Copy).then_inc(s.unit_used, 1)
            if core and c == 1:
                if isinstance(h, int) and h == 0:
                    act.wait_ge(k.x_spilled, 16)
                wait_apart(act, s.gated, h * 1 + 1, s.act_passed)
                act.activation(k.o_hi[:, bass.ds(h, 1), :].rearrange("p a t -> p (a t)"), k.qe[:, :],
                               ACT.Copy).then_inc(s.out_hi, 1)
        if proj:
            split_hi(act, k, Slab(SLAB_A, 4, j, 6), 2)
            for t in range(NT):
                act.wait_ge(s.unit_ready, j * UNITS + (G_UNIT + t + 1))
                wait(act, s.gated, j * 1)
                act.activation(k.sg[:, tg(t)], k.bank[t][:, 0:TG], ACT.Silu).then_inc(s.unit_used, 1)
                if t == 0:
                    for n, bank in enumerate((6, 7, 4)):
                        act.wait_ge(s.vt_ready, j * 3 + (n + 1))
                        rows, tiles = (P, 4) if n < 2 else (DEC, 1)
                        act.activation(k.v[0:rows, 4 * n:4 * n + tiles, :].rearrange("p a d -> p (a d)"),
                                       k.bank[bank][0:rows, 0:tiles * P], ACT.Copy).then_inc(s.v_ready, 1)
            split_hi(act, k, Slab(SLAB_A, 4, j, 7), 3)

    branch_a(act, iteration)


def a_vector(dve, k, s):
    def slot(h, n):
        if n == 0:
            dve.memset(k.s[0][:, :], 0.0).then_inc(s.state, 1)
        if 2 <= n < 10:
            m = n - 2
            dve.wait_ge(s.o_ready, h * 9 + (m + 1))
            dve.tensor_copy(k.qe[:, m * P:(m + 1) * P], k.bank[3][:, 0:P]).then_inc(s.o_used, 1)
        if 1 <= n < 9:
            for c in (2 * (n - 1), 2 * (n - 1) + 1):
                dve.wait_ge(s.u_used, h * 16 + (c + 1))
                dve.wait_ge(s.state, h * 17 + (c + 1))
                dve.scalar_tensor_tensor(k.s[(c + 1) % 4][:, :], k.s[c % 4][:, :], k.el[:, c:c + 1],
                                         k.ue[(n - 1) % 2][:, c % 2, :], ALU.mult, ALU.add).then_inc(s.state, 1)
        if n < 8:
            wait_apart(dve, s.sc_ready, h * 8 + (n + 1), s.dve_passed)
            dve.copy_predicated(k.sc[n % 2][:, :], k.mask[:, :], k.bank[5][:, 0:P]).then_inc(s.sc_used, 1)
        if n in (8, 9):
            q = n - 8
            if q:
                dve.wait_ge(s.u_ready, h * 18 + 17)
            dve.tensor_tensor(k.vm[0:DEC, :, :], k.v[0:DEC, 8:9, :].to_broadcast((DEC, 4, P)),
                              k.ident[0:DEC, 4 * q:4 * q + 4].unsqueeze(2).to_broadcast((DEC, 4, P)),
                              ALU.mult).then_inc(s.vm_ready, 1)
        if n in (9, 10):
            q = n - 9
            dve.wait_ge(s.u_ready, h * 18 + (17 + q))
            dve.wait_ge(s.ss_loaded, h * 16 + 16)
            for b in range(4 * q, 4 * q + 4):
                dve.scalar_tensor_tensor(k.ss[:, b, :], k.ss[:, b, :], k.el[:, 16 + b:17 + b],
                                         k.bank[6 + q][:, (b % 4) * P:(b % 4 + 1) * P],
                                         ALU.mult, ALU.add).then_inc(s.ss_new, 1)
        if n == 11:
            dve.wait_ge(s.o_ready, h * 9 + 9)
            dve.tensor_copy(k.qe[:, SEQ:T], k.bank[3][:, 0:DEC]).then_inc(s.o_used, 1)
            wait(dve, s.pstate_stored, h * 16)
            dve.wait_ge(s.state, h * 17 + 17)
            dve.tensor_copy(k.s_out[:, :], k.s[0][:, :]).then_inc(s.pstate_ready, 1)

    def iteration(j, proj, core):
        h = j - 1
        for half in range(12):
            if core:
                slot(h, half)
            if proj and half == 5:
                split_lo(dve, k, Slab(SLAB_A, 4, j, 4), 0)
                dve.wait_ge(s.unit_used, j * UNITS + (3 if core else 5))
                dve.tensor_scalar(k.f[:, :], k.f[:, :], k.par[:, 1, bass.ds(j, 1)], k.par[:, 0, bass.ds(j, 1)],
                                  ALU.mult, ALU.add).then_inc(s.f_ready, 1)
        if proj:
            split_lo(dve, k, Slab(SLAB_A, 4, j, 5), 1)
            dve.wait_ge(s.f_ready, j * 1 + 1)
            dve.tensor_copy(k.el[:, 16:24], k.f[:, SEQ:T]).then_inc(s.el_s, 1)
            dve.wait_ge(s.logf, j * 1 + 1)
            dve.tensor_tensor_scan(k.b[:, :], k.reset[:, :], k.b[:, :], 0.0, ALU.mult, ALU.add).then_inc(s.cum, 1)
            dve.wait_ge(s.el_s, j * 1 + 1)
            dve.tensor_scalar(k.f[:, :], k.f[:, :], -1.0, 1.0, ALU.mult, ALU.add).then_inc(s.key, 1)
            dve.wait_ge(s.key, j * 1 + 1)
            dve.tensor_copy(k.ke[:, SEQ:T], k.f[:, SEQ:T]).then_inc(s.ke_s, 1)
            dve.wait_ge(s.exp_minus, j * 1 + 1)
            dve.tensor_tensor(k.ke[:, 0:SEQ], k.ke[:, 0:SEQ], k.f[:, 0:SEQ], ALU.mult).then_inc(s.ke_ready, 1)
            dve.wait_ge(s.exp_plus, j * 1 + 1)
            dve.tensor_copy(k.el[:, 0:16], k.b[:, CHUNK - 1:SEQ:CHUNK]).then_inc(s.el_p, 1)
        if core:
            o = k.qe[:, :]
            dve.wait_ge(s.rstd, h * 1 + 1)
            dve.scalar_tensor_tensor(o, o, k.vec[:, GO, bass.ds(h, 1)], k.sq[:, :], ALU.mult, ALU.mult)\
                .then_inc(s.scaled, 1)
            dve.wait_ge(s.scaled, h * 1 + 1)
            dve.tensor_tensor(o, o, k.sg[:, :], ALU.mult).then_inc(s.gated, 1)
            dve.wait_ge(s.out_hi, h * 1 + 1)
            one = bass.ds(h, 1)
            dve.tensor_tensor(k.o_lo[:, one, :].rearrange("p a t -> p (a t)"), o,
                              k.o_hi[:, one, :].rearrange("p a t -> p (a t)").bitcast(F32),
                              ALU.subtract).then_inc(s.out_lo, 1)
        if proj:
            wait(dve, s.out_lo, j * 1)
            dve.wait_ge(s.unit_used, j * UNITS + 6)
            dve.tensor_copy(k.qe[:, SEQ:T], k.q[:, SEQ:T]).then_inc(s.qe_s, 1)
            dve.wait_ge(s.el_p, j * 1 + 1)
            dve.wait_ge(s.qe_s, j * 1 + 1)
            dve.tensor_tensor(k.qe[:, 0:SEQ], k.q[:, 0:SEQ], k.b[:, :], ALU.mult).then_inc(s.qe_ready, 1)
            split_lo(dve, k, Slab(SLAB_A, 4, j, 6), 2)
            split_lo(dve, k, Slab(SLAB_A, 4, j, 7), 3)

    branch_a(dve, iteration)


def a_sync(sp, k, s):
    def slabs(j):
        for c in range(4):
            load_slab(sp, k, Slab(SLAB_A, 4, j, c))

    slabs(0)
    slabs(1)
    a_states(sp, k, s, None, 0)
    slabs(2)
    with sp.Fori(3, HEADS) as j:
        a_states(sp, k, s, j - 3, j - 2)
        slabs(j)
    a_states(sp, k, s, HEADS - 3, HEADS - 2)


def a_states(sp, k, s, store, load):
    if store is not None:
        sp.wait_ge(s.ss_new, store * 8 + 8)
        sp.wait_ge(s.o_ready, store * 9 + 9)
        sp.dma_start(k.hgrn_s[bass.ds(store, 1)].rearrange("a p c -> p (a c)"),
                     k.ss[:, :, :].rearrange("p b d -> p (b d)")).then_inc(s.ss_stored, 16)
        sp.wait_ge(s.pstate_ready, store * 1 + 1)
        sp.dma_start(k.hgrn_p[bass.ds(store, 1)].rearrange("a p c -> p (a c)"), k.s_out[:, :])\
            .then_inc(s.pstate_stored, 16)
        sp.wait_ge(s.ss_stored, store * 16 + 16)
    if load is not None:
        sp.dma_start(k.ss[:, :, :].rearrange("p b d -> p (b d)"),
                     k.state_hgrn[bass.ds(load, 1)].rearrange("a p c -> p (a c)")).then_inc(s.ss_loaded, 16)



def merge_tensor(pe, k, s):
    def pair(i):
        for p in range(2):
            for c, (hi, lo) in enumerate(((k.h_hi, k.h_lo), (k.o_hi, k.o_lo))):
                slot = 2 * p + c
                pe.wait_ge(k.slab_ready, Slab(s.first, 4, i, slot).number + 1)
                for t in range(NT):
                    wait(pe, (s.gate_used, s.up_used)[c], i * 6 + (3 * p + t - 2))
                    if isinstance(i, int) and p == 0 and c == 1 and t == 0:
                        s.branch_done(pe)
                    product(pe, k, k.bank[3 * c + t][:, 0:TG], slot, hi, lo, tg(t))\
                        .then_inc((s.gate_ready, s.up_ready)[c], 1)

    s.banks_free(pe)
    pair(0)
    with pe.Fori(1, KT // 2) as i:
        pair(i)


def merge_scalar(act, k, s):
    def store(j, buf):
        act.wait_ge(s.up_used, j * 3 + 3)
        act.dma_start(k.m_dram[bass.ds(j, 1)].rearrange("a p t -> p (a t)"), k.mt[buf][:, :])\
            .then_inc(s.stored[buf], 16)

    def pair(i):
        first = isinstance(i, int)
        for p in range(2):
            for t in range(NT):
                u = i * 6 + (3 * p + t)
                act.wait_ge(s.gate_ready, u + 1)
                wait(act, s.multiplied, u - 2)
                act.activation(s.sgt[:, tg(t)], k.bank[t][:, 0:TG], ACT.Sigmoid).then_inc(s.gate_used, 1)
            split_hi(act, k, Slab(s.first, 4, i, 4 + 2 * p), 2 * p)
            if s.spill and not (first and p == 0):
                store(i * 2 + (p - 1), 1 - p)
            act.wait_ge(s.up_ready, i * 6 + 3 * (p + 1))
            split_hi(act, k, Slab(s.first, 4, i, 5 + 2 * p), 2 * p + 1)

    pair(0)
    with act.Fori(1, KT // 2) as i:
        pair(i)
    if s.spill:
        store(KT - 1, 1)


def merge_vector(dve, k, s):
    def pair(i):
        for p in range(2):
            split_lo(dve, k, Slab(s.first, 4, i, 4 + 2 * p), 2 * p)
            for t in range(NT):
                u = i * 6 + (3 * p + t)
                dve.wait_ge(s.up_ready, u + 1)
                dve.wait_ge(s.gate_used, u + 1)
                if s.spill:
                    if t == 0:
                        wait(dve, s.stored[p], i * 16)
                    dve.tensor_tensor(k.mt[p][:, tg(t)], s.sgt[:, tg(t)], k.bank[3 + t][:, 0:TG], ALU.mult)\
                        .then_inc(s.up_used, 1)
                else:
                    dve.tensor_tensor(k.mtb[:, tg(t)], s.sgt[:, tg(t)], k.bank[3 + t][:, 0:TG], ALU.mult)\
                        .then_inc(s.up_used, 1)
                    dve.wait_ge(s.up_used, u + 1)
                    at = (slice(None), bass.ds(i * 2 + p, 1), tg(t))
                    m = k.m[at].rearrange("p a t -> p (a t)")
                    dve.tensor_tensor(m, m, k.mtb[:, tg(t)], ALU.add).then_inc(s.m_ready, 1)
            split_lo(dve, k, Slab(s.first, 4, i, 5 + 2 * p), 2 * p + 1)

    if not s.spill:
        dve.wait_ge(s.m_loaded, 16 * KT)
    pair(0)
    with dve.Fori(1, KT // 2) as i:
        pair(i)




def branch_b(engine, body):
    body(0, 0, 0, False)
    body(1, 1, 0, True)
    with engine.Fori(1, KT // 2) as i:
        body(i * 2, 0, i, True)
        body(i * 2 + 1, 1, i, True)


def b_tensor(pe, k, s):
    def gates(j, p, t):
        if t == 0:
            pe.wait_ge(s.conv, j * 8 + 8)
            pe.wait_ge(s.blocks_ready, j * 1 + 1)
        wait(pe, s.gates_used, j * 6 + (2 if t == 2 else 0))
        for c in range(2):
            pe.matmul(k.bank[3 + 2 * c + t % 2][:, 0:TG], k.lw[p][:, c, :], k.xc[:, tg(t)],
                      start=True, stop=True).then_inc(s.gates_ready, 1)

    def block(j, p, i, before):
        for c in range(2):
            pe.wait_ge(k.slab_ready, Slab(SLAB_B, 4, i, 2 * p + c).number + 1)
            for t in range(NT):
                wait(pe, s.unit_used, j * 6 + (3 * c + t - 2))
                product(pe, k, k.bank[t][:, 0:TG], 2 * p + c, k.h_hi, k.h_lo, tg(t)).then_inc(s.unit_ready, 1)
                if before and c == 0:
                    gates(j - 1, 1 - p, t)

    s.banks_free(pe)
    branch_b(pe, block)
    for t in range(NT):
        gates(KT - 1, 1, t)


def b_gpsimd(pool, k, s):
    def block(j, p):
        wait(pool, s.gates_ready, j * 6 - 6)
        pool.tensor_copy(k.lw[p][:, :, :], k.lru_w[:, :, bass.ds(j, 1), :].rearrange("p a b d -> p (a b) d"))\
            .then_inc(s.blocks_ready, 1)

    pool.wait_ge(k.lru_w_loaded, 16)
    block(0, 0)
    block(1, 1)
    with pool.Fori(1, KT // 2) as i:
        block(i * 2, 0)
        block(i * 2 + 1, 1)


def b_scalar(act, k, s):
    def gates(j, t):
        for c, (dst, bias) in enumerate(((k.rb, BA), (k.ib, BX))):
            wait_apart(act, s.gates_ready, j * 6 + (2 * t + c + 1), s.act_passed)
            act.activation(dst[:, tg(t)], k.bank[3 + 2 * c + t % 2][:, 0:TG], ACT.Sigmoid,
                           bias=k.vec[:, bias, bass.ds(j, 1)]).then_inc(s.gates_used, 1)

    def decay(j):
        wait_apart(act, s.gates_used, j * 6 + 6, s.act_passed)
        act.activation(k.tb[:, :], k.rb[:, :], ACT.Tanh, scale=k.par[:, 2, bass.ds(j, 1)]).then_inc(s.decay, 1)
        act.activation(k.rb[:, :], k.rb[:, :], ACT.Exp, scale=k.par[:, 3, bass.ds(j, 1)]).then_inc(s.decay, 1)
        act.wait_ge(s.decay, j * 3 + 2)
        wait(act, s.out_lo, j * 1)
        act.activation(k.z[:, :], k.rb[:, :], ACT.Square).then_inc(s.decay, 1)

    def tail(j):
        act.wait_ge(s.mult2, j * 1 + 1)
        act.activation(k.tb[:, :], k.tb[:, :], ACT.Sqrt).then_inc(s.mult, 1)
        wait_apart(act, s.ob_ready, j * 1 + 1, s.act_passed)
        act.activation(k.o_hi[:, bass.ds(j, 1), :].rearrange("p a t -> p (a t)"), k.z[:, :], ACT.Copy)\
            .then_inc(s.out_hi, 1)

    def block(j, p, i, before):
        for t in range(NT):
            act.wait_ge(s.unit_ready, j * 6 + (t + 1))
            wait(act, s.conv, j * 8)
            act.activation(k.xr[:, 3 + t * TG:3 + (t + 1) * TG], k.bank[t][:, 0:TG], ACT.Copy).then_inc(s.unit_used, 1)
            if before:
                gates(j - 1, t)
        split_hi(act, k, Slab(SLAB_B, 4, i, 4 + 2 * p), 2 * p)
        if before:
            decay(j - 1)
        for t in range(NT):
            act.wait_ge(s.unit_ready, j * 6 + (3 + t + 1))
            act.activation(k.yb[p][:, tg(t)], k.bank[t][:, 0:TG], ACT.Gelu_apprx_tanh).then_inc(s.unit_used, 1)
        split_hi(act, k, Slab(SLAB_B, 4, i, 5 + 2 * p), 2 * p + 1)
        if before:
            tail(j - 1)

    s.memory_free(act)
    act.wait_ge(k.par_ready, 1)
    branch_b(act, block)
    for t in range(NT):
        gates(KT - 1, t)
    decay(KT - 1)
    tail(KT - 1)


def b_vector(dve, k, s):
    def gated(j):
        dve.wait_ge(s.gates_used, j * 6 + 6)
        dve.tensor_tensor(k.ib[:, :], k.ib[:, :], k.xc[:, :], ALU.mult).then_inc(s.gated_in, 1)

    def mult2(j):
        dve.wait_ge(s.decay, j * 3 + 3)
        dve.scalar_tensor_tensor(k.tb[:, :], k.z[:, :], 1.0, k.tb[:, :], ALU.add, ALU.mult).then_inc(s.mult2, 1)

    def tail(j, p):
        one = bass.ds(j, 1)
        dve.wait_ge(s.mult, j * 1 + 1)
        dve.wait_ge(s.gated_in, j * 1 + 1)
        dve.tensor_tensor(k.ib[:, :], k.ib[:, :], k.tb[:, :], ALU.mult).then_inc(s.driven, 1)
        dve.wait_ge(s.driven, j * 1 + 1)
        dve.tensor_tensor_scan(k.tb[:, 0:SEQ], k.rb[:, 0:SEQ], k.ib[:, 0:SEQ], 0.0, ALU.mult, ALU.add)\
            .then_inc(s.states, 1)
        dve.tensor_tensor(k.tb[:, SEQ:T], k.rb[:, SEQ:T], k.h0[:, one, :].rearrange("p a b -> p (a b)"), ALU.mult)\
            .then_inc(s.states, 1)
        dve.wait_ge(s.states, j * 5 + 2)
        dve.tensor_tensor(k.tb[:, SEQ:T], k.tb[:, SEQ:T], k.ib[:, SEQ:T], ALU.add).then_inc(s.states, 1)
        dve.wait_ge(s.states, j * 5 + 3)
        dve.tensor_copy(k.lru_out[:, one, 0:1].rearrange("p a b -> p (a b)"), k.tb[:, SEQ - 1:SEQ]).then_inc(s.states, 1)
        dve.tensor_copy(k.lru_out[:, one, 1:9].rearrange("p a b -> p (a b)"), k.tb[:, SEQ:T]).then_inc(s.states, 1)
        dve.tensor_tensor(k.z[:, :], k.tb[:, :], k.yb[p][:, :], ALU.mult).then_inc(s.ob_ready, 1)
        dve.wait_ge(s.out_hi, j * 1 + 1)
        dve.tensor_tensor(k.o_lo[:, one, :].rearrange("p a t -> p (a t)"), k.z[:, :],
                          k.o_hi[:, one, :].rearrange("p a t -> p (a t)").bitcast(F32), ALU.subtract)\
            .then_inc(s.out_lo, 1)

    def block(j, p, i, before):
        one = bass.ds(j, 1)
        w = [k.vec[:, CW0 + n, one] for n in range(4)]

        def old(n):
            return k.conv_s[:, one, n * DEC:(n + 1) * DEC].rearrange("p a b -> p (a b)")

        split_lo(dve, k, Slab(SLAB_B, 4, i, 4 + 2 * p), 2 * p)
        if before:
            gated(j - 1)
        dve.wait_ge(s.unit_used, j * 6 + 3)
        wait(dve, s.gated_in, j * 1)
        dve.tensor_scalar(k.xc[:, 0:SEQ], k.xr[:, 0:SEQ], w[0], k.vec[:, CB, one], ALU.mult, ALU.add)\
            .then_inc(s.conv, 1)
        dve.tensor_scalar(k.xc[:, SEQ:T], old(0), w[0], k.vec[:, CB, one], ALU.mult, ALU.add).then_inc(s.conv, 1)
        for n in range(1, 4):
            dve.wait_ge(s.conv, j * 8 + 2 * n)
            dve.scalar_tensor_tensor(k.xc[:, 0:SEQ], k.xr[:, n:n + SEQ], w[n], k.xc[:, 0:SEQ], ALU.mult, ALU.add)\
                .then_inc(s.conv, 1)
            dve.scalar_tensor_tensor(k.xc[:, SEQ:T], old(n) if n < 3 else k.xr[:, SEQ + 3:T + 3], w[n],
                                     k.xc[:, SEQ:T], ALU.mult, ALU.add).then_inc(s.conv, 1)
            if n == 2:
                dve.tensor_copy(k.conv_po[:, one, :].rearrange("p a b -> p (a b)"), k.xr[:, SEQ:SEQ + 3])\
                    .then_inc(s.kept, 1)
                dve.tensor_copy(k.conv_so[:, one, 0:2 * DEC].rearrange("p a b -> p (a b)"),
                                k.conv_s[:, one, DEC:3 * DEC].rearrange("p a b -> p (a b)")).then_inc(s.kept, 1)
                dve.tensor_copy(k.conv_so[:, one, 2 * DEC:3 * DEC].rearrange("p a b -> p (a b)"),
                                k.xr[:, SEQ + 3:T + 3]).then_inc(s.kept, 1)
        if before:
            mult2(j - 1)
        split_lo(dve, k, Slab(SLAB_B, 4, i, 5 + 2 * p), 2 * p + 1)
        if before:
            tail(j - 1, 1 - p)

    s.memory_free(dve)
    dve.memset(k.xr[:, 0:3], 0.0).then_inc(s.pad, 1)
    dve.wait_ge(s.pad, 1)
    branch_b(dve, block)
    gated(KT - 1)
    mult2(KT - 1)
    tail(KT - 1, 1)




OUT_UNITS = NT * KT


def out_unit(n):
    return (n // NT, n % NT) if n < OUT_UNITS // 2 else (KT // 2 + n % 4, (n - OUT_UNITS // 2) // 4)


def out_scalar(act, k, s):
    act.wait_ge(s.merge.up_ready, 3 * KT)
    act.dma_start(k.x[:, :, :].rearrange("p m t -> p (m t)"), k.x_dram).then_inc(s.x_loaded, 16)
    act.wait_ge(s.merge.m_ready, 3 * KT)
    for t in range(NT):
        act.activation(k.h_hi[:, :, tg(t)], k.m[:, :, tg(t)], ACT.Copy).then_inc(s.m_hi, 1)
    for c in range(KT // 2):
        act.wait_ge(s.unit_ready, 3 * c + 3)
        split_hi(act, k, Slab(SLAB_OUT, 4, 1, c), c)
    act.wait_ge(s.m_lo, NT)
    for c in (0, 1):
        split_hi(act, k, Slab(SLAB_FFN2, 6, 0, c), 4 + c)

    def splits():
        act.wait_ge(s.unit_ready, OUT_UNITS)
        for c in (2, 3):
            split_hi(act, k, Slab(SLAB_FFN2, 6, 0, c), c - 2)

    norm_behind_scalar(act, k, s.next_norm, splits)


def out_vector(dve, k, s):
    def add(n):
        c, t = out_unit(n)
        dve.wait_ge(s.unit_ready, n + 1)
        dve.tensor_tensor(k.x[:, c, tg(t)], k.x[:, c, tg(t)], k.bank[n % 3][:, 0:TG], ALU.add).then_inc(s.unit_used, 1)

    for t in range(NT):
        dve.wait_ge(s.m_hi, t + 1)
        dve.tensor_tensor(k.h_lo[:, :, tg(t)], k.m[:, :, tg(t)], k.h_hi[:, :, tg(t)].bitcast(F32), ALU.subtract)\
            .then_inc(s.m_lo, 1)
    dve.wait_ge(s.x_loaded, 16)
    for n in range(OUT_UNITS // 2):
        add(n)
        if n % NT == 2:
            split_lo(dve, k, Slab(SLAB_OUT, 4, 1, n // NT), n // NT)
    for c in (0, 1):
        split_lo(dve, k, Slab(SLAB_FFN2, 6, 0, c), 4 + c)
    for n in range(OUT_UNITS // 2, OUT_UNITS):
        add(n)
        if n >= OUT_UNITS - 4:
            first = 3 * (n - (OUT_UNITS - 4))
            for tile in range(first, first + 3):
                norm_apply(dve, k, s.next_norm, tile // KT, tile % KT)
    for tile in range(12, 2 * KT):
        norm_apply(dve, k, s.next_norm, tile // KT, tile % KT)
    for c in (2, 3):
        split_lo(dve, k, Slab(SLAB_FFN2, 6, 0, c), c - 2)
    for m in range(KT):
        norm_apply(dve, k, s.next_norm, 2, m)


def out_tensor(pe, k, s):
    for n in range(OUT_UNITS):
        c, t = out_unit(n)
        pe.wait_ge(k.slab_ready, SLAB_OUT + c + 1)
        if c == 0:
            pe.wait_ge(s.m_lo, t + 1)
        wait(pe, s.unit_used, n - 2)
        product(pe, k, k.bank[n % 3][:, 0:TG], c % 4, k.h_hi, k.h_lo, tg(t)).then_inc(s.unit_ready, 1)
        if n in (17, 21):
            norm_mean(pe, k, s.next_norm, (n - 17) // 4)



def params_scalar(act, k, s):
    act.wait_ge(s.arg, 5)
    for dst, n in ((2, 2), (4, 4), (5, 5)):
        act.activation(k.tmp[:, dst, :], k.tmp[:, n, :], ACT.Exp).then_inc(s.exp, 1)


def params_vector(dve, k, s):
    lb, oml, c8, neg_c8 = (k.par[:, n, :] for n in range(4))
    mx, x, z, w, e0, e1, q, s2 = (k.tmp[:, n, :] for n in range(8))
    l0, l1, lam = k.vec[:, LB0, :], k.vec[:, LB1, :], k.vec[:, LAM, :]
    done = [0]

    def then(ins):
        done[0] += 1
        ins.then_inc(s.arg, 1)
        dve.wait_ge(s.arg, done[0])

    dve.memset(k.eps[:, :], EPS).then_inc(s.eps, 1)
    dve.wait_ge(k.vec_loaded, 16)
    then(dve.tensor_tensor(mx, l0, l1, ALU.max))
    then(dve.tensor_tensor(e0, l0, mx, ALU.subtract))
    then(dve.tensor_tensor(e1, l1, mx, ALU.subtract))
    then(dve.tensor_scalar(x, lam, -1.0, None, ALU.mult))
    then(dve.tensor_tensor(z, x, lam, ALU.min))
    dve.wait_ge(s.exp, 3)
    then(dve.tensor_tensor(w, e0, e1, ALU.add))
    then(dve.reciprocal(w, w))
    then(dve.tensor_tensor(lb, e0, w, ALU.mult))
    then(dve.tensor_scalar(oml, lb, -1.0, 1.0, ALU.mult, ALU.add))
    then(dve.tensor_scalar(w, z, 2.0, None, ALU.add))
    then(dve.reciprocal(w, w))
    then(dve.tensor_tensor(z, z, w, ALU.mult))
    then(dve.tensor_tensor(s2, z, z, ALU.mult))
    then(dve.tensor_scalar(q, s2, 1.0 / 17, None, ALU.mult))
    for n in (15, 13, 11, 9, 7, 5, 3):
        then(dve.scalar_tensor_tensor(q, q, 1.0 / n, s2, ALU.add, ALU.mult))
    then(dve.scalar_tensor_tensor(q, q, 1.0, z, ALU.add, ALU.mult))
    then(dve.tensor_scalar(x, x, 0.0, 8.0, ALU.max, ALU.mult))
    then(dve.scalar_tensor_tensor(c8, q, 16.0, x, ALU.mult, ALU.add))
    dve.tensor_scalar(neg_c8, c8, -1.0, None, ALU.mult).then_inc(k.par_ready, 1)



def build(nc, x_t, w_slabs, lru_w, vec, state_hgrn, state_lru, state_conv, consts,
          y_out, hgrn_p, hgrn_s, lru_out, conv_p, conv_s):
    k = Names(w_slabs=w_slabs, state_hgrn=state_hgrn, hgrn_p=hgrn_p, hgrn_s=hgrn_s)
    k.x_dram = nc.dram_tensor("x_kept", (P, KT * T), F32, kind="Internal").ap()
    k.m_dram = nc.dram_tensor("m_kept", (KT, P, T), F32, kind="Internal").ap()
    x_t = x_t.rearrange("(m p) t -> p m t", p=P)
    y_out = y_out.rearrange("(m p) t -> p m t", p=P)

    class Region:
        def __init__(self, start, end):
            self.at, self.end = start, end

        def put(self, name, shape, dtype):
            size = {F32: 4, F32R: 4, BF16: 2, U8: 1}[dtype]
            for n in shape[1:]:
                size *= n
            t = nc.alloc_sbuf_tensor_at(name, list(shape), dtype, offset=self.at)
            self.at += (size + 31) // 32 * 32
            assert self.at <= self.end, (name, self.at, self.end)
            return t

    ACTS = KT * T * 4
    fixed = Region(1280, 8704)
    k.vec = fixed.put("vec", [P, NVEC, KT], F32)
    k.par = fixed.put("par", [P, 4, KT], F32)
    k.tmp = fixed.put("tmp", [P, 8, KT], F32)
    k.eps = fixed.put("eps", [P, 1], F32)
    k.consts = fixed.put("consts", [P, 4, P], F32)
    k.ident, k.ones_d, k.ones_h = (k.consts[:, n, :] for n in range(3))
    k.mask = fixed.put("mask", [P, P], U8)
    k.reset = fixed.put("reset", [P, SEQ], BF16)
    k.conv_s = fixed.put("conv_state", [P, KT, 3 * DEC], F32)
    k.conv_so = fixed.put("conv_state_new", [P, KT, 3 * DEC], F32)
    k.conv_po = fixed.put("conv_state_prompt", [P, KT, 3], F32)
    k.h0 = fixed.put("lru_state", [P, KT, DEC], F32)
    k.lru_out = fixed.put("lru_state_new", [P, KT, DEC + 1], F32)

    acts = Region(8704, 8704 + 2 * ACTS)
    k.h_hi = acts.put("h_hi", [P, KT, T], F32R)
    k.h_lo = acts.put("h_lo", [P, KT, T], F32R)
    k.y = Region(8704, 8704 + ACTS).put("y", [P, KT, T], F32)

    second = acts.end
    outs = Region(second, second + 2 * ACTS)
    k.o_hi = outs.put("o_hi", [P, KT, T], F32R)
    k.o_lo = outs.put("o_lo", [P, KT, T], F32R)
    ffn = Region(second, second + 2 * ACTS)
    k.x = ffn.put("x", [P, KT, T], F32)
    k.hid_hi = ffn.put("hid_hi", [P, 2, T], F32R)
    k.hid_lo = ffn.put("hid_lo", [P, 2, T], F32R)

    ring = Region(outs.end, outs.end + 4096 * 14)
    k.raw = [ring.put(f"raw{n}", [P, KT * P], F32) for n in range(2)]
    k.w_hi, k.w_lo = [], []
    for n in range(6):
        if n == 4:
            work = ring.at
        k.w_hi.append(ring.put(f"w_hi{n}", [P, KT * P], F32R))
        k.w_lo.append(ring.put(f"w_lo{n}", [P, KT * P], F32R))

    end = 229344
    r = Region(ring.at, end)
    k.gate = r.put("gate", [P, T], F32)
    k.hid = [r.put(f"hid{n}", [P, TG], F32) for n in range(2)]
    k.rstd = r.put("rstd", [P, T], F32)
    k.htmp = [r.put(f"htmp{n}", [P, TG], F32) for n in range(4)]
    k.square = [r.put(f"square{n}", [P, TG], F32) for n in range(4)]
    k.sumsq = [r.put(f"sumsq{n}", [P, TG], F32) for n in range(2)]

    r = Region(work, end)
    k.f = r.put("f", [P, T], F32)
    k.b = r.put("b", [P, SEQ], F32)
    k.q = r.put("q", [P, T], F32)
    k.v = r.put("v", [P, TILES + 1, P], F32)
    k.ke = r.put("ke", [P, T], F32)
    k.qe = r.put("qe", [P, T], F32)
    k.sg = r.put("sg", [P, T], F32)
    k.ss = r.put("ss", [P, DEC, P], F32)
    k.vm = r.put("vm", [P, 4, P], F32)
    k.el = r.put("el", [P, 24], F32)
    k.s = [r.put(f"s{n}", [P, P], F32) for n in range(4)]
    k.s_out = r.put("s_out", [P, P], F32)
    k.kt = [r.put(f"kt{n}", [P, P], F32) for n in range(2)]
    k.sc = [r.put(f"sc{n}", [P, P], F32) for n in range(2)]
    k.ue = [r.put(f"ue{n}", [P, 2, P], F32) for n in range(2)]
    k.sq = r.put("sq", [P, T], F32)

    r = Region(work, end)
    k.sgt_a = r.put("sgt_a", [P, T], F32)
    k.mt = [r.put(f"mt{n}", [P, T], F32) for n in range(2)]

    r = Region(work, end)
    k.rb = r.put("rb", [P, T], F32)
    k.tb = r.put("tb", [P, T], F32)
    k.ib = r.put("ib", [P, T], F32)
    k.xr = r.put("xr", [P, T + 3], F32)
    k.xc = r.put("xc", [P, T], F32)
    k.yb = [r.put(f"yb{n}", [P, T], F32) for n in range(2)]
    k.z = r.put("z", [P, T], F32)
    k.lru_w = r.put("lru_w", [P, 2, KT, P], F32)
    k.lw = [r.put(f"lw{n}", [P, 2, P], F32) for n in range(2)]

    r = Region(work, end)
    k.m = r.put("m", [P, KT, T], F32)
    k.sgt_b = r.put("sgt_b", [P, T], F32)
    k.mtb = r.put("mtb", [P, T], F32)

    with ExitStack() as ctx:
        k.bank = [ctx.enter_context(nc.psum_tensor(f"bank{n}", [P, 512], F32)) for n in range(8)]

        def sem(name):
            return ctx.enter_context(nc.semaphore(name))

        def stage(prefix, names, **fields):
            s = Names(**fields)
            for name in names.split():
                s[name] = sem(f"{prefix}_{name}")
            return s

        k.slab_loaded = [sem("slab_loaded0"), sem("slab_loaded1")]
        for name in ("slab_hi", "slab_ready", "x_spilled", "vec_loaded", "consts_loaded", "lru_w_loaded",
                     "states_loaded", "reset_ready", "par_ready", "stored"):
            k[name] = sem(name)
        x_loaded = [sem(f"x_loaded{t}") for t in range(NT)]

        NORM = "squared added mean_ready ln rstd_ready h_ready h_hi h_lo h_lo_pool"
        FFN = "gate_ready gate_used up_ready hidden hidden_hi hidden_lo down_ready down_used"
        par = stage("par", "arg exp eps")
        n1 = stage("n1", NORM, gain=G1, spill=False, final=False, bank=7)
        nm = stage("nm", NORM, gain=GMIX, spill=True, final=False, bank=3)
        f1 = stage("f1", FFN, first=SLAB_FFN1, next_slabs=4, shift=0, norm=n1, next_norm=nm)
        a = stage("a", "unit_ready unit_used kt_ready kt_used sc_ready sc_used u_ready u_used state o_ready "
                  "o_used ss_new ss_loaded ss_stored pstate_ready pstate_stored vm_ready squared mean_ready ln "
                  "rstd scaled gated out_hi out_lo f_ready logf cum key exp_minus exp_plus el_s el_p ke_s "
                  "ke_ready qe_s qe_ready vt_ready v_ready zeroed act_passed dve_passed", norm=nm)
        ma = stage("ma", "gate_ready gate_used up_ready up_used", first=SLAB_MA, spill=True,
                   stored=[sem("ma_stored0"), sem("ma_stored1")])
        ma.multiplied = ma.up_used
        b = stage("b", "unit_ready unit_used conv kept blocks_ready gates_ready gates_used decay mult2 mult "
                  "gated_in driven states ob_ready out_hi out_lo pad act_passed")
        mb = stage("mb", "gate_ready gate_used up_ready up_used m_ready", first=SLAB_MB, spill=False,
                   m_loaded=sem("m_loaded"))
        mb.multiplied = mb.up_used
        n2 = stage("n2", NORM, gain=G2, spill=False, final=False, bank=7)
        o = stage("o", "x_loaded m_hi m_lo unit_ready unit_used", merge=mb, next_norm=n2)
        n3 = stage("n3", NORM, gain=GFIN, spill=False, final=True, bank=3)
        f2 = stage("f2", FFN, first=SLAB_FFN2, next_slabs=0, shift=4, norm=n2, next_norm=n3)

        def out_done(eng, t, m):
            eng.wait_ge(o.unit_used, 1 + (NT * m + t if m < KT // 2 else OUT_UNITS // 2 + 4 * t + m - KT // 2))

        n1.x_ready = lambda eng, t, m: eng.wait_ge(x_loaded[t], 16)
        nm.x_ready = lambda eng, t, m: eng.wait_ge(f1.down_used, (PAIRS - 1) * 24 + 8 * t + m + 1)
        n2.x_ready = out_done
        f1.banks_read = lambda pe: None
        f2.banks_read = lambda pe: pe.wait_ge(o.unit_used, OUT_UNITS)
        n3.x_ready = lambda eng, t, m: eng.wait_ge(f2.down_used, (PAIRS - 1) * 24 + 8 * t + m + 1)

        def ma_banks(pe):
            pe.wait_ge(a.unit_used, UNITS * HEADS)

        def ma_branch(pe):
            pe.wait_ge(a.out_lo, HEADS)

        def b_banks(pe):
            pe.wait_ge(ma.gate_used, 3 * KT)
            pe.wait_ge(ma.up_used, 3 * KT)

        def b_memory(eng):
            for n in range(2):
                eng.wait_ge(ma.stored[n], 16 * KT // 2)
            eng.wait_ge(a.ss_stored, 16 * HEADS)
            eng.wait_ge(a.pstate_stored, 16 * HEADS)

        def mb_banks(pe):
            pe.wait_ge(b.unit_used, 6 * KT)
            pe.wait_ge(b.gates_used, 6 * KT)

        def mb_branch(pe):
            pe.wait_ge(b.out_lo, KT)

        ma.banks_free, ma.branch_done, ma.sgt = ma_banks, ma_branch, k.sgt_a
        b.banks_free, b.memory_free = b_banks, b_memory
        mb.banks_free, mb.branch_done, mb.sgt = mb_banks, mb_branch, k.sgt_b

        block = ctx.enter_context(nc.Block())

        @block.sync
        def _(sp):
            sp.dma_start(k.vec[:, :, :], vec).then_inc(k.vec_loaded, 16)
            sp.dma_start(k.consts[:, :, :], consts).then_inc(k.consts_loaded, 16)
            for n in range(2):
                load_slab(sp, k, Slab(0, 2, 0, n))
            sp.dma_start(k.h0[:, :, :], state_lru).then_inc(k.states_loaded, 16)
            sp.dma_start(k.conv_s[:, :, :], state_conv).then_inc(k.states_loaded, 16)
            with sp.Fori(1, FFN_SLABS // 2) as i:
                load_slab(sp, k, Slab(SLAB_FFN1, 2, i, 0))
                load_slab(sp, k, Slab(SLAB_FFN1, 2, i, 1))
            a_sync(sp, k, a)
            for c in range(4):
                load_slab(sp, k, Slab(SLAB_MA, 4, 0, c))
            a_states(sp, k, a, HEADS - 2, HEADS - 1)
            for c in range(4):
                load_slab(sp, k, Slab(SLAB_MA, 4, 1, c))
            a_states(sp, k, a, HEADS - 1, None)
            with sp.Fori(4, (SLAB_B - SLAB_MA) // 2) as i:
                load_slab(sp, k, Slab(SLAB_MA, 2, i, 0))
                load_slab(sp, k, Slab(SLAB_MA, 2, i, 1))
            for c in range(4):
                load_slab(sp, k, Slab(SLAB_B, 4, 0, c))
            b_memory(sp)
            sp.wait_ge(a.out_lo, HEADS)
            sp.dma_start(k.lru_w[:, :, :, :], lru_w).then_inc(k.lru_w_loaded, 16)
            with sp.Fori(2, (SLAB_OUT - SLAB_B) // 2) as i:
                load_slab(sp, k, Slab(SLAB_B, 2, i, 0))
                load_slab(sp, k, Slab(SLAB_B, 2, i, 1))
            sp.wait_ge(b.out_lo, KT)
            sp.dma_start(lru_out, k.lru_out[:, :, :]).then_inc(k.stored, 16)
            sp.dma_start(conv_p, k.conv_po[:, :, :]).then_inc(k.stored, 16)
            sp.dma_start(conv_s, k.conv_so[:, :, :]).then_inc(k.stored, 16)
            with sp.Fori(0, (SLABS - SLAB_OUT) // 2) as i:
                load_slab(sp, k, Slab(SLAB_OUT, 2, i, 0))
                load_slab(sp, k, Slab(SLAB_OUT, 2, i, 1))
            for t in range(NT):
                sp.wait_ge(n3.h_ready, (t + 1) * KT)
                sp.dma_start(y_out[:, :, tg(t)], k.y[:, :, tg(t)]).then_inc(k.stored, 16)
            sp.wait_ge(k.stored, 16 * (3 + NT))
            sp.wait_ge(a.ss_stored, 16 * HEADS)
            sp.wait_ge(a.pstate_stored, 16 * HEADS)

        @block.scalar
        def _(act):
            for t in range(NT):
                act.dma_start(k.x[:, :, tg(t)], x_t[:, :, tg(t)]).then_inc(x_loaded[t], 16)
            params_scalar(act, k, par)
            act.wait_ge(par.eps, 1)
            norm_first_scalar(act, k, n1)
            ffn_scalar(act, k, f1)
            a_scalar(act, k, a)
            merge_scalar(act, k, ma)
            b_scalar(act, k, b)
            act.wait_ge(b.out_lo, KT)
            for m in range(KT):
                act.dma_start(k.m[:, m, :], k.m_dram[m]).then_inc(mb.m_loaded, 16)
            merge_scalar(act, k, mb)
            out_scalar(act, k, o)
            ffn_scalar(act, k, f2)

        @block.vector
        def _(dve):
            params_vector(dve, k, par)
            norm_first_vector(dve, k, n1)
            ffn_vector(dve, k, f1)
            dve.wait_ge(k.reset_ready, 2)
            dve.wait_ge(k.consts_loaded, 16)
            dve.tensor_copy(k.mask[:, :], k.consts[:, 3, :]).then_inc(a.zeroed, 1)
            for n in range(2):
                dve.memset(k.sc[n][:, :], 0.0).then_inc(a.zeroed, 1)
            dve.wait_ge(a.zeroed, 3)
            a_vector(dve, k, a)
            merge_vector(dve, k, ma)
            dve.wait_ge(k.states_loaded, 32)
            b_vector(dve, k, b)
            merge_vector(dve, k, mb)
            out_vector(dve, k, o)
            ffn_vector(dve, k, f2)

        @block.gpsimd
        def _(pool):
            pool.memset(k.reset[:, :], 1.0).then_inc(k.reset_ready, 1)
            pool.wait_ge(k.reset_ready, 1)
            pool.memset(k.reset[:, 0:SEQ:CHUNK], 0.0).then_inc(k.reset_ready, 1)
            norm_gpsimd(pool, k, n1)
            norm_gpsimd(pool, k, nm)
            b_gpsimd(pool, k, b)
            norm_gpsimd(pool, k, n2)
            norm_gpsimd(pool, k, n3)

        @block.tensor
        def _(pe):
            pe.wait_ge(k.consts_loaded, 16)
            norm_mean(pe, k, n1, 0)
            norm_mean(pe, k, n1, 1)
            ffn_tensor(pe, k, f1)
            a_tensor(pe, k, a)
            merge_tensor(pe, k, ma)
            b_tensor(pe, k, b)
            merge_tensor(pe, k, mb)
            out_tensor(pe, k, o)
            ffn_tensor(pe, k, f2)
            norm_mean(pe, k, n3, 2)



def slabs_of_columns(w):
    n = w.shape[1] // P
    return w.reshape(KT, P, n, P).transpose(2, 1, 0, 3).reshape(n, P, KT * P)


def kernel(**inputs):
    import numpy as np
    import concourse.bacc as bacc
    from concourse.bass_utils import run_bass_kernel_spmd

    a = {name: np.asarray(value) for name, value in inputs.items()}

    def ffn_slabs(n):
        gate, up = (slabs_of_columns(a[f"ffn{n}_w_{w}"][0]) for w in ("gate", "up"))
        down = a[f"ffn{n}_w_down"][0].reshape(FT, P, D)
        order = []
        for i in range(PAIRS):
            for f in (2 * i, 2 * i + 1):
                order += [gate[f], up[f]]
            order += [down[2 * i], down[2 * i + 1]]
        return order

    w_in = slabs_of_columns(a["w_in"][0])
    q, f, v, g, xr, yr, ga, gb = (w_in[KT * n:KT * (n + 1)] for n in range(8))
    order = ffn_slabs(1)
    for j in range(HEADS):
        order += [f[j], q[j], v[j], g[j]]
    up = slabs_of_columns(a["w_a_up"][0])
    for j in range(KT):
        order += [ga[j], up[j]]
    for j in range(KT):
        order += [xr[j], yr[j]]
    up = slabs_of_columns(a["w_b_up"][0])
    for j in range(KT):
        order += [gb[j], up[j]]
    order += list(slabs_of_columns(a["w_out"][0]))
    order += ffn_slabs(2)

    vectors = [a["ffn1_norm"][0], a["mix_norm"][0], a["ffn2_norm"][0], a["final_norm"], a["hgrn_out_norm"][0],
               a["conv_b"][0], *a["conv_w"][0], a["lru_b_a"][0], a["lru_b_x"][0], a["lru_lambda"][0],
               a["hgrn_lower_bounds"][0], a["hgrn_lower_bounds"][1]]
    chunk_of = np.arange(P) // CHUNK
    causal = (chunk_of[:, None] == chunk_of[None, :]) & (np.arange(P)[:, None] <= np.arange(P)[None, :])
    arrays = {
        "x_t": np.ascontiguousarray(np.concatenate([a["x_prompt"][0], a["x_sample"][:, 0]]).T),
        "w_slabs": np.stack(order),
        "lru_w": np.ascontiguousarray(np.stack([a["lru_w_a"][0], a["lru_w_x"][0]]).transpose(2, 0, 1, 3)),
        "vec": np.ascontiguousarray(np.stack(vectors).reshape(NVEC, KT, P).transpose(2, 0, 1)),
        "state_hgrn": np.ascontiguousarray(a["state_hgrn"][0].transpose(1, 2, 0, 3)).reshape(HEADS, P, DEC * P),
        "state_lru": np.ascontiguousarray(a["state_lru"][0].reshape(DEC, KT, P).transpose(2, 1, 0)),
        "state_conv": np.ascontiguousarray(a["state_conv"][0].reshape(DEC, 3, KT, P).transpose(3, 2, 1, 0))
        .reshape(P, KT, 3 * DEC),
        "consts": np.stack([np.eye(P, dtype=np.float32), np.full((P, P), 1.0 / D, np.float32),
                            np.full((P, P), 1.0 / P, np.float32), causal.astype(np.float32)], axis=1),
    }
    outs = {"y_t": (D, T), "hgrn_p": (HEADS, P, P), "hgrn_s": (HEADS, P, DEC * P), "lru": (P, KT, DEC + 1),
            "conv_p": (P, KT, 3), "conv_s": (P, KT, 3 * DEC)}

    nc = bacc.Bacc("TRN2", target_bir_lowering=False, num_devices=1, dynamic_dma_scratch_size=1024)
    args = [nc.dram_tensor(n, v.shape, mybir.dt.from_np(v.dtype), kind="ExternalInput").ap()
            for n, v in arrays.items()]
    args += [nc.dram_tensor(n, shape, F32, kind="ExternalOutput").ap() for n, shape in outs.items()]
    build(nc, *args)
    r = run_bass_kernel_spmd(nc, [arrays], core_ids=[0]).results[0]

    y = r["y_t"].T
    lru = r["lru"].transpose(2, 1, 0).reshape(DEC + 1, D)
    return (
        np.ascontiguousarray(y[:SEQ])[None],
        np.ascontiguousarray(y[SEQ:])[:, None],
        r["hgrn_p"][None, None],
        lru[None, :1],
        np.ascontiguousarray(r["conv_p"].transpose(2, 1, 0)).reshape(1, 1, 3, D),
        np.ascontiguousarray(r["hgrn_s"].reshape(HEADS, P, DEC, P).transpose(2, 0, 1, 3))[None],
        lru[None, 1:],
        np.ascontiguousarray(r["conv_s"].reshape(P, KT, 3, DEC).transpose(3, 2, 1, 0)).reshape(1, DEC, 3, D),
    )
```

```python
from contextlib import ExitStack

import concourse.bass as bass
from concourse import mybir

ALU = mybir.AluOpType
ACT = mybir.ActivationFunctionType
F32 = mybir.dt.float32
F32R = mybir.dt.float32r
BF16 = mybir.dt.bfloat16
U8 = mybir.dt.uint8

P = 128
D = 1024
KT = D // P
SEQ = 1024
DEC = 8
T = SEQ + DEC
NT = 3
TG = T // NT
FT = 2816 // P
PAIRS = FT // 2
HEADS = 8
CHUNK = 64
TILES = SEQ // P
EPS = 1e-6

(G1, GMIX, G2, GFIN, GO, CB, CW0, CW1, CW2, CW3, BA, BX, LAM, LB0, LB1) = range(15)
NVEC = 15

FFN_SLABS = 3 * FT
SLAB_FFN1 = 0
SLAB_A = SLAB_FFN1 + FFN_SLABS
SLAB_MA = SLAB_A + 4 * HEADS
SLAB_B = SLAB_MA + 2 * KT
SLAB_MB = SLAB_B + 2 * KT
SLAB_OUT = SLAB_MB + 2 * KT
SLAB_FFN2 = SLAB_OUT + KT
SLABS = SLAB_FFN2 + FFN_SLABS


class Names(dict):

    def __getattr__(self, name):
        return self[name]

    def __setattr__(self, name, value):
        self[name] = value


def tg(t):
    return slice(t * TG, (t + 1) * TG)


def wait(eng, sem, value):
    if not (isinstance(value, int) and value <= 0):
        eng.wait_ge(sem, value)


def wait_apart(eng, sem, value, passed):
    eng.wait_ge(sem, value)
    eng.sem_inc(passed)


class Slab:

    def __init__(self, first, per, i, c):
        self.number = i * per + (first + c)
        self.pair = i * (per // 2) + (first + c) // 2
        self.buf = (first + c) % 2



def load_slab(sp, k, slab):
    wait(sp, k.slab_ready, slab.number - 1)
    src = k.w_slabs[bass.ds(slab.number, 1)].rearrange("a p c -> p (a c)")
    sp.dma_start(k.raw[slab.buf][:, :], src).then_inc(k.slab_loaded[slab.buf], 16)


def split_hi(act, k, slab, slot):
    act.wait_ge(k.slab_loaded[slab.buf], slab.pair * 16 + 16)
    act.activation(k.w_hi[slot][:, :], k.raw[slab.buf][:, :], ACT.Copy).then_inc(k.slab_hi, 1)


def split_lo(dve, k, slab, slot):
    dve.wait_ge(k.slab_hi, slab.number + 1)
    dve.tensor_tensor(k.w_lo[slot][:, :], k.raw[slab.buf][:, :], k.w_hi[slot][:, :].bitcast(F32),
                      ALU.subtract).then_inc(k.slab_ready, 1)


def weight(k, slot, b):
    cols = slice(b * P, (b + 1) * P)
    return k.w_hi[slot][:, cols], k.w_lo[slot][:, cols]


def three(pe, out, w, x, start, stop):
    (wh, wl), (xh, xl) = w, x
    pe.matmul(out, wh, xh, start=start, stop=False)
    pe.matmul(out, wh, xl, start=False, stop=False)
    return pe.matmul(out, wl, xh, start=False, stop=stop)


def product(pe, k, out, slot, hi, lo, cols, tiles=range(KT)):
    for m in tiles:
        last = three(pe, out, weight(k, slot, m), (hi[:, m, cols], lo[:, m, cols]), m == 0, m == KT - 1)
    return last



def norm_square(act, k, s, t, m):
    n = KT * t + m
    s.x_ready(act, t, m)
    if n >= 4:
        act.wait_ge(s.added, 7 * ((n - 4) // KT) + max((n - 4) % KT, 1))
    act.activation(k.square[n % 4][:, :], k.x[:, m, tg(t)], ACT.Square).then_inc(s.squared, 1)


def norm_rstd(act, k, s, t):
    act.wait_ge(s.mean_ready, t + 1)
    act.activation(k.rstd[:, tg(t)], k.bank[s.bank][:, 0:TG], ACT.Ln, bias=k.eps[:, 0:1]).then_inc(s.ln, 1)
    act.wait_ge(s.ln, t + 1)
    act.activation(k.rstd[:, tg(t)], k.rstd[:, tg(t)], ACT.Exp, scale=-0.5).then_inc(s.rstd_ready, 1)


def norm_hi(act, k, s, t, m):
    if not s.final:
        act.wait_ge(s.h_ready, t * KT + m + 1)
        act.activation(k.h_hi[:, m, tg(t)], k.htmp[m % 4][:, :], ACT.Copy).then_inc(s.h_hi, 1)


def norm_behind_scalar(act, k, s, early=False):
    for m in range(KT):
        norm_square(act, k, s, 0, m)
    for m in range(KT):
        norm_square(act, k, s, 1, m)
        if m == 3:
            norm_rstd(act, k, s, 0)
    norm_hi(act, k, s, 0, 0)
    for m in range(KT):
        if m + 1 < KT:
            norm_hi(act, k, s, 0, m + 1)
        if early and m == KT - 2:
            norm_rstd(act, k, s, 1)
        norm_square(act, k, s, 2, m)
    if s.spill:
        act.dma_start(k.x_dram, k.x[:, :, :].rearrange("p m t -> p (m t)")).then_inc(k.x_spilled, 16)
    if not early:
        norm_rstd(act, k, s, 1)
    for m in range(KT):
        norm_hi(act, k, s, 1, m)


def norm_last_scalar(act, k, s, between=lambda m: None):
    norm_rstd(act, k, s, 2)
    for m in range(KT):
        between(m)
        norm_hi(act, k, s, 2, m)


def norm_first_scalar(act, k, s):
    for m in range(KT):
        norm_square(act, k, s, 0, m)
    split_hi(act, k, Slab(0, 2, 0, 0), 0)
    norm_rstd(act, k, s, 0)
    for m in range(2):
        norm_square(act, k, s, 1, m)
    for m in range(KT):
        norm_hi(act, k, s, 0, m)
        if m < KT - 2:
            norm_square(act, k, s, 1, 2 + m)
    split_hi(act, k, Slab(0, 2, 0, 1), 1)
    for m in range(4):
        norm_square(act, k, s, 2, m)
    norm_rstd(act, k, s, 1)
    for m in range(KT):
        norm_hi(act, k, s, 1, m)
        if m < 4:
            norm_square(act, k, s, 2, 4 + m)
    norm_last_scalar(act, k, s)


def norm_low(eng, k, s, t, m):
    eng.wait_ge(s.h_hi, t * KT + m + 1)
    eng.tensor_tensor(k.h_lo[:, m, tg(t)], k.htmp[m % 4][:, :], k.h_hi[:, m, tg(t)].bitcast(F32),
                      ALU.subtract).then_inc(s.h_lo_pool if on_pool(s, t, m) else s.h_lo, 1)


def on_pool(s, t, m):
    return t >= s.pool_from and m % 2 == 1


def lows(s, t, m, pool):
    return sum(on_pool(s, n // KT, n % KT) == pool for n in range(KT * t + m + 1))


def norm_add(eng, k, s, t, m):
    eng.wait_ge(s.squared, KT * t + m + 1)
    if m > 1:
        eng.wait_ge(s.added, 7 * t + m - 1)
    before = k.square[0] if m == 1 else k.sumsq[t % 2]
    eng.tensor_tensor(k.sumsq[t % 2][:, :], before[:, :], k.square[m % 4][:, :], ALU.add).then_inc(s.added, 1)


def norm_gpsimd(pool, k, s, first=0):
    wait(pool, s.added, 7 * first)
    for t in range(first, NT):
        wait(pool, s.mean_ready, t - 1)
        for m in range(1, KT):
            norm_add(pool, k, s, t, m)
    if not s.final:
        for n in range(KT, NT * KT):
            if on_pool(s, n // KT, n % KT):
                norm_low(pool, k, s, n // KT, n % KT)


def norm_mean(pe, k, s, t):
    pe.wait_ge(s.added, 7 * (t + 1))
    wait(pe, s.ln, t)
    pe.matmul(k.bank[s.bank][:, 0:TG], k.ones_d[:, :], k.sumsq[t % 2][:, :], start=True, stop=True)\
        .then_inc(s.mean_ready, 1)


def norm_ready(pe, s, t):
    pe.wait_ge(s.h_lo, lows(s, t, KT - 1, False))
    if t >= s.pool_from:
        pe.wait_ge(s.h_lo_pool, lows(s, t, KT - 1, True))


def norm_apply(dve, k, s, t, m):
    if m == 0:
        dve.wait_ge(s.rstd_ready, t + 1)
    if s.final:
        dve.scalar_tensor_tensor(k.y[:, m, tg(t)], k.x[:, m, tg(t)], k.vec[:, s.gain, m:m + 1],
                                 k.rstd[:, tg(t)], ALU.mult, ALU.mult).then_inc(s.h_ready, 1)
        return
    n = KT * t + m
    if n >= 4:
        dve.wait_ge(s.h_hi, n - 3)
        former = divmod(n - 4, KT)
        if on_pool(s, *former):
            dve.wait_ge(s.h_lo_pool, lows(s, *former, True))
        else:
            dve.wait_ge(s.h_lo, lows(s, *former, False))
    dve.scalar_tensor_tensor(k.htmp[m % 4][:, :], k.x[:, m, tg(t)], k.vec[:, s.gain, m:m + 1],
                             k.rstd[:, tg(t)], ALU.mult, ALU.mult).then_inc(s.h_ready, 1)
    if m and not on_pool(s, t, m - 1):
        norm_low(dve, k, s, t, m - 1)
    if m == KT - 1 and not on_pool(s, t, m):
        norm_low(dve, k, s, t, m)


def norm_first_vector(dve, k, s, between):
    for m in range(1, KT):
        norm_add(dve, k, s, 0, m)
    for t in range(NT):
        if t < 2:
            split_lo(dve, k, Slab(0, 2, 0, t), t)
        between[t]()
        for m in range(KT):
            norm_apply(dve, k, s, t, m)


def norm_behind_vector(dve, k, s, add):
    norm_apply(dve, k, s, 0, 0)
    for m in range(KT):
        if m + 1 < KT:
            norm_apply(dve, k, s, 0, m + 1)
        add(m)
    for t in (1, 2):
        for m in range(KT):
            norm_apply(dve, k, s, t, m)



def ffn_slot(s, c):
    return (c + s.shift) % 6


def ffn_tensor(pe, k, s):
    def unit(i, f, t, which):
        u = i * 6 + (3 * f + t)
        slot = ffn_slot(s, 2 * f + (which == "up"))
        if which == "gate":
            wait(pe, s.gate_used, u - 1)
            bank, ready = k.bank[(3 * f + t) % 2], s.gate_ready
        else:
            wait(pe, s.hidden, u - 1)
            bank, ready = k.bank[2 + (3 * f + t) % 2], s.up_ready
        product(pe, k, bank[:, 0:TG], slot, k.h_hi, k.h_lo, tg(t)).then_inc(ready, 1)

    def group(i, first=False, last=False):
        for f in range(2):
            if first and f == 0:
                for t in range(NT):
                    norm_ready(pe, s.norm, t)
                    for c, which in enumerate(("gate", "up")):
                        if t == 0:
                            pe.wait_ge(k.slab_ready, s.first + c + 1)
                            if c:
                                s.banks_read(pe)
                        unit(i, f, t, which)
                        if t == 0 and c == s.norm.mean_behind:
                            norm_mean(pe, k, s.norm, 2)
                continue
            for c, which in enumerate(("gate", "up")):
                pe.wait_ge(k.slab_ready, Slab(s.first, 6, i, 2 * f + c).number + 1)
                for t in range(NT):
                    unit(i, f, t, which)
        for f in range(2):
            pe.wait_ge(k.slab_ready, Slab(s.first, 6, i, 4 + f).number + 1)
        for t in range(NT):
            pe.wait_ge(s.hidden_lo, i * 6 + (3 + t + 1))
            for m in range(KT):
                wait(pe, s.down_used, i * 24 + (8 * t + m - 3))
                for f in range(2):
                    done = three(pe, k.bank[4 + m % 4][:, 0:TG], weight(k, ffn_slot(s, 4 + f), m),
                                 (k.hid_hi[:, f, tg(t)], k.hid_lo[:, f, tg(t)]), f == 0, f == 1)
                done.then_inc(s.down_ready, 1)
                if last and t and m == 3:
                    norm_mean(pe, k, s.next_norm, t - 1)

    group(0, first=True)
    with pe.Fori(1, PAIRS - 1) as i:
        group(i)
    group(PAIRS - 1, last=True)


def ffn_scalar(act, k, s):
    def ahead(i, last, c):
        if not last:
            split_hi(act, k, Slab(s.first, 6, i, c + 6), ffn_slot(s, c))
        elif s.next_slabs > c:
            split_hi(act, k, Slab(s.first + FFN_SLABS, 0, 0, c), c)

    def silu(i, f, t):
        u = i * 6 + (3 * f + t)
        act.wait_ge(s.gate_ready, u + 1)
        wait(act, s.hidden, u - 2)
        act.activation(k.gate[:, tg(t)], k.bank[(3 * f + t) % 2][:, 0:TG], ACT.Silu).then_inc(s.gate_used, 1)

    def high(i, f, t):
        act.wait_ge(s.hidden, i * 6 + (3 * f + t + 1))
        act.activation(k.hid_hi[:, f, tg(t)], k.hid[(3 * f + t) % 2][:, :], ACT.Copy).then_inc(s.hidden_hi, 1)

    def group(i, first=False, last=False):
        for f in range(2):
            if first and f == 0:
                for t in range(NT):
                    silu(i, f, t)
                    high(i, f, t)
                    split_hi(act, k, Slab(s.first, 6, i, 2 + t), ffn_slot(s, 2 + t))
                continue
            if first:
                silu(i, f, 0)
                silu(i, f, 1)
                split_hi(act, k, Slab(s.first, 6, i, 5), ffn_slot(s, 5))
                silu(i, f, 2)
                for t in range(NT):
                    if t < 2:
                        ahead(i, last, t)
                    high(i, f, t)
                ahead(i, last, 2)
                ahead(i, last, 3)
                continue
            for t in range(NT):
                silu(i, f, t)
            ahead(i, last, 2 * f)
            for t in range(NT):
                high(i, f, t)
            ahead(i, last, 2 * f + 1)
        if last:
            norm_behind_scalar(act, k, s.next_norm, early=not s.next_norm.final)
            return
        act.wait_ge(s.down_ready, i * 24 + 24)
        ahead(i, last, 4)
        ahead(i, last, 5)

    group(0, first=True)
    with act.Fori(1, PAIRS - 1) as i:
        group(i)
    group(PAIRS - 1, last=True)


def ffn_vector(dve, k, s):
    def ahead(i, last, c):
        if not last:
            split_lo(dve, k, Slab(s.first, 6, i, c + 6), ffn_slot(s, c))
        elif s.next_slabs > c:
            split_lo(dve, k, Slab(s.first + FFN_SLABS, 0, 0, c), c)

    def hidden(i, f, t):
        u = i * 6 + (3 * f + t)
        dve.wait_ge(s.up_ready, u + 1)
        dve.wait_ge(s.gate_used, u + 1)
        wait(dve, s.hidden_hi, u - 1)
        dve.tensor_tensor(k.hid[(3 * f + t) % 2][:, :], k.gate[:, tg(t)], k.bank[2 + (3 * f + t) % 2][:, 0:TG],
                          ALU.mult).then_inc(s.hidden, 1)

    def low(i, f, t):
        dve.wait_ge(s.hidden_hi, i * 6 + (3 * f + t + 1))
        dve.tensor_tensor(k.hid_lo[:, f, tg(t)], k.hid[(3 * f + t) % 2][:, :], k.hid_hi[:, f, tg(t)].bitcast(F32),
                          ALU.subtract).then_inc(s.hidden_lo, 1)

    def group(i, first=False, last=False):
        for f in range(2):
            if first and f == 0:
                for t in range(NT):
                    hidden(i, f, t)
                    low(i, f, t)
                    split_lo(dve, k, Slab(s.first, 6, i, 2 + t), ffn_slot(s, 2 + t))
                continue
            if first:
                split_lo(dve, k, Slab(s.first, 6, i, 5), ffn_slot(s, 5))
                for t in range(NT):
                    if t < 2:
                        ahead(i, last, t)
                    hidden(i, f, t)
                    low(i, f, t)
                ahead(i, last, 2)
                continue
            ahead(i, last, 2 * f)
            for t in range(NT):
                hidden(i, f, t)
                low(i, f, t)
            if f == 0:
                ahead(i, last, 1)

        def add(t, m):
            dve.wait_ge(s.down_ready, i * 24 + (8 * t + m + 1))
            dve.scalar_tensor_tensor(k.x[:, m, tg(t)], k.bank[4 + m % 4][:, 0:TG], 0.5, k.x[:, m, tg(t)],
                                     ALU.mult, ALU.add).then_inc(s.down_used, 1)

        for t in range(2 if last else NT):
            for m in range(KT):
                add(t, m)
            if t == 0:
                ahead(i, last, 3)
        if last:
            norm_behind_vector(dve, k, s.next_norm, lambda m: add(2, m))
            return
        ahead(i, last, 4)
        ahead(i, last, 5)

    group(0, first=True)
    with dve.Fori(1, PAIRS - 1) as i:
        group(i)
    group(PAIRS - 1, last=True)



UNITS = 12
V_UNIT = 6
G_UNIT = 9


FIRST = [(c, t) for t in range(NT) for c in (0, 1, 3)] + [(2, t) for t in range(NT)]


def branch_a(engine, first, body):
    first()
    body(1, True, True)
    with engine.Fori(2, HEADS) as j:
        body(j, True, True)
    body(HEADS, False, True)


def mean_banks(proj):
    return (3, 4, 5) if proj else (6, 7, 0)


def a_tensor(pe, k, s):
    def keys(h, n):
        tok = slice(n * P, (n + 1) * P)
        wait(pe, s.kt_used, h * 9 + n)
        pe.transpose(k.bank[4][:, 0:P], k.ke[:, tok], k.ident[:, :]).then_inc(s.kt_ready, 1)
        wait(pe, s.sc_used, h * 8 + n)
        pe.matmul(k.bank[5][:, 0:P], k.ke[:, tok], k.qe[:, tok], start=True, stop=True).then_inc(s.sc_ready, 1)

    def updates(h, n):
        pe.wait_ge(s.kt_used, h * 9 + (n + 1))
        wait(pe, s.u_used, h * 16 + 2 * n)
        for c in range(2):
            rows = slice(c * CHUNK, (c + 1) * CHUNK)
            pe.matmul(k.bank[6 + c][:, 0:P], k.kt[n % 2][rows, :], k.v[rows, n, :], start=True, stop=True)\
                .then_inc(s.u_ready, 1)

    def output(h, n):
        pe.wait_ge(s.state, h * 17 + (2 * n + 2))
        pe.wait_ge(s.sc_used, h * 8 + (n + 1))
        wait(pe, s.o_used, h * 9 + n)
        o = k.bank[3]
        for c in range(2):
            cols = slice(n * P + c * CHUNK, n * P + (c + 1) * CHUNK)
            pe.matmul(o[:, c * CHUNK:(c + 1) * CHUNK], k.s[(2 * n + c) % 4][:, :], k.qe[:, cols],
                      start=c == 0, stop=False, skip_group_check=True)
        pe.matmul(o[:, 0:P], k.v[:, n, :], k.sc[n % 2][:, :], start=False, stop=True, skip_group_check=True)\
            .then_inc(s.o_ready, 1)

    def slot(h, n):
        if 2 <= n < 10:
            output(h, n - 2)
        if 1 <= n < 9:
            updates(h, n - 1)
        if n == 0:
            pe.wait_ge(s.ke_ready, h * 1 + 1)
            pe.wait_ge(s.qe_ready, h * 1 + 1)
            pe.wait_ge(s.v_ready, h * 3 + 3)
        if n < 8:
            keys(h, n)
        if n == 8:
            pe.wait_ge(s.kt_used, h * 9 + 8)
            pe.transpose(k.bank[4][0:DEC, 0:P], k.ke[:, SEQ:T], k.ident[:, :]).then_inc(s.kt_ready, 1)
        if n in (9, 10):
            q = n - 9
            pe.wait_ge(s.kt_used, h * 9 + 9)
            pe.wait_ge(s.vm_ready, h * 2 + (q + 1))
            pe.wait_ge(s.u_used, h * 16 + 16)
            pe.matmul(k.bank[6 + q][:, 0:4 * P], k.kt[0][0:DEC, :], k.vm[0:DEC, :, :], start=True, stop=True)\
                .then_inc(s.u_ready, 1)
        if n == 11:
            pe.wait_ge(s.ss_new, h * 8 + 8)
            pe.wait_ge(s.o_used, h * 9 + 8)
            for b in range(DEC):
                last = pe.matmul(k.bank[3][:, b:b + 1], k.ss[:, b, :], k.qe[:, SEQ + b:SEQ + b + 1],
                                 start=True, stop=True)
            last.then_inc(s.o_ready, 1)

    def means(h, banks):
        pe.wait_ge(s.squared, h * 1 + 1)
        pe.wait_ge(s.kt_used, h * 9 + 9)
        for t in range(NT):
            pe.matmul(k.bank[banks[t]][:, 0:TG], k.ones_h[:, :], k.sq[:, tg(t)], start=True, stop=True)\
                .then_inc(s.mean_ready, 1)

    def turn():
        for n in range(TILES + 1):
            rows = min(P, T - n * P)
            last = pe.transpose(k.bank[(6, 7, 4)[n // 4]][0:rows, (n % 4) * P:(n % 4 + 1) * P],
                                k.f[:, n * P:n * P + rows], k.ident[:, :])
            if n in (3, 7, 8):
                last.then_inc(s.vt_ready, 1)

    def iteration(j, proj, core):
        h = j - 1

        def free(c):
            wait(pe, s.unit_used, j * UNITS + (c - 2))
            return k.bank[c % 3]

        for half in range(12):
            u = half // 2
            if proj:
                c, t = u // 3, u % 3
                if half % 2 == 0:
                    if t == 0:
                        pe.wait_ge(k.slab_ready, Slab(SLAB_A, 4, j, c).number + 1)
                    bank = free(u)
                last = product(pe, k, bank[:, 0:TG], c, k.h_hi, k.h_lo, tg(t),
                               range(4 * (half % 2), 4 * (half % 2) + 4))
                if half % 2:
                    last.then_inc(s.unit_ready, 1)
            if not proj:
                merge_gate_tensor(pe, k, s.merge, 0, u // 3, u % 3, half % 2)
            if core:
                slot(h, half)
        if proj:
            pe.wait_ge(k.slab_ready, Slab(SLAB_A, 4, j, 2).number + 1)
        for c in range(3):
            if proj:
                bank = free(V_UNIT + c)
                product(pe, k, bank[:, 0:TG], 2, k.h_hi, k.h_lo, tg(c), range(0, 4))
            if core and c == 0:
                if not proj:
                    pe.wait_ge(s.merge.gate_used, 4)
                means(h, mean_banks(proj))
            if proj:
                product(pe, k, bank[:, 0:TG], 2, k.h_hi, k.h_lo, tg(c), range(4, 8)).then_inc(s.unit_ready, 1)
        if proj:
            pe.wait_ge(k.slab_ready, Slab(SLAB_A, 4, j, 3).number + 1)
            for t in range(NT):
                bank = free(G_UNIT + t)
                product(pe, k, bank[:, 0:TG], 3, k.h_hi, k.h_lo, tg(t)).then_inc(s.unit_ready, 1)
                if t == 0:
                    pe.wait_ge(s.unit_used, j * UNITS + (V_UNIT + 3))
                    pe.wait_ge(s.ln, h * 3 + 3)
                    turn()

    def first():
        for u, (c, t) in enumerate(FIRST):
            if t == 0:
                pe.wait_ge(k.slab_ready, SLAB_A + c + 1)
            if c == 0:
                norm_ready(pe, s.norm, t)
            wait(pe, s.unit_used, u - 2)
            product(pe, k, k.bank[u % 3][:, 0:TG], c, k.h_hi, k.h_lo, tg(t)).then_inc(s.unit_ready, 1)
            if u == 0:
                norm_mean(pe, k, s.norm, 2)
        pe.wait_ge(s.unit_used, UNITS)
        turn()

    branch_a(pe, first, iteration)


def a_scalar(act, k, s):
    def slot(h, n):
        if 1 <= n < 9:
            m = n - 1
            for c in range(2):
                act.wait_ge(s.u_ready, h * 18 + (2 * m + c + 1))
                if m >= 2:
                    act.wait_ge(s.state, h * 17 + (2 * m - 1))
                act.activation(k.ue[m % 2][:, c, :], k.bank[6 + c][:, 0:P], ACT.Identity,
                               scale=k.el[:, 2 * m + c:2 * m + c + 1]).then_inc(s.u_used, 1)
        if n < 9:
            rows = P if n < 8 else DEC
            act.wait_ge(s.kt_ready, h * 9 + (n + 1))
            if n >= 2:
                act.wait_ge(s.u_ready, h * 18 + 2 * (n - 1))
            act.activation(k.kt[n % 2][0:rows, :], k.bank[4][0:rows, 0:P], ACT.Copy).then_inc(s.kt_used, 1)

    def turned(j):
        for n, bank in enumerate((6, 7, 4)):
            act.wait_ge(s.vt_ready, j * 3 + (n + 1))
            rows, tiles = (P, 4) if n < 2 else (DEC, 1)
            act.activation(k.v[0:rows, 4 * n:4 * n + tiles, :].rearrange("p a d -> p (a d)"),
                           k.bank[bank][0:rows, 0:tiles * P], ACT.Copy).then_inc(s.v_ready, 1)

    def first():
        def read(u):
            c, t = FIRST[u]
            act.wait_ge(s.unit_ready, u + 1)
            to = (k.f, k.q, k.f, k.sg)[c]
            function = (ACT.Sigmoid, ACT.Silu, ACT.Copy, ACT.Silu)[c]
            act.activation(to[:, tg(t)], k.bank[u % 3][:, 0:TG], function).then_inc(s.unit_used, 1)
            if t == 2 and c < 2:
                split_hi(act, k, Slab(SLAB_A, 4, 0, 4 + c), c)

        def between(m):
            for u in {0: (0, 1), 4: (2,)}.get(m, ()):
                read(u)

        norm_last_scalar(act, k, s.norm, between)
        for u in range(3, 9):
            read(u)
        act.wait_ge(s.f_ready, 1)
        act.activation(k.b[:, :], k.f[:, 0:SEQ], ACT.Ln).then_inc(s.logf, 1)
        act.wait_ge(s.cum, 1)
        act.activation(k.ke[:, 0:SEQ], k.b[:, :], ACT.Exp, scale=-1.0).then_inc(s.exp_minus, 1)
        act.activation(k.b[:, :], k.b[:, :], ACT.Exp).then_inc(s.exp_plus, 1)
        act.wait_ge(s.ke_ready, 1)
        for u in range(9, 12):
            read(u)
        split_hi(act, k, Slab(SLAB_A, 4, 0, 6), 2)
        turned(0)
        split_hi(act, k, Slab(SLAB_A, 4, 0, 7), 3)

    def iteration(j, proj, core):
        h = j - 1
        for half in range(12):
            u = half // 2
            if proj and half % 2:
                act.wait_ge(s.unit_ready, j * UNITS + (u + 1))
                c, t = u // 3, u % 3
                if c == 0:
                    act.activation(k.f[:, tg(t)], k.bank[t][:, 0:TG], ACT.Sigmoid).then_inc(s.unit_used, 1)
                else:
                    wait(act, s.qe_ready, j * 1)
                    act.activation(k.q[:, tg(t)], k.bank[u % 3][:, 0:TG], ACT.Silu).then_inc(s.unit_used, 1)
                if t == 2:
                    split_hi(act, k, Slab(SLAB_A, 4, j, 4 + c), c)
            if not proj and half % 2:
                if half == 1:
                    act.wait_ge(s.qe_ready, HEADS)
                merge_sigmoid(act, k, s.merge, 0, u // 3, u % 3)
            if core:
                slot(h, half)
        if core:
            act.wait_ge(s.o_used, h * 9 + 9)
            wait(act, s.scaled, h * 1)
            act.activation(k.sq[:, :], k.qe[:, :], ACT.Square).then_inc(s.squared, 1)
        if proj:
            act.wait_ge(s.f_ready, j * 1 + 1)
            act.activation(k.b[:, :], k.f[:, 0:SEQ], ACT.Ln).then_inc(s.logf, 1)
        if core:
            for t in range(NT):
                act.wait_ge(s.mean_ready, h * 3 + (t + 1))
                act.activation(k.sq[:, tg(t)], k.bank[mean_banks(proj)[t]][:, 0:TG], ACT.Ln,
                               bias=k.eps[:, 0:1]).then_inc(s.ln, 1)
        if proj:
            act.wait_ge(s.cum, j * 1 + 1)
            act.activation(k.ke[:, 0:SEQ], k.b[:, :], ACT.Exp, scale=-1.0).then_inc(s.exp_minus, 1)
            act.activation(k.b[:, :], k.b[:, :], ACT.Exp).then_inc(s.exp_plus, 1)
        if core:
            act.wait_ge(s.ln, h * 3 + 3)
            act.activation(k.sq[:, :], k.sq[:, :], ACT.Exp, scale=-0.5).then_inc(s.rstd, 1)
        if proj:
            act.wait_ge(s.ke_ready, j * 1 + 1)
        for c in range(3):
            if proj:
                act.wait_ge(s.unit_ready, j * UNITS + (V_UNIT + c + 1))
                act.activation(k.f[:, tg(c)], k.bank[c][:, 0:TG], ACT.Copy).then_inc(s.unit_used, 1)
            if core and c == 1:
                if isinstance(h, int) and h == 0:
                    act.wait_ge(k.x_spilled, 16)
                wait_apart(act, s.gated, h * 1 + 1, s.act_passed)
                act.activation(k.o_hi[:, bass.ds(h, 1), :].rearrange("p a t -> p (a t)"), k.qe[:, :],
                               ACT.Copy).then_inc(s.out_hi, 1)
        if proj:
            split_hi(act, k, Slab(SLAB_A, 4, j, 6), 2)
            for t in range(NT):
                act.wait_ge(s.unit_ready, j * UNITS + (G_UNIT + t + 1))
                wait(act, s.gated, j * 1)
                act.activation(k.sg[:, tg(t)], k.bank[t][:, 0:TG], ACT.Silu).then_inc(s.unit_used, 1)
                if t == 0:
                    turned(j)
            split_hi(act, k, Slab(SLAB_A, 4, j, 7), 3)

    branch_a(act, first, iteration)


def a_vector(dve, k, s):
    def slot(h, n):
        if n == 0:
            dve.memset(k.s[0][:, :], 0.0).then_inc(s.state, 1)
        if 2 <= n < 10:
            m = n - 2
            dve.wait_ge(s.o_ready, h * 9 + (m + 1))
            dve.tensor_copy(k.qe[:, m * P:(m + 1) * P], k.bank[3][:, 0:P]).then_inc(s.o_used, 1)
        if 1 <= n < 9:
            for c in (2 * (n - 1), 2 * (n - 1) + 1):
                dve.wait_ge(s.u_used, h * 16 + (c + 1))
                dve.wait_ge(s.state, h * 17 + (c + 1))
                dve.scalar_tensor_tensor(k.s[(c + 1) % 4][:, :], k.s[c % 4][:, :], k.el[:, c:c + 1],
                                         k.ue[(n - 1) % 2][:, c % 2, :], ALU.mult, ALU.add).then_inc(s.state, 1)
        if n < 8:
            wait_apart(dve, s.sc_ready, h * 8 + (n + 1), s.dve_passed)
            dve.copy_predicated(k.sc[n % 2][:, :], k.mask[:, :], k.bank[5][:, 0:P]).then_inc(s.sc_used, 1)
        if n in (8, 9):
            q = n - 8
            if q:
                dve.wait_ge(s.u_ready, h * 18 + 17)
            dve.tensor_tensor(k.vm[0:DEC, :, :], k.v[0:DEC, 8:9, :].to_broadcast((DEC, 4, P)),
                              k.ident[0:DEC, 4 * q:4 * q + 4].unsqueeze(2).to_broadcast((DEC, 4, P)),
                              ALU.mult).then_inc(s.vm_ready, 1)
        if n in (9, 10):
            q = n - 9
            dve.wait_ge(s.u_ready, h * 18 + (17 + q))
            dve.wait_ge(s.ss_loaded, h * 16 + 16)
            for b in range(4 * q, 4 * q + 4):
                dve.scalar_tensor_tensor(k.ss[:, b, :], k.ss[:, b, :], k.el[:, 16 + b:17 + b],
                                         k.bank[6 + q][:, (b % 4) * P:(b % 4 + 1) * P],
                                         ALU.mult, ALU.add).then_inc(s.ss_new, 1)
        if n == 11:
            dve.wait_ge(s.o_ready, h * 9 + 9)
            dve.tensor_copy(k.qe[:, SEQ:T], k.bank[3][:, 0:DEC]).then_inc(s.o_used, 1)
            wait(dve, s.pstate_stored, h * 16)
            dve.wait_ge(s.state, h * 17 + 17)
            dve.tensor_copy(k.s_out[:, :], k.s[0][:, :]).then_inc(s.pstate_ready, 1)

    def iteration(j, proj, core):
        h = j - 1
        for half in range(12):
            if core:
                slot(h, half)
            if not proj and half == 5:
                split_lo(dve, k, Slab(SLAB_MA, 4, 0, 4), 0)
            if proj and half == 5:
                split_lo(dve, k, Slab(SLAB_A, 4, j, 4), 0)
                dve.wait_ge(s.unit_used, j * UNITS + (3 if core else 7))
                dve.tensor_scalar(k.f[:, :], k.f[:, :], k.par[:, 1, bass.ds(j, 1)], k.par[:, 0, bass.ds(j, 1)],
                                  ALU.mult, ALU.add).then_inc(s.f_ready, 1)
        if not proj:
            split_lo(dve, k, Slab(SLAB_MA, 4, 0, 5), 1)
        if proj:
            split_lo(dve, k, Slab(SLAB_A, 4, j, 5), 1)
            dve.wait_ge(s.f_ready, j * 1 + 1)
            dve.tensor_copy(k.el[:, 16:24], k.f[:, SEQ:T]).then_inc(s.el_s, 1)
            dve.wait_ge(s.logf, j * 1 + 1)
            dve.tensor_tensor_scan(k.b[:, :], k.reset[:, :], k.b[:, :], 0.0, ALU.mult, ALU.add).then_inc(s.cum, 1)
            dve.wait_ge(s.el_s, j * 1 + 1)
            dve.tensor_scalar(k.f[:, :], k.f[:, :], -1.0, 1.0, ALU.mult, ALU.add).then_inc(s.key, 1)
            dve.wait_ge(s.key, j * 1 + 1)
            dve.tensor_copy(k.ke[:, SEQ:T], k.f[:, SEQ:T]).then_inc(s.ke_s, 1)
            dve.wait_ge(s.exp_minus, j * 1 + 1)
            dve.tensor_tensor(k.ke[:, 0:SEQ], k.ke[:, 0:SEQ], k.f[:, 0:SEQ], ALU.mult).then_inc(s.ke_ready, 1)
            dve.wait_ge(s.exp_plus, j * 1 + 1)
            dve.tensor_copy(k.el[:, 0:16], k.b[:, CHUNK - 1:SEQ:CHUNK]).then_inc(s.el_p, 1)
        if core:
            o = k.qe[:, :]
            dve.wait_ge(s.rstd, h * 1 + 1)
            dve.scalar_tensor_tensor(o, o, k.vec[:, GO, bass.ds(h, 1)], k.sq[:, :], ALU.mult, ALU.mult)\
                .then_inc(s.scaled, 1)
            dve.wait_ge(s.scaled, h * 1 + 1)
            dve.tensor_tensor(o, o, k.sg[:, :], ALU.mult).then_inc(s.gated, 1)
            dve.wait_ge(s.out_hi, h * 1 + 1)
            one = bass.ds(h, 1)
            dve.tensor_tensor(k.o_lo[:, one, :].rearrange("p a t -> p (a t)"), o,
                              k.o_hi[:, one, :].rearrange("p a t -> p (a t)").bitcast(F32),
                              ALU.subtract).then_inc(s.out_lo, 1)
        if proj:
            wait(dve, s.out_lo, j * 1)
            dve.wait_ge(s.unit_used, j * UNITS + (6 if core else 8))
            dve.tensor_copy(k.qe[:, SEQ:T], k.q[:, SEQ:T]).then_inc(s.qe_s, 1)
            dve.wait_ge(s.el_p, j * 1 + 1)
            dve.wait_ge(s.qe_s, j * 1 + 1)
            dve.tensor_tensor(k.qe[:, 0:SEQ], k.q[:, 0:SEQ], k.b[:, :], ALU.mult).then_inc(s.qe_ready, 1)
            split_lo(dve, k, Slab(SLAB_A, 4, j, 6), 2)
            split_lo(dve, k, Slab(SLAB_A, 4, j, 7), 3)

    branch_a(dve, lambda: iteration(0, True, False), iteration)


def a_sync(sp, k, s):
    def slabs(j):
        for c in range(4):
            load_slab(sp, k, Slab(SLAB_A, 4, j, c))

    slabs(0)
    slabs(1)
    a_states(sp, k, s, None, 0)
    slabs(2)
    with sp.Fori(3, HEADS) as j:
        a_states(sp, k, s, j - 3, j - 2)
        slabs(j)
    a_states(sp, k, s, HEADS - 3, HEADS - 2)


def a_states(sp, k, s, store, load):
    if store is not None:
        sp.wait_ge(s.ss_new, store * 8 + 8)
        sp.wait_ge(s.o_ready, store * 9 + 9)
        sp.dma_start(k.hgrn_s[bass.ds(store, 1)].rearrange("a p c -> p (a c)"),
                     k.ss[:, :, :].rearrange("p b d -> p (b d)")).then_inc(s.ss_stored, 16)
        sp.wait_ge(s.pstate_ready, store * 1 + 1)
        sp.dma_start(k.hgrn_p[bass.ds(store, 1)].rearrange("a p c -> p (a c)"), k.s_out[:, :])\
            .then_inc(s.pstate_stored, 16)
        sp.wait_ge(s.ss_stored, store * 16 + 16)
    if load is not None:
        sp.dma_start(k.ss[:, :, :].rearrange("p b d -> p (b d)"),
                     k.state_hgrn[bass.ds(load, 1)].rearrange("a p c -> p (a c)")).then_inc(s.ss_loaded, 16)



PAIRS_M = KT // 2


def merge_gate_tensor(pe, k, s, i, p, t, half):
    if half == 0:
        if t == 0:
            pe.wait_ge(k.slab_ready, Slab(s.first, 4, i, p).number + 1)
        if isinstance(i, int) and i == 0 and p == 0:
            s.bank_free(pe, t)
        else:
            pe.wait_ge(s.gate_used, i * 6 + (3 * p + t - 2))
    last = product(pe, k, k.bank[t][:, 0:TG], p, k.h_hi, k.h_lo, tg(t), range(4 * half, 4 * half + 4))
    if half:
        last.then_inc(s.gate_ready, 1)


def merge_sigmoid(act, k, s, i, p, t):
    u = i * 6 + (3 * p + t)
    act.wait_ge(s.gate_ready, u + 1)
    wait(act, s.up_used, u - 5)
    act.activation(s.sgt[:, p, tg(t)], k.bank[t][:, 0:TG], ACT.Sigmoid).then_inc(s.gate_used, 1)
    if t == 2:
        split_hi(act, k, Slab(s.first, 4, i, 4 + p), p)


def merge_tensor(pe, k, s):
    def pair(i, gates=True):
        if gates:
            for u in range(6):
                for half in range(2):
                    merge_gate_tensor(pe, k, s, i, u // 3, u % 3, half)
        for p in range(2):
            pe.wait_ge(k.slab_ready, Slab(s.first, 4, i, 2 + p).number + 1)
            apart = isinstance(i, int) and i == 0 and p == 0
            if apart:
                s.branch_done(pe, KT - 1)
            for t in range(NT):
                if not apart:
                    pe.wait_ge(s.up_used, i * 6 + (3 * p + t - 2))
                last = product(pe, k, k.bank[3 + t][:, 0:TG], 2 + p, k.o_hi, k.o_lo, tg(t),
                               range(KT - 1) if apart else range(KT))
                if not apart:
                    last.then_inc(s.up_ready, 1)
            if apart:
                s.branch_done(pe, KT)
                for t in range(NT):
                    product(pe, k, k.bank[3 + t][:, 0:TG], 2 + p, k.o_hi, k.o_lo, tg(t),
                            range(KT - 1, KT)).then_inc(s.up_ready, 1)

    pair(0, gates=False)
    with pe.Fori(1, PAIRS_M) as i:
        pair(i)


def merge_scalar(act, k, s):
    def pair(i, gates=True, last=False):
        if gates:
            for u in range(6):
                merge_sigmoid(act, k, s, i, u // 3, u % 3)
        for p in range(2):
            if last:
                for m in range(3 * p, 3 * p + 3):
                    m_high(act, k, s.out, m)
            if last and p:
                m_high(act, k, s.out, KT - 2)
                for t in range(NT):
                    m_high(act, k, s.out, KT - 1, t)
            act.wait_ge(s.up_ready, i * 6 + 3 * (p + 1))
            if last and p:
                for n in range(2):
                    act.dma_start(k.x[:, 4 * n:4 * n + 4, :].rearrange("p m t -> p (m t)"),
                                  k.x_dram[:, 4 * n * T:4 * (n + 1) * T]).then_inc(s.out.x_loaded[n], 16)
            split_hi(act, k, Slab(s.first, 4, i, 6 + p), 2 + p)
            if s.spill:
                act.wait_ge(s.up_used, i * 6 + 3 * (p + 1))
                act.dma_start(k.m_dram[bass.ds(i * 2 + p, 1)].rearrange("a p t -> p (a t)"), k.mt[p][:, :])\
                    .then_inc(s.stored[p], 16)

    pair(0, gates=False)
    with act.Fori(1, PAIRS_M - 1) as i:
        pair(i)
    pair(PAIRS_M - 1, last=not s.spill)


def merge_vector(dve, k, s):
    def pair(i, gates=True, last=False):
        if gates:
            for p in range(2):
                split_lo(dve, k, Slab(s.first, 4, i, 4 + p), p)
        for p in range(2):
            if last:
                for m in range(3 * p, 3 * p + 3):
                    m_low(dve, k, s.out, m)
            if last and p:
                m_low(dve, k, s.out, KT - 2)
            if s.spill:
                wait(dve, s.stored[p], i * 16)
            if not s.spill and not gates:
                dve.wait_ge(s.m_loaded[p], 16)
            for t in range(NT):
                u = i * 6 + (3 * p + t)
                dve.wait_ge(s.up_ready, u + 1)
                dve.wait_ge(s.gate_used, u + 1)
                to = k.mt[p] if s.spill else k.mtb
                dve.tensor_tensor(to[:, tg(t)], s.sgt[:, p, tg(t)], k.bank[3 + t][:, 0:TG], ALU.mult)\
                    .then_inc(s.up_used, 1)
                if not s.spill:
                    dve.wait_ge(s.up_used, u + 1)
                    at = (slice(None), bass.ds(i * 2 + p, 1), tg(t))
                    m = k.m[at].rearrange("p a t -> p (a t)")
                    dve.tensor_tensor(m, m, k.mtb[:, tg(t)], ALU.add).then_inc(s.m_ready, 1)
                if last and p:
                    m_low(dve, k, s.out, KT - 1, t)
            split_lo(dve, k, Slab(s.first, 4, i, 6 + p), 2 + p)

    pair(0, gates=False)
    if not s.spill:
        for tile in range(2, KT):
            dve.wait_ge(s.m_loaded[tile], 16)
    with dve.Fori(1, PAIRS_M - 1) as i:
        pair(i)
    pair(PAIRS_M - 1, last=not s.spill)



def m_part(m, t):
    return (slice(None), m, slice(None) if t is None else tg(t)), m + (t or 0) + 1


def m_high(act, k, s, m, t=None):
    at, _ = m_part(m, t)
    act.wait_ge(s.merge.gate_ready, 3 * KT)
    act.wait_ge(s.merge.m_ready, 3 * m + (3 if t is None else t + 1))
    act.activation(k.h_hi[at], k.m[at], ACT.Copy).then_inc(s.m_hi, 1)


def m_low(dve, k, s, m, t=None):
    at, count = m_part(m, t)
    dve.wait_ge(s.m_hi, count)
    dve.tensor_tensor(k.h_lo[at], k.m[at], k.h_hi[at].bitcast(F32), ALU.subtract).then_inc(s.m_lo, 1)




def branch_b(engine, body):
    body(0, 0, 0, False)
    body(1, 1, 0, True)
    with engine.Fori(1, KT // 2) as i:
        body(i * 2, 0, i, True)
        body(i * 2 + 1, 1, i, True)


def b_tensor(pe, k, s):
    def gates(j, p, t):
        if t == 0:
            pe.wait_ge(s.conv, j * 8 + 8)
            pe.wait_ge(s.blocks_ready, j * 1 + 1)
        wait(pe, s.gates_used, j * 6 + (2 if t == 2 else 0))
        for c in range(2):
            pe.matmul(k.bank[3 + 2 * c + t % 2][:, 0:TG], k.lw[p][:, c, :], k.xc[:, tg(t)],
                      start=True, stop=True).then_inc(s.gates_ready, 1)

    def block(j, p, i, before):
        for c in range(2):
            pe.wait_ge(k.slab_ready, Slab(SLAB_B, 4, i, 2 * p + c).number + 1)
            for t in range(NT):
                wait(pe, s.unit_used, j * 6 + (3 * c + t - 2))
                product(pe, k, k.bank[t][:, 0:TG], 2 * p + c, k.h_hi, k.h_lo, tg(t)).then_inc(s.unit_ready, 1)
                if before and c == 0:
                    gates(j - 1, 1 - p, t)

    s.banks_free(pe)
    branch_b(pe, block)
    for t in range(NT):
        for half in range(2):
            merge_gate_tensor(pe, k, s.merge, 0, 0, t, half)
        gates(KT - 1, 1, t)
    for t in range(NT):
        for half in range(2):
            merge_gate_tensor(pe, k, s.merge, 0, 1, t, half)
    pe.wait_ge(s.gates_used, 6 * KT)


def b_gpsimd(pool, k, s):
    def block(j, p):
        wait(pool, s.gates_ready, j * 6 - 6)
        pool.tensor_copy(k.lw[p][:, :, :], k.lru_w[:, :, bass.ds(j, 1), :].rearrange("p a b d -> p (a b) d"))\
            .then_inc(s.blocks_ready, 1)

    pool.wait_ge(k.lru_w_loaded, 16)
    block(0, 0)
    block(1, 1)
    with pool.Fori(1, KT // 2) as i:
        block(i * 2, 0)
        block(i * 2 + 1, 1)


def b_scalar(act, k, s):
    def gates(j, t):
        for c, (dst, bias) in enumerate(((k.rb, BA), (k.ib, BX))):
            wait_apart(act, s.gates_ready, j * 6 + (2 * t + c + 1), s.act_passed)
            act.activation(dst[:, tg(t)], k.bank[3 + 2 * c + t % 2][:, 0:TG], ACT.Sigmoid,
                           bias=k.vec[:, bias, bass.ds(j, 1)]).then_inc(s.gates_used, 1)

    def decay(j):
        wait_apart(act, s.gates_used, j * 6 + 6, s.act_passed)
        act.activation(k.tb[:, :], k.rb[:, :], ACT.Tanh, scale=k.par[:, 2, bass.ds(j, 1)]).then_inc(s.decay, 1)
        act.activation(k.rb[:, :], k.rb[:, :], ACT.Exp, scale=k.par[:, 3, bass.ds(j, 1)]).then_inc(s.decay, 1)
        act.wait_ge(s.decay, j * 3 + 2)
        wait(act, s.out_lo, j * 1)
        act.activation(k.z[:, :], k.rb[:, :], ACT.Square).then_inc(s.decay, 1)

    def root(j):
        act.wait_ge(s.mult2, j * 1 + 1)
        act.activation(k.tb[:, :], k.tb[:, :], ACT.Sqrt).then_inc(s.mult, 1)

    def high(j):
        wait_apart(act, s.ob_ready, j * 1 + 1, s.act_passed)
        act.activation(k.o_hi[:, bass.ds(j, 1), :].rearrange("p a t -> p (a t)"), k.z[:, :], ACT.Copy)\
            .then_inc(s.out_hi, 1)

    def block(j, p, i, before):
        for t in range(NT):
            act.wait_ge(s.unit_ready, j * 6 + (t + 1))
            wait(act, s.conv, j * 8)
            act.activation(k.xr[:, 3 + t * TG:3 + (t + 1) * TG], k.bank[t][:, 0:TG], ACT.Copy).then_inc(s.unit_used, 1)
            if before:
                gates(j - 1, t)
        split_hi(act, k, Slab(SLAB_B, 4, i, 4 + 2 * p), 2 * p)
        if before:
            decay(j - 1)
        for t in range(NT):
            act.wait_ge(s.unit_ready, j * 6 + (3 + t + 1))
            act.activation(k.yb[p][:, tg(t)], k.bank[t][:, 0:TG], ACT.Gelu_apprx_tanh).then_inc(s.unit_used, 1)
        split_hi(act, k, Slab(SLAB_B, 4, i, 5 + 2 * p), 2 * p + 1)
        if before:
            root(j - 1)
            high(j - 1)

    s.memory_free(act)
    act.wait_ge(k.par_ready, 1)
    branch_b(act, block)
    act.wait_ge(s.blocks_ready, KT)
    for t in range(NT):
        merge_sigmoid(act, k, s.merge, 0, 0, t)
        gates(KT - 1, t)
    decay(KT - 1)
    root(KT - 1)
    for t in range(NT):
        merge_sigmoid(act, k, s.merge, 0, 1, t)
    high(KT - 1)


def b_vector(dve, k, s):
    def gated(j):
        dve.wait_ge(s.gates_used, j * 6 + 6)
        dve.tensor_tensor(k.ib[:, :], k.ib[:, :], k.xc[:, :], ALU.mult).then_inc(s.gated_in, 1)

    def mult2(j):
        dve.wait_ge(s.decay, j * 3 + 3)
        dve.scalar_tensor_tensor(k.tb[:, :], k.z[:, :], 1.0, k.tb[:, :], ALU.add, ALU.mult).then_inc(s.mult2, 1)

    def tail(j, p):
        one = bass.ds(j, 1)
        dve.wait_ge(s.mult, j * 1 + 1)
        dve.wait_ge(s.gated_in, j * 1 + 1)
        dve.tensor_tensor(k.ib[:, :], k.ib[:, :], k.tb[:, :], ALU.mult).then_inc(s.driven, 1)
        dve.wait_ge(s.driven, j * 1 + 1)
        dve.tensor_tensor_scan(k.tb[:, 0:SEQ], k.rb[:, 0:SEQ], k.ib[:, 0:SEQ], 0.0, ALU.mult, ALU.add)\
            .then_inc(s.states, 1)
        dve.tensor_tensor(k.tb[:, SEQ:T], k.rb[:, SEQ:T], k.h0[:, one, :].rearrange("p a b -> p (a b)"), ALU.mult)\
            .then_inc(s.states, 1)
        dve.wait_ge(s.states, j * 5 + 2)
        dve.tensor_tensor(k.tb[:, SEQ:T], k.tb[:, SEQ:T], k.ib[:, SEQ:T], ALU.add).then_inc(s.states, 1)
        dve.wait_ge(s.states, j * 5 + 3)
        dve.tensor_copy(k.lru_out[:, one, 0:1].rearrange("p a b -> p (a b)"), k.tb[:, SEQ - 1:SEQ]).then_inc(s.states, 1)
        dve.tensor_copy(k.lru_out[:, one, 1:9].rearrange("p a b -> p (a b)"), k.tb[:, SEQ:T]).then_inc(s.states, 1)
        dve.tensor_tensor(k.z[:, :], k.tb[:, :], k.yb[p][:, :], ALU.mult).then_inc(s.ob_ready, 1)
        dve.wait_ge(s.out_hi, j * 1 + 1)
        dve.tensor_tensor(k.o_lo[:, one, :].rearrange("p a t -> p (a t)"), k.z[:, :],
                          k.o_hi[:, one, :].rearrange("p a t -> p (a t)").bitcast(F32), ALU.subtract)\
            .then_inc(s.out_lo, 1)

    def block(j, p, i, before):
        one = bass.ds(j, 1)
        w = [k.vec[:, CW0 + n, one] for n in range(4)]

        def old(n):
            return k.conv_s[:, one, n * DEC:(n + 1) * DEC].rearrange("p a b -> p (a b)")

        split_lo(dve, k, Slab(SLAB_B, 4, i, 4 + 2 * p), 2 * p)
        if before:
            gated(j - 1)
        dve.wait_ge(s.unit_used, j * 6 + 3)
        wait(dve, s.gated_in, j * 1)
        dve.tensor_scalar(k.xc[:, 0:SEQ], k.xr[:, 0:SEQ], w[0], k.vec[:, CB, one], ALU.mult, ALU.add)\
            .then_inc(s.conv, 1)
        dve.tensor_scalar(k.xc[:, SEQ:T], old(0), w[0], k.vec[:, CB, one], ALU.mult, ALU.add).then_inc(s.conv, 1)
        for n in range(1, 4):
            dve.wait_ge(s.conv, j * 8 + 2 * n)
            dve.scalar_tensor_tensor(k.xc[:, 0:SEQ], k.xr[:, n:n + SEQ], w[n], k.xc[:, 0:SEQ], ALU.mult, ALU.add)\
                .then_inc(s.conv, 1)
            dve.scalar_tensor_tensor(k.xc[:, SEQ:T], old(n) if n < 3 else k.xr[:, SEQ + 3:T + 3], w[n],
                                     k.xc[:, SEQ:T], ALU.mult, ALU.add).then_inc(s.conv, 1)
            if n == 2:
                dve.tensor_copy(k.conv_po[:, one, :].rearrange("p a b -> p (a b)"), k.xr[:, SEQ:SEQ + 3])\
                    .then_inc(s.kept, 1)
                dve.tensor_copy(k.conv_so[:, one, 0:2 * DEC].rearrange("p a b -> p (a b)"),
                                k.conv_s[:, one, DEC:3 * DEC].rearrange("p a b -> p (a b)")).then_inc(s.kept, 1)
                dve.tensor_copy(k.conv_so[:, one, 2 * DEC:3 * DEC].rearrange("p a b -> p (a b)"),
                                k.xr[:, SEQ + 3:T + 3]).then_inc(s.kept, 1)
        if before:
            mult2(j - 1)
        split_lo(dve, k, Slab(SLAB_B, 4, i, 5 + 2 * p), 2 * p + 1)
        if before:
            tail(j - 1, 1 - p)

    s.memory_free(dve)
    dve.memset(k.xr[:, 0:3], 0.0).then_inc(s.pad, 1)
    dve.wait_ge(s.pad, 1)
    branch_b(dve, block)
    split_lo(dve, k, Slab(SLAB_MB, 4, 0, 4), 0)
    gated(KT - 1)
    mult2(KT - 1)
    tail(KT - 1, 1)
    split_lo(dve, k, Slab(SLAB_MB, 4, 0, 5), 1)




OUT_UNITS = NT * KT
M_PARTS = KT - 1 + NT


def out_unit(n):
    return (n // NT, n % NT) if n < OUT_UNITS // 2 else (KT // 2 + n % 4, (n - OUT_UNITS // 2) // 4)


def out_scalar(act, k, s):
    for c in range(KT // 2):
        act.wait_ge(s.unit_ready, 3 * c + 3)
        split_hi(act, k, Slab(SLAB_OUT, 4, 1, c), c)
    act.wait_ge(s.m_lo, M_PARTS)
    for c in (0, 1):
        split_hi(act, k, Slab(SLAB_FFN2, 6, 0, c), 4 + c)

    norm_behind_scalar(act, k, s.next_norm, early=True)
    norm_last_scalar(act, k, s.next_norm)


def out_vector(dve, k, s):
    def add(n):
        c, t = out_unit(n)
        dve.wait_ge(s.unit_ready, n + 1)
        dve.tensor_tensor(k.x[:, c, tg(t)], k.x[:, c, tg(t)], k.bank[n % 3][:, 0:TG], ALU.add).then_inc(s.unit_used, 1)

    dve.wait_ge(s.x_loaded[0], 16)
    for n in range(OUT_UNITS // 2):
        add(n)
        if n % NT == 2:
            split_lo(dve, k, Slab(SLAB_OUT, 4, 1, n // NT), n // NT)
    for c in (0, 1):
        split_lo(dve, k, Slab(SLAB_FFN2, 6, 0, c), 4 + c)
    dve.wait_ge(s.x_loaded[1], 16)
    for n in range(OUT_UNITS // 2, OUT_UNITS):
        add(n)
        for tile in {19: range(0, 3), 20: range(3, 6), 21: range(6, 8), 22: range(8, 9), 23: range(9, 24)}.get(n, ()):
            norm_apply(dve, k, s.next_norm, tile // KT, tile % KT)


def out_tensor(pe, k, s):
    for n in range(OUT_UNITS):
        c, t = out_unit(n)
        pe.wait_ge(k.slab_ready, SLAB_OUT + c + 1)
        if c == 0:
            pe.wait_ge(s.m_lo, KT + t)
        wait(pe, s.unit_used, n - 2)
        product(pe, k, k.bank[n % 3][:, 0:TG], c % 4, k.h_hi, k.h_lo, tg(t)).then_inc(s.unit_ready, 1)
        if n in (17, 21):
            norm_mean(pe, k, s.next_norm, (n - 17) // 4)



def params_scalar(act, k, s):
    act.wait_ge(s.arg, 5)
    for dst, n in ((2, 2), (4, 4), (5, 5)):
        act.activation(k.tmp[:, dst, :], k.tmp[:, n, :], ACT.Exp).then_inc(s.exp, 1)


def params_vector(dve, k, s, part):
    lb, oml, c8, neg_c8 = (k.par[:, n, :] for n in range(4))
    mx, x, z, w, e0, e1, q, s2 = (k.tmp[:, n, :] for n in range(8))
    l0, l1, lam = k.vec[:, LB0, :], k.vec[:, LB1, :], k.vec[:, LAM, :]

    def then(ins):
        s.steps += 1
        ins.then_inc(s.arg, 1)
        dve.wait_ge(s.arg, s.steps)

    if part == 0:
        dve.memset(k.eps[:, :], EPS).then_inc(s.eps, 1)
        dve.wait_ge(k.vec_loaded, 16)
        then(dve.tensor_tensor(mx, l0, l1, ALU.max))
        then(dve.tensor_tensor(e0, l0, mx, ALU.subtract))
        then(dve.tensor_tensor(e1, l1, mx, ALU.subtract))
        then(dve.tensor_scalar(x, lam, -1.0, None, ALU.mult))
        then(dve.tensor_tensor(z, x, lam, ALU.min))
    if part == 1:
        dve.wait_ge(s.exp, 3)
        then(dve.tensor_tensor(w, e0, e1, ALU.add))
        then(dve.reciprocal(w, w))
        then(dve.tensor_tensor(lb, e0, w, ALU.mult))
        then(dve.tensor_scalar(oml, lb, -1.0, 1.0, ALU.mult, ALU.add))
        then(dve.tensor_scalar(w, z, 2.0, None, ALU.add))
        then(dve.reciprocal(w, w))
        then(dve.tensor_tensor(z, z, w, ALU.mult))
        then(dve.tensor_tensor(s2, z, z, ALU.mult))
        then(dve.tensor_scalar(q, s2, 1.0 / 17, None, ALU.mult))
    if part == 2:
        for n in (15, 13, 11, 9, 7, 5, 3):
            then(dve.scalar_tensor_tensor(q, q, 1.0 / n, s2, ALU.add, ALU.mult))
        then(dve.scalar_tensor_tensor(q, q, 1.0, z, ALU.add, ALU.mult))
        then(dve.tensor_scalar(x, x, 0.0, 8.0, ALU.max, ALU.mult))
        then(dve.scalar_tensor_tensor(c8, q, 16.0, x, ALU.mult, ALU.add))
        dve.tensor_scalar(neg_c8, c8, -1.0, None, ALU.mult).then_inc(k.par_ready, 1)



def build(nc, x_t, w_slabs, lru_w, vec, state_hgrn, state_lru, state_conv, consts,
          y_out, hgrn_p, hgrn_s, lru_out, conv_p, conv_s):
    k = Names(w_slabs=w_slabs, state_hgrn=state_hgrn, hgrn_p=hgrn_p, hgrn_s=hgrn_s)
    k.x_dram = nc.dram_tensor("x_kept", (P, KT * T), F32, kind="Internal").ap()
    k.m_dram = nc.dram_tensor("m_kept", (KT, P, T), F32, kind="Internal").ap()
    x_t = x_t.rearrange("(m p) t -> p m t", p=P)
    y_out = y_out.rearrange("(m p) t -> p m t", p=P)

    class Region:
        def __init__(self, start, end):
            self.at, self.end = start, end

        def put(self, name, shape, dtype):
            size = {F32: 4, F32R: 4, BF16: 2, U8: 1}[dtype]
            for n in shape[1:]:
                size *= n
            t = nc.alloc_sbuf_tensor_at(name, list(shape), dtype, offset=self.at)
            self.at += (size + 31) // 32 * 32
            assert self.at <= self.end, (name, self.at, self.end)
            return t

    ACTS = KT * T * 4
    fixed = Region(1280, 8704)
    k.vec = fixed.put("vec", [P, NVEC, KT], F32)
    k.par = fixed.put("par", [P, 4, KT], F32)
    k.tmp = fixed.put("tmp", [P, 8, KT], F32)
    k.eps = fixed.put("eps", [P, 1], F32)
    k.consts = fixed.put("consts", [P, 4, P], F32)
    k.ident, k.ones_d, k.ones_h = (k.consts[:, n, :] for n in range(3))
    k.mask = fixed.put("mask", [P, P], U8)
    k.reset = fixed.put("reset", [P, SEQ], BF16)
    k.conv_s = fixed.put("conv_state", [P, KT, 3 * DEC], F32)
    k.conv_so = fixed.put("conv_state_new", [P, KT, 3 * DEC], F32)
    k.conv_po = fixed.put("conv_state_prompt", [P, KT, 3], F32)
    k.h0 = fixed.put("lru_state", [P, KT, DEC], F32)
    k.lru_out = fixed.put("lru_state_new", [P, KT, DEC + 1], F32)

    acts = Region(8704, 8704 + 2 * ACTS)
    k.h_hi = acts.put("h_hi", [P, KT, T], F32R)
    k.h_lo = acts.put("h_lo", [P, KT, T], F32R)
    k.y = Region(8704, 8704 + ACTS).put("y", [P, KT, T], F32)

    second = acts.end
    outs = Region(second, second + 2 * ACTS)
    k.o_hi = outs.put("o_hi", [P, KT, T], F32R)
    k.o_lo = outs.put("o_lo", [P, KT, T], F32R)
    ffn = Region(second, second + 2 * ACTS)
    k.x = ffn.put("x", [P, KT, T], F32)
    k.hid_hi = ffn.put("hid_hi", [P, 2, T], F32R)
    k.hid_lo = ffn.put("hid_lo", [P, 2, T], F32R)

    ring = Region(outs.end, outs.end + 4096 * 14)
    k.raw = [ring.put(f"raw{n}", [P, KT * P], F32) for n in range(2)]
    k.w_hi, k.w_lo = [], []
    for n in range(6):
        if n == 4:
            work = ring.at
        k.w_hi.append(ring.put(f"w_hi{n}", [P, KT * P], F32R))
        k.w_lo.append(ring.put(f"w_lo{n}", [P, KT * P], F32R))

    end = 229344
    r = Region(ring.at, end)
    k.gate = r.put("gate", [P, T], F32)
    k.hid = [r.put(f"hid{n}", [P, TG], F32) for n in range(2)]
    k.rstd = r.put("rstd", [P, T], F32)
    k.htmp = [r.put(f"htmp{n}", [P, TG], F32) for n in range(4)]
    k.square = [r.put(f"square{n}", [P, TG], F32) for n in range(4)]
    k.sumsq = [r.put(f"sumsq{n}", [P, TG], F32) for n in range(2)]

    r = Region(work, end)
    k.f = r.put("f", [P, T], F32)
    k.b = r.put("b", [P, SEQ], F32)
    k.q = r.put("q", [P, T], F32)
    k.sg = r.put("sg", [P, T], F32)
    k.v = r.put("v", [P, TILES + 1, P], F32)
    k.ke = r.put("ke", [P, T], F32)
    k.qe = r.put("qe", [P, T], F32)
    k.ss = r.put("ss", [P, DEC, P], F32)
    k.vm = r.put("vm", [P, 4, P], F32)
    k.el = r.put("el", [P, 24], F32)
    k.s = [r.put(f"s{n}", [P, P], F32) for n in range(4)]
    k.s_out = r.put("s_out", [P, P], F32)
    k.kt = [r.put(f"kt{n}", [P, P], F32) for n in range(2)]
    k.sc = [r.put(f"sc{n}", [P, P], F32) for n in range(2)]
    k.ue = [r.put(f"ue{n}", [P, 2, P], F32) for n in range(2)]
    k.sq = r.put("sq", [P, T], F32)

    r = Region(work, end)
    k.sgt_a = r.put("sgt_a", [P, 2, T], F32)
    k.mt = [r.put(f"mt{n}", [P, T], F32) for n in range(2)]

    r = Region(work, end)
    k.rb = r.put("rb", [P, T], F32)
    k.tb = r.put("tb", [P, T], F32)
    k.ib = r.put("ib", [P, T], F32)
    k.xr = r.put("xr", [P, T + 3], F32)
    k.xc = r.put("xc", [P, T], F32)
    k.yb = [r.put(f"yb{n}", [P, T], F32) for n in range(2)]
    k.z = r.put("z", [P, T], F32)
    k.lw = [r.put(f"lw{n}", [P, 2, P], F32) for n in range(2)]

    tail = end - 2 * T * 4
    assert r.at <= tail
    k.lru_w = Region(end - 2 * KT * P * 4, end).put("lru_w", [P, 2, KT, P], F32)

    r = Region(work, tail)
    k.m = r.put("m", [P, KT, T], F32)
    k.mtb = r.put("mtb", [P, T], F32)
    k.sgt_b = Region(tail, end).put("sgt_b", [P, 2, T], F32)

    with ExitStack() as ctx:
        k.bank = [ctx.enter_context(nc.psum_tensor(f"bank{n}", [P, 512], F32)) for n in range(8)]

        def sem(name):
            return ctx.enter_context(nc.semaphore(name))

        def stage(prefix, names, **fields):
            s = Names(**fields)
            for name in names.split():
                s[name] = sem(f"{prefix}_{name}")
            return s

        k.slab_loaded = [sem("slab_loaded0"), sem("slab_loaded1")]
        for name in ("slab_hi", "slab_ready", "x_spilled", "vec_loaded", "consts_loaded", "lru_w_loaded",
                     "states_loaded", "reset_ready", "par_ready", "stored"):
            k[name] = sem(name)
        x_loaded = [sem(f"x_loaded{n}") for n in range(NT + 1)]

        NORM = "squared added mean_ready ln rstd_ready h_ready h_hi h_lo h_lo_pool"
        FFN = "gate_ready gate_used up_ready hidden hidden_hi hidden_lo down_ready down_used"
        par = stage("par", "arg exp eps", steps=0)
        n1 = stage("n1", NORM, gain=G1, spill=False, final=False, bank=7, pool_from=2, mean_behind=1)
        nm = stage("nm", NORM, gain=GMIX, spill=True, final=False, bank=3, pool_from=1)
        f1 = stage("f1", FFN, first=SLAB_FFN1, next_slabs=4, shift=0, norm=n1, next_norm=nm)
        a = stage("a", "unit_ready unit_used kt_ready kt_used sc_ready sc_used u_ready u_used state o_ready "
                  "o_used ss_new ss_loaded ss_stored pstate_ready pstate_stored vm_ready squared mean_ready ln "
                  "rstd scaled gated out_hi out_lo f_ready logf cum key exp_minus exp_plus el_s el_p ke_s "
                  "ke_ready qe_s qe_ready vt_ready v_ready zeroed act_passed dve_passed", norm=nm)
        ma = stage("ma", "gate_ready gate_used up_ready up_used", first=SLAB_MA, spill=True,
                   stored=[sem("ma_stored0"), sem("ma_stored1")])
        b = stage("b", "unit_ready unit_used conv kept blocks_ready gates_ready gates_used decay mult2 mult "
                  "gated_in driven states ob_ready out_hi out_lo pad act_passed")
        mb = stage("mb", "gate_ready gate_used up_ready up_used m_ready", first=SLAB_MB, spill=False,
                   m_loaded=[sem(f"m_loaded{tile}") for tile in range(KT)])
        n2 = stage("n2", NORM, gain=G2, spill=False, final=False, bank=7, pool_from=1, mean_behind=0)
        o = stage("o", "m_hi m_lo unit_ready unit_used", merge=mb, next_norm=n2,
                  x_loaded=[sem("o_x_loaded0"), sem("o_x_loaded1")])
        a.merge, b.merge, mb.out = ma, mb, o
        n3 = stage("n3", NORM, gain=GFIN, spill=False, final=True, bank=3)
        f2 = stage("f2", FFN, first=SLAB_FFN2, next_slabs=0, shift=4, norm=n2, next_norm=n3)

        def out_done(eng, t, m):
            eng.wait_ge(o.unit_used, 1 + (NT * m + t if m < KT // 2 else OUT_UNITS // 2 + 4 * t + m - KT // 2))

        n1.x_ready = lambda eng, t, m: eng.wait_ge(x_loaded[t + 1 if t else m // 4], 16)
        nm.x_ready = lambda eng, t, m: eng.wait_ge(f1.down_used, (PAIRS - 1) * 24 + 8 * t + m + 1)
        n2.x_ready = out_done
        f1.banks_read = lambda pe: None
        f2.banks_read = lambda pe: pe.wait_ge(o.unit_used, OUT_UNITS)
        n3.x_ready = lambda eng, t, m: eng.wait_ge(f2.down_used, (PAIRS - 1) * 24 + 8 * t + m + 1)

        def ma_banks(pe, t):
            pe.wait_ge(a.unit_used, UNITS * HEADS - 2 + t)

        def ma_branch(pe, tiles):
            pe.wait_ge(a.out_lo, tiles)

        def b_banks(pe):
            pe.wait_ge(ma.gate_used, 3 * KT)
            pe.wait_ge(ma.up_used, 3 * KT)

        def b_memory(eng):
            for n in range(2):
                eng.wait_ge(ma.stored[n], 16 * KT // 2)
            eng.wait_ge(a.ss_stored, 16 * HEADS)
            eng.wait_ge(a.pstate_stored, 16 * HEADS)

        def mb_banks(pe, t):
            pe.wait_ge(b.unit_used, 6 * KT - 2 + t)

        def mb_branch(pe, tiles):
            pe.wait_ge(b.out_lo, tiles)

        ma.bank_free, ma.branch_done, ma.sgt = ma_banks, ma_branch, k.sgt_a
        b.banks_free, b.memory_free = b_banks, b_memory
        mb.bank_free, mb.branch_done, mb.sgt = mb_banks, mb_branch, k.sgt_b

        block = ctx.enter_context(nc.Block())

        @block.sync
        def _(sp):
            sp.dma_start(k.vec[:, :, :], vec).then_inc(k.vec_loaded, 16)
            for t in range(NT):
                if t == 0:
                    for n in range(2):
                        m = slice(4 * n, 4 * n + 4)
                        sp.dma_start(k.x[:, m, tg(t)], x_t[:, m, tg(t)]).then_inc(x_loaded[n], 16)
                    sp.dma_start(k.consts[:, :, :], consts).then_inc(k.consts_loaded, 16)
                else:
                    sp.dma_start(k.x[:, :, tg(t)], x_t[:, :, tg(t)]).then_inc(x_loaded[t + 1], 16)
                if t < 2:
                    load_slab(sp, k, Slab(0, 2, 0, t))
            sp.dma_start(k.h0[:, :, :], state_lru).then_inc(k.states_loaded, 16)
            sp.dma_start(k.conv_s[:, :, :], state_conv).then_inc(k.states_loaded, 16)
            with sp.Fori(1, FFN_SLABS // 2) as i:
                load_slab(sp, k, Slab(SLAB_FFN1, 2, i, 0))
                load_slab(sp, k, Slab(SLAB_FFN1, 2, i, 1))
            a_sync(sp, k, a)
            for c in range(4):
                load_slab(sp, k, Slab(SLAB_MA, 4, 0, c))
            a_states(sp, k, a, HEADS - 2, HEADS - 1)
            for c in range(4):
                load_slab(sp, k, Slab(SLAB_MA, 4, 1, c))
            a_states(sp, k, a, HEADS - 1, None)
            with sp.Fori(4, (SLAB_B - SLAB_MA) // 2) as i:
                load_slab(sp, k, Slab(SLAB_MA, 2, i, 0))
                load_slab(sp, k, Slab(SLAB_MA, 2, i, 1))
            for c in range(4):
                load_slab(sp, k, Slab(SLAB_B, 4, 0, c))
            b_memory(sp)
            sp.wait_ge(a.out_lo, HEADS)
            sp.dma_start(k.lru_w[:, :, :, :], lru_w).then_inc(k.lru_w_loaded, 16)
            with sp.Fori(2, (SLAB_OUT - SLAB_B) // 2) as i:
                load_slab(sp, k, Slab(SLAB_B, 2, i, 0))
                load_slab(sp, k, Slab(SLAB_B, 2, i, 1))
            sp.wait_ge(b.out_lo, KT)
            sp.dma_start(lru_out, k.lru_out[:, :, :]).then_inc(k.stored, 16)
            sp.dma_start(conv_p, k.conv_po[:, :, :]).then_inc(k.stored, 16)
            sp.dma_start(conv_s, k.conv_so[:, :, :]).then_inc(k.stored, 16)
            with sp.Fori(0, (SLABS - SLAB_OUT) // 2) as i:
                load_slab(sp, k, Slab(SLAB_OUT, 2, i, 0))
                load_slab(sp, k, Slab(SLAB_OUT, 2, i, 1))
            for t in range(NT):
                for m in (0, 4):
                    sp.wait_ge(n3.h_ready, t * KT + m + 4)
                    sp.dma_start(y_out[:, m:m + 4, tg(t)], k.y[:, m:m + 4, tg(t)]).then_inc(k.stored, 16)
            sp.wait_ge(k.stored, 16 * (3 + 2 * NT))
            sp.wait_ge(a.ss_stored, 16 * HEADS)
            sp.wait_ge(a.pstate_stored, 16 * HEADS)

        @block.scalar
        def _(act):
            params_scalar(act, k, par)
            act.wait_ge(par.eps, 1)
            norm_first_scalar(act, k, n1)
            ffn_scalar(act, k, f1)
            a_scalar(act, k, a)
            merge_scalar(act, k, ma)
            b_scalar(act, k, b)
            act.wait_ge(b.out_lo, KT)
            for m in range(KT):
                act.dma_start(k.m[:, m, :], k.m_dram[m]).then_inc(mb.m_loaded[m], 16)
            merge_scalar(act, k, mb)
            out_scalar(act, k, o)
            ffn_scalar(act, k, f2)
            norm_last_scalar(act, k, n3)

        @block.vector
        def _(dve):
            params_vector(dve, k, par, 0)
            norm_first_vector(dve, k, n1, (lambda: None, lambda: params_vector(dve, k, par, 1),
                                           lambda: params_vector(dve, k, par, 2)))
            ffn_vector(dve, k, f1)
            dve.wait_ge(k.reset_ready, 2)
            dve.wait_ge(k.consts_loaded, 16)
            dve.tensor_copy(k.mask[:, :], k.consts[:, 3, :]).then_inc(a.zeroed, 1)
            for n in range(2):
                dve.memset(k.sc[n][:, :], 0.0).then_inc(a.zeroed, 1)
            dve.wait_ge(a.zeroed, 3)
            a_vector(dve, k, a)
            merge_vector(dve, k, ma)
            dve.wait_ge(k.states_loaded, 32)
            b_vector(dve, k, b)
            merge_vector(dve, k, mb)
            out_vector(dve, k, o)
            ffn_vector(dve, k, f2)

        @block.gpsimd
        def _(pool):
            pool.memset(k.reset[:, :], 1.0).then_inc(k.reset_ready, 1)
            pool.wait_ge(k.reset_ready, 1)
            pool.memset(k.reset[:, 0:SEQ:CHUNK], 0.0).then_inc(k.reset_ready, 1)
            norm_gpsimd(pool, k, n1, first=1)
            norm_gpsimd(pool, k, nm)
            b_gpsimd(pool, k, b)
            norm_gpsimd(pool, k, n2)
            norm_gpsimd(pool, k, n3)

        @block.tensor
        def _(pe):
            pe.wait_ge(k.consts_loaded, 16)
            norm_mean(pe, k, n1, 0)
            norm_mean(pe, k, n1, 1)
            ffn_tensor(pe, k, f1)
            a_tensor(pe, k, a)
            merge_tensor(pe, k, ma)
            b_tensor(pe, k, b)
            merge_tensor(pe, k, mb)
            out_tensor(pe, k, o)
            ffn_tensor(pe, k, f2)
            norm_mean(pe, k, n3, 2)



def slabs_of_columns(w):
    n = w.shape[1] // P
    return w.reshape(KT, P, n, P).transpose(2, 1, 0, 3).reshape(n, P, KT * P)


def kernel(**inputs):
    import numpy as np
    import concourse.bacc as bacc
    from concourse.bass_utils import run_bass_kernel_spmd

    a = {name: np.asarray(value) for name, value in inputs.items()}

    def ffn_slabs(n):
        gate, up = (slabs_of_columns(a[f"ffn{n}_w_{w}"][0]) for w in ("gate", "up"))
        down = a[f"ffn{n}_w_down"][0].reshape(FT, P, D)
        order = []
        for i in range(PAIRS):
            for f in (2 * i, 2 * i + 1):
                order += [gate[f], up[f]]
            order += [down[2 * i], down[2 * i + 1]]
        return order

    w_in = slabs_of_columns(a["w_in"][0])
    q, f, v, g, xr, yr, ga, gb = (w_in[KT * n:KT * (n + 1)] for n in range(8))
    order = ffn_slabs(1)
    for j in range(HEADS):
        order += [f[j], q[j], v[j], g[j]]
    up = slabs_of_columns(a["w_a_up"][0])
    for j in range(0, KT, 2):
        order += [ga[j], ga[j + 1], up[j], up[j + 1]]
    for j in range(KT):
        order += [xr[j], yr[j]]
    up = slabs_of_columns(a["w_b_up"][0])
    for j in range(0, KT, 2):
        order += [gb[j], gb[j + 1], up[j], up[j + 1]]
    order += list(slabs_of_columns(a["w_out"][0]))
    order += ffn_slabs(2)

    vectors = [a["ffn1_norm"][0], a["mix_norm"][0], a["ffn2_norm"][0], a["final_norm"], a["hgrn_out_norm"][0],
               a["conv_b"][0], *a["conv_w"][0], a["lru_b_a"][0], a["lru_b_x"][0], a["lru_lambda"][0],
               a["hgrn_lower_bounds"][0], a["hgrn_lower_bounds"][1]]
    chunk_of = np.arange(P) // CHUNK
    causal = (chunk_of[:, None] == chunk_of[None, :]) & (np.arange(P)[:, None] <= np.arange(P)[None, :])
    arrays = {
        "x_t": np.ascontiguousarray(np.concatenate([a["x_prompt"][0], a["x_sample"][:, 0]]).T),
        "w_slabs": np.stack(order),
        "lru_w": np.ascontiguousarray(np.stack([a["lru_w_a"][0], a["lru_w_x"][0]]).transpose(2, 0, 1, 3)),
        "vec": np.ascontiguousarray(np.stack(vectors).reshape(NVEC, KT, P).transpose(2, 0, 1)),
        "state_hgrn": np.ascontiguousarray(a["state_hgrn"][0].transpose(1, 2, 0, 3)).reshape(HEADS, P, DEC * P),
        "state_lru": np.ascontiguousarray(a["state_lru"][0].reshape(DEC, KT, P).transpose(2, 1, 0)),
        "state_conv": np.ascontiguousarray(a["state_conv"][0].reshape(DEC, 3, KT, P).transpose(3, 2, 1, 0))
        .reshape(P, KT, 3 * DEC),
        "consts": np.stack([np.eye(P, dtype=np.float32), np.full((P, P), 1.0 / D, np.float32),
                            np.full((P, P), 1.0 / P, np.float32), causal.astype(np.float32)], axis=1),
    }
    outs = {"y_t": (D, T), "hgrn_p": (HEADS, P, P), "hgrn_s": (HEADS, P, DEC * P), "lru": (P, KT, DEC + 1),
            "conv_p": (P, KT, 3), "conv_s": (P, KT, 3 * DEC)}

    nc = bacc.Bacc("TRN2", target_bir_lowering=False, num_devices=1, dynamic_dma_scratch_size=1024)
    args = [nc.dram_tensor(n, v.shape, mybir.dt.from_np(v.dtype), kind="ExternalInput").ap()
            for n, v in arrays.items()]
    args += [nc.dram_tensor(n, shape, F32, kind="ExternalOutput").ap() for n, shape in outs.items()]
    build(nc, *args)
    r = run_bass_kernel_spmd(nc, [arrays], core_ids=[0]).results[0]

    y = r["y_t"].T
    lru = r["lru"].transpose(2, 1, 0).reshape(DEC + 1, D)
    return (
        np.ascontiguousarray(y[:SEQ])[None],
        np.ascontiguousarray(y[SEQ:])[:, None],
        r["hgrn_p"][None, None],
        lru[None, :1],
        np.ascontiguousarray(r["conv_p"].transpose(2, 1, 0)).reshape(1, 1, 3, D),
        np.ascontiguousarray(r["hgrn_s"].reshape(HEADS, P, DEC, P).transpose(2, 0, 1, 3))[None],
        lru[None, 1:],
        np.ascontiguousarray(r["conv_s"].reshape(P, KT, 3, DEC).transpose(3, 2, 1, 0)).reshape(1, DEC, 3, D),
    )
```
